# Optimizing a Trainium2 kernel written in Bass

```python
import jax, jax.numpy as jnp
from jax import lax
import numpy as np
import math

D_MODEL = 1024
BATCH = 1
SEQ = 1024
DEPTH = 1

N_HEADS = 8
N_KV_HEADS = 2
HEAD_DIM = 64
ATTN_WIDTH = N_HEADS * HEAD_DIM
CONV_CH = D_MODEL - ATTN_WIDTH
N_IDX_HEADS = 8
IDX_DIM = 64
TOPK_MAX = 256
CONV_K = 31
D_FF = 4 * D_MODEL
ROPE_THETA = 500000.0
Q_BLOCK = 128
EPS = 1e-6
SPLITS = (ATTN_WIDTH, N_KV_HEADS * HEAD_DIM, N_KV_HEADS * HEAD_DIM,
          N_IDX_HEADS * IDX_DIM, IDX_DIM, N_IDX_HEADS, 2 * CONV_CH)
D_IN = ATTN_WIDTH + 4 * N_KV_HEADS * HEAD_DIM // 2 + N_IDX_HEADS * IDX_DIM + IDX_DIM + N_IDX_HEADS + 2 * CONV_CH


def _rmsnorm(x, g):
    xf = x.astype(jnp.float32)
    y = xf * lax.rsqrt(jnp.mean(xf * xf, axis=-1, keepdims=True) + EPS)
    return (y * g.astype(jnp.float32)).astype(x.dtype)

def _layernorm(x, g, b):
    xf = x.astype(jnp.float32)
    mu = jnp.mean(xf, axis=-1, keepdims=True)
    var = jnp.mean(jnp.square(xf - mu), axis=-1, keepdims=True)
    y = (xf - mu) * lax.rsqrt(var + EPS)
    return (y * g.astype(jnp.float32) + b.astype(jnp.float32)).astype(x.dtype)

def _partial_rope(x, positions):
    d = x.shape[-1]
    rot = d // 4
    half = rot // 2
    inv_freq = jnp.power(ROPE_THETA, -jnp.arange(half, dtype=jnp.float32) * 2.0 / rot)
    ang = positions.astype(jnp.float32)[:, :, None] * inv_freq
    cos = jnp.cos(ang)[:, :, None, :]
    sin = jnp.sin(ang)[:, :, None, :]
    xf = x.astype(jnp.float32)
    x1, x2, rest = xf[..., :half], xf[..., half:rot], xf[..., rot:]
    out = jnp.concatenate([x1 * cos - x2 * sin, x2 * cos + x1 * sin, rest], axis=-1)
    return out.astype(x.dtype)

def _dsa_attention(q, k, v, q_idx, k_idx, w_idx):
    B, S = q.shape[0], q.shape[1]
    nb = S // Q_BLOCK
    topk = min(TOPK_MAX, S // 4)
    groups = N_HEADS // N_KV_HEADS
    key_pos = jnp.arange(S, dtype=jnp.int32)

    def to_blocks(a):
        a = a.reshape((B, nb, Q_BLOCK) + a.shape[2:])
        return jnp.moveaxis(a, 1, 0)

    xs = (to_blocks(q), to_blocks(q_idx), to_blocks(w_idx),
          key_pos.reshape(nb, Q_BLOCK))

    def block_fn(blk):
        qb, qib, wb, tb = blk
        logits = jnp.einsum('bthd,bsd->bths', qib.astype(jnp.float32),
                            k_idx.astype(jnp.float32)) * (IDX_DIM ** -0.5)
        score = jnp.einsum('bth,bths->bts', wb.astype(jnp.float32), jax.nn.relu(logits))
        causal = key_pos[None, :] <= tb[:, None]
        score = jnp.where(causal[None], score, -jnp.inf)
        _, sel = lax.top_k(score, topk)
        sel_ok = sel <= tb[None, :, None]
        k_sel = jax.vmap(lambda kb, ib: kb[ib])(k, sel)
        v_sel = jax.vmap(lambda vb, ib: vb[ib])(v, sel)
        qg = qb.reshape(B, Q_BLOCK, N_KV_HEADS, groups, HEAD_DIM)
        s = jnp.einsum('btkgd,btnkd->btkgn', qg, k_sel).astype(jnp.float32) * (HEAD_DIM ** -0.5)
        s = jnp.where(sel_ok[:, :, None, None, :], s, -jnp.inf)
        p = jax.nn.softmax(s, axis=-1).astype(v.dtype)
        o = jnp.einsum('btkgn,btnkd->btkgd', p, v_sel)
        return o.reshape(B, Q_BLOCK, ATTN_WIDTH)

    out = lax.map(block_fn, xs)
    return jnp.moveaxis(out, 0, 1).reshape(B, S, ATTN_WIDTH)

def _conformer_conv(u, conv_w, conv_b, norm_g, norm_b):
    a, g = jnp.split(u, 2, axis=-1)
    glu = a * jax.nn.sigmoid(g)
    y = lax.conv_general_dilated(
        glu, conv_w[:, None, :], window_strides=(1,),
        padding=[(CONV_K - 1, 0)],
        dimension_numbers=('NWC', 'WIO', 'NWC'),
        feature_group_count=CONV_CH) + conv_b
    y = _layernorm(y, norm_g, norm_b)
    return jax.nn.silu(y)

def first_inputs(seed: int = 0) -> dict:
    key = jax.random.key(seed)
    ks = jax.random.split(key, 20)
    f32 = jnp.float32
    nrm = lambda k, shp, s: jax.random.normal(k, shp, f32) * s
    x = jax.random.normal(ks[0], (BATCH, SEQ, D_MODEL), f32)
    c = jax.random.normal(ks[1], (BATCH, D_MODEL), f32)
    offset = jax.random.randint(ks[2], (BATCH, 1), 0, 1024, dtype=jnp.int32)
    positions = offset + jnp.arange(SEQ, dtype=jnp.int32)[None, :]
    return {
        "x": x,
        "c": c,
        "positions": positions,
        "w_ada": nrm(ks[3], (DEPTH, D_MODEL, 6 * D_MODEL), 0.5 * D_MODEL ** -0.5),
        "b_ada": nrm(ks[4], (DEPTH, 6 * D_MODEL), 0.01),
        "g_mix": 1.0 + nrm(ks[5], (DEPTH, D_MODEL), 0.02),
        "w_in": nrm(ks[6], (DEPTH, D_MODEL, D_IN), D_MODEL ** -0.5),
        "conv_w": nrm(ks[7], (DEPTH, CONV_K, CONV_CH), CONV_K ** -0.5),
        "conv_b": nrm(ks[8], (DEPTH, CONV_CH), 0.01),
        "conv_norm_g": 1.0 + nrm(ks[9], (DEPTH, CONV_CH), 0.02),
        "conv_norm_b": nrm(ks[10], (DEPTH, CONV_CH), 0.01),
        "w_out": nrm(ks[11], (DEPTH, D_MODEL, D_MODEL), D_MODEL ** -0.5),
        "g_mlp": 1.0 + nrm(ks[12], (DEPTH, D_MODEL), 0.02),
        "w_up": nrm(ks[13], (DEPTH, D_MODEL, D_FF), D_MODEL ** -0.5),
        "w_down": nrm(ks[14], (DEPTH, D_FF, D_MODEL), D_FF ** -0.5),
        "g_final": 1.0 + nrm(ks[15], (D_MODEL,), 0.02),
    }

def first_block(x, c, positions, w_ada, b_ada, g_mix, w_in, conv_w, conv_b,
              conv_norm_g, conv_norm_b, w_out, g_mlp, w_up, w_down, g_final):
    B, S, _ = x.shape
    split_at = [int(i) for i in np.cumsum(SPLITS)[:-1]]
    cond = jax.nn.silu(c)
    for i in range(DEPTH):
        mod = jnp.einsum('bd,de->be', cond, w_ada[i]) + b_ada[i]
        sh1, sc1, gt1, sh2, sc2, gt2 = jnp.split(mod, 6, axis=-1)

        h = _rmsnorm(x, g_mix[i]) * (1.0 + sc1[:, None, :]) + sh1[:, None, :]
        proj = jnp.einsum('bsd,de->bse', h, w_in[i])
        q, k, v, qi, ki, wi, cu = jnp.split(proj, split_at, axis=-1)
        q = _partial_rope(q.reshape(B, S, N_HEADS, HEAD_DIM), positions)
        k = _partial_rope(k.reshape(B, S, N_KV_HEADS, HEAD_DIM), positions)
        v = v.reshape(B, S, N_KV_HEADS, HEAD_DIM)
        qi = _partial_rope(qi.reshape(B, S, N_IDX_HEADS, IDX_DIM), positions)
        ki = _partial_rope(ki.reshape(B, S, 1, IDX_DIM), positions)[:, :, 0, :]
        wi = wi * (N_IDX_HEADS ** -0.5)
        attn_out = _dsa_attention(q, k, v, qi, ki, wi)
        conv_out = _conformer_conv(cu, conv_w[i], conv_b[i],
                                   conv_norm_g[i], conv_norm_b[i])
        mixed = jnp.concatenate([attn_out, conv_out], axis=-1)
        x = x + gt1[:, None, :] * jnp.einsum('bse,ed->bsd', mixed, w_out[i])

        h = _rmsnorm(x, g_mlp[i]) * (1.0 + sc2[:, None, :]) + sh2[:, None, :]
        u = jnp.square(jax.nn.relu(jnp.einsum('bsd,df->bsf', h, w_up[i])))
        x = x + gt2[:, None, :] * jnp.einsum('bsf,fd->bsd', u, w_down[i])
    return _rmsnorm(x, g_final)


CHUNK = 64
MIX_WIDTH = D_MODEL
POOL_WIDTH = D_MODEL // 2
POOL_GROUPS = 4
POOL_GROUP_DIM = POOL_WIDTH // POOL_GROUPS
POOL_WINDOWS = (2, 4, 8, 16)
GDN_WIDTH = MIX_WIDTH - POOL_WIDTH
GDN_HEADS = 4
GDN_HEAD_DIM = GDN_WIDTH // GDN_HEADS
CONV_WIDTH = 4
D_FF_2 = 4 * D_MODEL
IN_WIDTH = POOL_WIDTH + 4 * GDN_WIDTH + 2 * GDN_HEADS


def rms_norm(x, w):
    xf = x.astype(jnp.float32)
    y = xf * lax.rsqrt(jnp.mean(xf * xf, axis=-1, keepdims=True) + EPS)
    return (y * w.astype(jnp.float32)).astype(x.dtype)

def l2_norm(t):
    return t * lax.rsqrt(jnp.sum(t * t, axis=-1, keepdims=True) + EPS)

def pool_mixer(u, w_pool, pool_scale):
    B, S, _ = u.shape
    uf = u.astype(jnp.float32)
    cs = jnp.cumsum(uf, axis=1)
    count = jnp.arange(1, S + 1, dtype=jnp.float32)[None, :, None]
    outs = []
    for g, w in enumerate(POOL_WINDOWS):
        sl = slice(g * POOL_GROUP_DIM, (g + 1) * POOL_GROUP_DIM)
        c = cs[..., sl]
        prev = jnp.pad(c, ((0, 0), (w, 0), (0, 0)))[:, :S]
        mean = (c - prev) / jnp.minimum(count, float(w))
        outs.append(mean - uf[..., sl])
    pooled = jnp.stack(outs, axis=2).astype(u.dtype)
    mixed = jnp.einsum('bsgc,gcd->bsgd', pooled, w_pool)
    return mixed.reshape(B, S, POOL_WIDTH) * pool_scale

def causal_conv_silu(x, w):
    C = x.shape[-1]
    y = lax.conv_general_dilated(x, w[:, None, :].astype(x.dtype), window_strides=(1,),
                                 padding=[(CONV_WIDTH - 1, 0)],
                                 dimension_numbers=('NWC', 'WIO', 'NWC'),
                                 feature_group_count=C)
    return jax.nn.silu(y)

def gated_delta_net(q, k, v, z, a, b, a_log, dt_bias, gdn_norm):
    B, S, _ = q.shape
    H, Dh, C = GDN_HEADS, GDN_HEAD_DIM, CHUNK
    N = S // C
    f32 = jnp.float32

    def heads(t):
        return t.astype(f32).reshape(B, N, C, H, Dh).transpose(0, 3, 1, 2, 4)

    def per_head(t):
        return t.reshape(B, N, C, H).transpose(0, 3, 1, 2)

    qh = l2_norm(heads(q)) * (Dh ** -0.5)
    kh = l2_norm(heads(k))
    vh = heads(v)
    beta = per_head(jax.nn.sigmoid(b.astype(f32)))
    g = -jnp.exp(a_log.astype(f32)) * jax.nn.softplus(a.astype(f32) + dt_bias.astype(f32))
    gcum = jnp.cumsum(per_head(g), axis=-1)

    idx = jnp.arange(C)
    incl = idx[:, None] >= idx[None, :]
    strict = idx[:, None] > idx[None, :]
    diff = gcum[..., :, None] - gcum[..., None, :]
    decay_incl = jnp.exp(jnp.where(incl, diff, -jnp.inf))
    decay_strict = jnp.where(strict, decay_incl, 0.0)

    kb = kh * beta[..., None]
    m = jnp.einsum('bhncd,bhnjd->bhncj', kb, kh) * decay_strict
    lhs = jnp.eye(C, dtype=f32) + m
    rhs = jnp.concatenate([vh * beta[..., None], kb * jnp.exp(gcum)[..., None]], axis=-1)
    sol = lax.linalg.triangular_solve(lhs, rhs, left_side=True, lower=True)
    value, k_cumdecay = sol[..., :Dh], sol[..., Dh:]
    attn_inner = jnp.einsum('bhncd,bhnjd->bhncj', qh, kh) * decay_incl
    q_dec = qh * jnp.exp(gcum)[..., None]
    g_last = gcum[..., -1]
    k_dec = kh * jnp.exp(g_last[..., None] - gcum)[..., None]

    def step(state, inp):
        qd, kc, val, ai, kd, gl = inp
        v_new = val - jnp.einsum('bhcd,bhde->bhce', kc, state)
        o = jnp.einsum('bhcd,bhde->bhce', qd, state) + jnp.einsum('bhcj,bhje->bhce', ai, v_new)
        state = state * jnp.exp(gl)[..., None, None] + jnp.einsum('bhcd,bhce->bhde', kd, v_new)
        return state, o

    xs = (jnp.moveaxis(q_dec, 2, 0), jnp.moveaxis(k_cumdecay, 2, 0), jnp.moveaxis(value, 2, 0),
          jnp.moveaxis(attn_inner, 2, 0), jnp.moveaxis(k_dec, 2, 0), jnp.moveaxis(g_last, 2, 0))
    state0 = jnp.zeros((B, H, Dh, Dh), f32)
    _, o = lax.scan(step, state0, xs)
    o = o.transpose(1, 0, 3, 2, 4).reshape(B, S, H, Dh)
    o = o * lax.rsqrt(jnp.mean(o * o, axis=-1, keepdims=True) + EPS) * gdn_norm.astype(f32)
    o = o * jax.nn.silu(z.astype(f32).reshape(B, S, H, Dh))
    return o.reshape(B, S, GDN_WIDTH).astype(q.dtype)

def second_inputs(seed: int = 0) -> dict:
    key = jax.random.key(seed)
    ks = jax.random.split(key, 16)
    nrm = jax.random.normal
    H, Dh = GDN_HEADS, GDN_HEAD_DIM
    x = nrm(ks[0], (BATCH, SEQ, D_MODEL), jnp.float32)
    norm_mix = 1.0 + 0.02 * nrm(ks[1], (DEPTH, D_MODEL), jnp.float32)
    w_in = nrm(ks[2], (DEPTH, D_MODEL, IN_WIDTH), jnp.float32) * D_MODEL ** -0.5
    conv_w = nrm(ks[3], (DEPTH, CONV_WIDTH, 3 * GDN_WIDTH), jnp.float32) * CONV_WIDTH ** -0.5
    w_pool = nrm(ks[4], (DEPTH, POOL_GROUPS, POOL_GROUP_DIM, POOL_GROUP_DIM), jnp.float32) * POOL_GROUP_DIM ** -0.5
    pool_scale = 1.0 + 0.1 * nrm(ks[5], (DEPTH, POOL_WIDTH), jnp.float32)
    a_log = jnp.log(jax.random.uniform(ks[6], (DEPTH, H), jnp.float32, 1.0, 16.0))
    dt = jnp.exp(jax.random.uniform(ks[7], (DEPTH, H), jnp.float32, math.log(1e-3), math.log(1e-1)))
    dt_bias = dt + jnp.log(-jnp.expm1(-dt))
    gdn_norm = 1.0 + 0.02 * nrm(ks[8], (DEPTH, Dh), jnp.float32)
    w_out = nrm(ks[9], (DEPTH, MIX_WIDTH, D_MODEL), jnp.float32) * MIX_WIDTH ** -0.5
    norm_mlp = 1.0 + 0.02 * nrm(ks[10], (DEPTH, D_MODEL), jnp.float32)
    w_up = nrm(ks[11], (DEPTH, D_MODEL, D_FF_2), jnp.float32) * D_MODEL ** -0.5
    w_down = nrm(ks[12], (DEPTH, D_FF_2, D_MODEL), jnp.float32) * D_FF_2 ** -0.5
    norm_final = 1.0 + 0.02 * nrm(ks[13], (D_MODEL,), jnp.float32)
    return {"x": x, "norm_mix": norm_mix, "w_in": w_in, "conv_w": conv_w, "w_pool": w_pool,
            "pool_scale": pool_scale, "a_log": a_log, "dt_bias": dt_bias, "gdn_norm": gdn_norm,
            "w_out": w_out, "norm_mlp": norm_mlp, "w_up": w_up, "w_down": w_down,
            "norm_final": norm_final}

def second_block(x, norm_mix, w_in, conv_w, w_pool, pool_scale, a_log, dt_bias, gdn_norm,
              w_out, norm_mlp, w_up, w_down, norm_final):
    P, G, H = POOL_WIDTH, GDN_WIDTH, GDN_HEADS
    h = x
    for l in range(DEPTH):
        u = rms_norm(h, norm_mix[l])
        proj = u @ w_in[l]
        pool_out = pool_mixer(proj[..., :P], w_pool[l], pool_scale[l])
        qkv = causal_conv_silu(proj[..., P:P + 3 * G], conv_w[l])
        z = proj[..., P + 3 * G:P + 4 * G]
        a = proj[..., P + 4 * G:P + 4 * G + H]
        b = proj[..., P + 4 * G + H:P + 4 * G + 2 * H]
        gdn_out = gated_delta_net(qkv[..., :G], qkv[..., G:2 * G], qkv[..., 2 * G:], z, a, b,
                                  a_log[l], dt_bias[l], gdn_norm[l])
        mix = jnp.concatenate([pool_out, gdn_out], axis=-1)
        h = h + mix @ w_out[l]
        u = rms_norm(h, norm_mlp[l])
        h = h + jnp.square(jax.nn.relu(u @ w_up[l])) @ w_down[l]
    return rms_norm(h, norm_final)


def setup_inputs(seed=0):
    out = dict(first_inputs(seed))
    for name, value in second_inputs(seed + 1).items():
        if name != "x":
            out[name + "_2"] = value
    return out


def reference(
    x, c, positions, w_ada, b_ada, g_mix, w_in, conv_w, conv_b, conv_norm_g, conv_norm_b, w_out,
    g_mlp, w_up, w_down, g_final, norm_mix_2, w_in_2, conv_w_2, w_pool_2, pool_scale_2, a_log_2,
    dt_bias_2, gdn_norm_2, w_out_2, norm_mlp_2, w_up_2, w_down_2, norm_final_2,
):
    x = first_block(
        x, c, positions, w_ada, b_ada, g_mix, w_in, conv_w, conv_b, conv_norm_g, conv_norm_b,
        w_out, g_mlp, w_up, w_down, g_final,
    )
    return second_block(
        x, norm_mix_2, w_in_2, conv_w_2, w_pool_2, pool_scale_2, a_log_2, dt_bias_2, gdn_norm_2,
        w_out_2, norm_mlp_2, w_up_2, w_down_2, norm_final_2,
    )


_drawn_inputs = setup_inputs


def setup_inputs(seed=0):
    import zlib

    import numpy as np

    out = dict(_drawn_inputs(seed))
    spreads = {}
    factors = {'b_ada': 3.071,
     'g_mix': 8.0,
     'conv_b': 30.944,
     'conv_norm_g': 23.09,
     'conv_norm_b': 43.07,
     'g_mlp': 5.419,
     'norm_mix_2': 3.5,
     'gdn_norm_2': 22.654,
     'norm_mlp_2': 11.621,
     'norm_final_2': 7.854,
     'pool_scale_2': 3.428}
    for name, (base, spread) in spreads.items():
        noise = np.random.default_rng([zlib.crc32(name.encode()), seed]).standard_normal(out[name].shape)
        drawn = base * np.exp(spread * noise) if base else spread * noise
        out[name] = __import__('jax').numpy.asarray(drawn.astype(out[name].dtype))
    for name, factor in factors.items():
        out[name] = (out[name] * factor).astype(out[name].dtype)
    return out
```

```python
from contextlib import ExitStack

import numpy as np
import concourse.bass as bass
from concourse import mybir

ALU = mybir.AluOpType
ACT = mybir.ActivationFunctionType
AX = mybir.AxisListType
F32 = mybir.dt.float32
F32R = mybir.dt.float32r
I32 = mybir.dt.int32

P = 128
S = 1024
D = 1024
NT = S // P
NK = D // P
HALF = 512
DFF = 4 * D
EPS = 1e-6

NH, NKV, HD = 8, 2, 64
TOPK = 256
CONV_CH, CONV_K = 512, 31
NCC = CONV_CH // P
ROT = HD // 4
HROT = ROT // 2
COL_Q, COL_K, COL_V = 0, NH * HD, NH * HD + NKV * HD
COL_QI = COL_V + NKV * HD
COL_KI = COL_QI + NH * HD
COL_WI = COL_KI + HD
COL_CU = COL_WI + NH
TM_COLS = [(0, HALF), (HALF, HALF), (2 * HALF, COL_CU - 2 * HALF)]
MASKED = -3.0e38
TAKEN = -3.4e38
ROUNDS = TOPK // 8
IDX_TILES = [t for t in range(NT) if (t + 1) * P > TOPK]

PW, GW = D // 2, D // 2
GH, GD, CHUNK = 4, 128, 64
WINDOWS = (2, 4, 8, 16)
TAPS = 4
ABC = PW + 4 * GW

VEC = {}
_n = 0
for _name, _rows in (("c", NK), ("b_ada", 6 * NK), ("g_mix", NK), ("g_mlp", NK), ("conv_b", NCC),
                     ("conv_norm_g", NCC), ("conv_norm_b", NCC), ("norm_mix_2", NK),
                     ("norm_mlp_2", NK), ("pool_scale_2", GH), ("gdn_norm_2", 1)):
    VEC[_name] = (_n, _n + _rows)
    _n += _rows
NVEC = _n

def build(nc, a, out, upto=None, dumps=None):
    with ExitStack() as ctx:
        sems = {}

        def sem(name):
            if name not in sems:
                sems[name] = ctx.enter_context(nc.semaphore(name))
            return sems[name]

        BASE = 16512
        AX_, ARAW, AWHI, AWLO, AH, AU, AC = (BASE + 1024 * n for n in (0, 32, 48, 64, 80, 144, 176))

        def at(name, shape, dt, offset):
            return nc.alloc_sbuf_tensor_at(name, shape, dt, offset=offset).ap()

        K1 = 1024
        x = at("x", [P, NT, D], F32, AX_)
        raw = at("raw", [P, 4, 1024], F32, ARAW)
        w_hi = at("w_hi", [P, 4, 1024], F32R, AWHI)
        w_lo = at("w_lo", [P, 4, 1024], F32R, AWLO)
        h_hi = at("h_hi", [P, NK, S], F32R, AH)
        h_lo = at("h_lo", [P, NK, S], F32R, AH + 32 * K1)
        xn = at("xn", [P, NT, D], F32, AU)
        u_hi = at("u_hi", [P, 4, S], F32R, AU)
        u_lo = at("u_lo", [P, 4, S], F32R, AU + 16 * K1)
        qT = at("qT", [P, 4, S], F32, AX_)
        qiT = at("qiT", [P, 4, S], F32, AX_ + 16 * K1)
        ropet = at("ropet", [P, 4, HALF], F32, AX_ + 16 * K1)
        pr0 = at("pr0", [P, NT, 512], F32, AU)
        pr1 = at("pr1", [P, NT, 384], F32, AU + 16 * K1)
        vtok = at("vtok", [P, NT, P], F32, AU + 28 * K1)
        glu = at("glu", [P, NCC, S], F32, AU)
        idx0 = at("idx0", [P, S], F32, AU + 16 * K1)
        otok = at("otok", [P, 512], F32, AU + 20 * K1)
        diag = at("diag", [P, 8, P], F32, AU + 22 * K1)
        relu = at("relu", [P, 2, S], F32, AWHI)
        prob = at("prob", [P, 2, S], F32, AWHI + 8 * K1)
        probT = at("probT", [P, 2, NT, P], F32, AWLO)
        score01 = at("score01", [P, 2, S], F32, AWLO + 8 * K1)
        conv = at("conv", [P, NCC, S], F32, AH + 48 * K1)
        off = [AC]

        def small(name, shape, dt=F32):
            n = int(np.prod(shape[1:])) * 4
            t = at(name, shape, dt, off[0])
            off[0] += (n + 31) // 32 * 32
            return t

        ident = small("ident", [P, P])
        ones = small("ones", [P, P])
        vec = small("vec", [P, P])
        cw = small("cw", [P, P])
        cw2 = small("cw2", [P, TAPS * 12])
        mod = small("mod", [P, 6 * NK])
        csil = small("csil", [P, NK])
        eps = small("eps", [P, 1])
        zero = small("zero", [P, 1])
        scl = small("scl", [P, 2, NK])
        pos = small("pos", [P, NT])
        freq = small("freq", [P, HROT])
        cosv = small("cosv", [P, NT, HROT])
        sinv = small("sinv", [P, NT, HROT])
        ss = small("ss", [P, NT])
        sd = small("sd", [P, NT])
        rs = small("rs", [P, NT])
        wi = small("wi", [P, NT, NH])
        best = small("best", [P, 8])
        smax = small("smax", [P, NH])
        snm = small("snm", [P, NH])
        ssum = small("ssum", [P, 2, NH])
        srec = small("srec", [P, NH])
        invc = small("invc", [P, 16])
        dtb = small("dtb", [P, GH])
        alog = small("alog", [P, GH])
        abraw = small("abraw", [P, NK, 2 * GH])
        ab_hi = small("ab_hi", [P, NK, 2 * GH], F32R)
        ab_lo = small("ab_lo", [P, NK, 2 * GH], F32R)
        ab = small("ab", [P, NT, 2 * GH])
        gs = {nm: small(f"g_{nm}", [P, NT, GH]) for nm in ("t1", "t2", "g", "beta", "gcum", "egc", "edec", "bege")}
        osum = small("osum", [P, GH])
        orec = small("orec", [P, GH])
        eps2 = small("eps2", [P, 1])
        AD = off[0]
        pr2 = at("pr2", [P, NT, 392], F32, AD)
        tmp2 = at("tmp2", [P, 2, HALF], F32, AD)
        act_r = at("act_r", [P, 4, HALF], F32, AD + 4 * K1)
        score = [score01[:, 0, :], score01[:, 1, :], at("score2", [P, S], F32, AD + 4 * K1)]
        junk = at("junk", [P, 2, D], F32, AD + 4 * K1)
        rowsv = at("rowsv", [P, 3, P], F32, AD)
        rowsi = at("rowsi", [NT, P], I32, AD + 2 * K1)
        rowsp = at("rowsp", [NT, P], F32, AD + 3 * K1)
        angt = at("angt", [P, 4, NT, HROT], F32, AD + 4 * K1)
        AE = AD + 12 * K1 + 256
        kT = at("kT", [P, S], F32, AE)
        kiT = at("kiT", [P, S], F32, AE + 4 * K1)
        gate1 = at("gate1", [P, D], F32, AE + 8 * K1)
        gate2 = at("gate2", [P, D], F32, AE)
        frow = at("frow", [P, D], F32, AE + 4 * K1)
        gdiag = at("gdiag", [P, NK, P], F32, AU)

        qc = at("qc", [P, GH, S], F32, AX_)
        kc = at("kc", [P, GH, S], F32, AX_ + 16 * K1)
        vc = at("vc", [P, GH, S], F32, AU)
        zc = at("zc", [P, GH, S], F32, AU + 16 * K1)
        pm = at("pm", [P, GH, S], F32, AD)
        yt = at("yt", [P, 2, S], F32, AD + 16 * K1)
        wpool = at("wpool", [P, GH, P], F32, AD + 24 * K1)
        masks = at("masks", [P, 8, P], F32, AD + 16 * K1)
        tri, strict, blk = masks[:, 0, :], masks[:, 1, :], cw
        level = [masks[:, 2 + i, :] for i in range(6)]
        state = at("state", [P, GH, P], F32, AD + 16 * K1 + 4096)
        vnew = at("vnew", [P, GH, P], F32, AD + 16 * K1 + 6144)
        ot = at("ot", [P, GH, P], F32, AD + 16 * K1 + 8192)
        prep = []
        for i in range(2):
            names = ["e1", "e2", "egb", "m", "b0", "b1", "z", "t", "u", "kbe", "vb", "ait", "kd", "val", "kct", "qdec"]
            prep.append({nm: at(f"{nm}_{i}", [P, GH, P], F32, AH + i * 32 * K1 + j * 2 * K1)
                         for j, nm in enumerate(names)})

        ps = nc.alloc_psum_tensor("ps", [P, 8, HALF], F32).ap()

        def v3(ap, n):
            return ap.rearrange("p (n m) -> p n m", n=n)

        def vcol(name, i=0):
            return vec[:, VEC[name][0] + i:VEC[name][0] + i + 1]

        def vcols(name):
            return vec[:, VEC[name][0]:VEC[name][1]]

        def kp(name):
            return a[name].rearrange("l (k p) n -> (l p) k n", p=P) if len(a[name].shape) == 3 else a[name]

        w_ada, w_in, w_out = kp("w_ada"), kp("w_in"), kp("w_out")
        slots = []
        for j in range(2 * NK):
            slots.append(("ada", w_ada[:, :, j * P:(j + 1) * P], (NK, P)))
        for c0, cn in TM_COLS:
            for kk in range(4):
                slots.append(("w", w_in[:, 2 * kk:2 * kk + 2, c0:c0 + cn], (2, cn)))
        for c in range(NCC):
            for part in range(2):
                c0 = COL_CU + part * CONV_CH + c * P
                slots.append(("w", w_in[:, :, c0:c0 + P], (NK, P)))
        for j in range(2 * NK, 6 * NK):
            slots.append(("ada", w_ada[:, :, j * P:(j + 1) * P], (NK, P)))
        for j in range(2):
            for kk in range(4):
                slots.append(("w", w_out[:, 2 * kk:2 * kk + 2, j * HALF:(j + 1) * HALF], (2, HALF)))
        N_FIRST = len(slots)
        assert N_FIRST % 4 == 0
        nw = nada = 0
        freed = []
        for kind, _, _ in slots:
            if kind == "w":
                nw += 1
                freed.append(("split_done", nw))
            else:
                nada += 1
                freed.append(("ada_done", nada))
        W_FIRST = nw
        used = []
        for j in range(len(TM_COLS)):
            used += [("tm_part", 3 * j + kk + 1) for kk in range(3)] + [("tm_full", NT * (j + 1))]
        used += [("cm_full", 2 * i + 2) for i in range(2 * NCC)]
        for j in range(2):
            used += [("wo_part", 3 * j + kk + 1) for kk in range(3)] + [("wo_full", NT * (j + 1))]
        assert len(used) == W_FIRST
        raw_in = [sem(f"raw_in{r}") for r in range(4)]
        w_in_2, w_out_2 = kp("w_in_2"), kp("w_out_2")
        CH2 = [("pool", i) for i in range(GH)] + [("qkv", i) for i in range(3 * GH)] + [("z", i) for i in range(GH)]
        slots2 = [("w", w_in_2[:, :, i * P:(i + 1) * P], (NK, P)) for i in range(len(CH2))]
        for j in range(2):
            for kk in range(4):
                slots2.append(("w", w_out_2[:, 2 * kk:2 * kk + 2, j * HALF:(j + 1) * HALF], (2, HALF)))
        GROUPS = DFF // 512
        N_MLP0, M_MLP0 = N_FIRST, W_FIRST
        N_2, M_2 = N_MLP0 + 8 * GROUPS, M_MLP0 + 8 * GROUPS
        N_MLP1, M_MLP1 = N_2 + len(slots2), M_2 + len(slots2)
        assert len(slots2) % 4 == 0 and M_2 % 4 == 0
        used2 = [("cm2_full", 2 * i + 2) for i in range(len(CH2))]
        for j in range(2):
            used2 += [("wo2_part", 3 * j + kk + 1) for kk in range(3)] + [("wo2_full", NT * (j + 1))]

        ch_read, ch_free = [], []
        for kind, c in CH2:
            ch_read.append({"pool": ("pool_u", c + 1), "qkv": ("taps", 3 * (c + 1)), "z": ("z_silu", c + 1)}[kind])
            ch_free.append({"pool": ("pm_out", c + 1), "qkv": ("l2_done", c + 1) if c < 2 * GH else ("conv_silu", c + 1),
                            "z": None}[kind])
        aux_read = {i: (("pm_out", c + 1) if kind == "pool" else ("l2_sd", c + 1))
                    for i, (kind, c) in enumerate(CH2) if kind == "pool" or (kind == "qkv" and c < 2 * GH)}

        GSTEPS = []
        for slot in range(4 * NT + 10):
            for t in range(NT):
                j = slot - 4 * t
                if j == 7:
                    GSTEPS.append(("chunk", t, 0))
                if j == 8:
                    GSTEPS.append(("finish", t, 0))
            for t in range(NT):
                j = slot - 4 * t
                if j == 0:
                    GSTEPS.append(("head", t, 0))
                if 1 <= j <= 5:
                    GSTEPS.append(("level", t, j))
                if j == 6:
                    GSTEPS.append(("tail", t, 0))
            for t in range(NT):
                if slot - 4 * t == 7:
                    GSTEPS.append(("chunk", t, 1))
        PREP = {
            "mm": ["gb", "gram", "kq", "turn"] + [x for l in range(1, 6) for x in ((f"z{l}", f"t{l}", f"u{l}") if l < 5 else ("z5", "u5"))]
                  + ["ktp", "vtp", "val", "kct"],
            "dve": ["tg", "df", "e12", "m", "ait", "u0"] + [x for l in range(1, 6) for x in ((f"t{l}", f"u{l}") if l < 5 else ("u5",))]
                   + ["kbe", "kd", "vb"],
            "act": ["egb", "e1", "e2"] + [f"z{l}" for l in range(1, 6)] + ["val", "kct"],
            "pool": ["e1m", "e2m", "qdec", "b0", "t0", "b1", "b2", "b3", "b4", "b5"],
        }
        SCAN = {
            "mm": ["kq0", "kdv0", "kq1", "kdv1", "ai", "otp"],
            "dve": ["vnew0", "sdec0", "snew0", "vnew1", "sdec1", "snew1", "sq", "sum", "rec", "on", "gated"],
            "act": ["ot", "sd"],
        }

        def prep_sem(kind, t):
            return sem(f"prep_{kind}{t % 2}")

        def prep_count(kind, t, what):
            return (t // 2) * len(PREP[kind]) + PREP[kind].index(what) + 1

        def scan_count(kind, t, what):
            return t * len(SCAN[kind]) + SCAN[kind].index(what) + 1

        def hb(mask):
            return mask.unsqueeze(1).to_broadcast([P, GH, P])

        def tb(col):
            return col.unsqueeze(2).to_broadcast([P, GH, P])

        def bank(b):
            return v3(ps[:, b, :], GH)


        MICRO = []
        TOPK_PARTS = {t: 2 * NH if t == IDX_TILES[0] else NH for t in IDX_TILES}
        TAPS_PER_SLOT = {0: 2, 1: 2, 2: 4, 3: 5, 4: 5, 5: 6, 6: 7, 7: 0}
        assert NH * sum(TAPS_PER_SLOT.values()) == 2 * NCC * CONV_K
        LN = {0: ("ln_mean", 0), 1: ("ln_square", 0), 2: ("ln_scale", 0), 3: ("ln_silu", 0),
              4: ("ln_mean", 1), 5: ("ln_square", 1), 6: ("ln_scale", 1), 7: ("ln_silu", 1)}
        MICRO += [("index", IDX_TILES[0], h) for h in range(NH)]
        tap = col = 0
        for t in range(NT):
            for i in range(NH):
                n = NH * t + i
                MICRO.append(("scores", t, i))
                if t >= 2 and t + 2 < NT:
                    MICRO.append(("index", t + 2, i))
                if t < 2 and n % 2 == 0:
                    MICRO.append(("index", IDX_TILES[0] + 1, n // 2))
                last = (t, i - 1) if i else (t - 1, NH - 1)
                if n:
                    MICRO.append(("turn",) + last)
                MICRO.append(("exp", t, i))
                cols = 1 if t < 2 else 2 if t == 2 else 0
                if cols:
                    MICRO.append(("ada", col, col + cols))
                    col += cols
                MICRO.append(("conv", tap, tap + TAPS_PER_SLOT[t]))
                tap += TAPS_PER_SLOT[t]
                if t == NT - 1:
                    MICRO.append(LN[i] + (0,))
                if n:
                    MICRO.append(("values",) + last)
                if t < 2:
                    MICRO.append(("topk", IDX_TILES[0], n))
                elif t + 1 < NT:
                    MICRO.append(("topk", t + 1, i))
                if n and i == 0:
                    MICRO.append(("divide", t - 1, 0))
                if t and i == 1:
                    MICRO.append(("out", t - 1, 0))
        MICRO += [("turn", NT - 1, NH - 1), ("values", NT - 1, NH - 1), ("divide", NT - 1, 0), ("out", NT - 1, 0)]
        unit_of, units = {}, []
        for kind, t, i in MICRO:
            if kind == "index":
                unit_of[kind, t, i] = len(units)
                units.append(("relu_done", NH * (t - IDX_TILES[0]) + i + 1))
            if kind == "scores":
                unit_of[kind, t, i] = len(units)
                units.append(("masked", NH * t + i + 1))
        tp_of, tp_free = {}, []
        tp_count = []
        tp_last, tp_outs = [], []
        n_full = n_out = n_ada = 0
        for kind, t, i in MICRO:
            if kind == "turn":
                for g in range(t // 4 + 1):
                    tp_of[t, i, g] = len(tp_free)
                    n_out += 1
                    n_full += 1
                    tp_free.append(("tp_out", n_out))
                    tp_count.append(n_full)
                tp_last.append(n_full)
                tp_outs.append(n_out)
            if kind == "out":
                tp_of[t, "o"] = len(tp_free)
                n_full += 1
                tp_free.append(("attn_lo", t + 1))
                tp_count.append(n_full)
            if kind == "ada":
                tp_of["ada", t] = len(tp_free)
                n_ada += 1
                tp_free.append(("mod_out", n_ada))
                tp_count.append(n_full)
        HEADS = [j + 4 * half for j in range(4) for half in range(2)]

        x_mid = nc.dram_tensor("x_mid", [NT, P, D], F32, kind="Internal").ap()

        block = ctx.enter_context(nc.Block())

        @block.sync
        def _(sp):
            n = 0
            for kind, src, (n1, n2) in slots:
                if n >= 4:
                    sp.wait_ge(sem(freed[n - 4][0]), freed[n - 4][1])
                dst = raw[:, n % 4, 0:n1 * n2].rearrange("p (k n) -> p k n", k=n1)
                sp.dma_start(dst, src).then_inc(raw_in[n % 4], 16)
                n += 1

            def mlp(k, n0, freed0, up, down):
                with sp.Fori(0, GROUPS) as g:
                    for s in range(8):
                        sp.wait_ge(sem("split_done"), g * 8 + (freed0 + s - 3))
                        if s < 4:
                            dst = v3(raw[:, s, :], NK)
                            src = up[:, :, bass.ds(g * 512 + s * P, P)]
                        else:
                            j, kk = (s - 4) // 2, s % 2
                            dst = v3(raw[:, s - 4, :], 2)
                            src = down[:, :, bass.ds(g * 4 + 2 * kk, 2), j * HALF:(j + 1) * HALF].rearrange("l p k n -> (l p) k n")
                        sp.dma_start(dst, src).then_inc(raw_in[s % 4], 16)

            w_down = a["w_down"].rearrange("l (k p) n -> l p k n", p=P)
            mlp(0, N_FIRST, W_FIRST, kp("w_up"), w_down)
            for i, (_, src, (n1, n2)) in enumerate(slots2):
                sp.wait_ge(sem("split_done"), M_2 + i - 3)
                sp.dma_start(raw[:, i % 4, :].rearrange("p (k n) -> p k n", k=n1), src).then_inc(raw_in[i % 4], 16)
                if i == 3:
                    for t in range(NT):
                        sp.wait_ge(sem("x_final"), t + 1)
                        sp.dma_start(x_mid[t], x[:, t, :]).then_inc(sem("x_out"), 16)
            mlp(1, N_MLP1, M_MLP1, kp("w_up_2"), a["w_down_2"].rearrange("l (k p) n -> l p k n", p=P))
            for t in range(NT):
                sp.wait_ge(sem("y_final"), t + 1)
                sp.dma_start(out[0, t * P:(t + 1) * P, :], x[:, t, :]).then_inc(sem("out_done"), 16)
            sp.wait_ge(sem("out_done"), 16 * NT)

        @block.gpsimd
        def _(pool):
            g = nc.gpsimd
            g.memset(ident, 0.0).then_inc(sem("pool_mem"), 1)
            g.memset(eps, EPS).then_inc(sem("pool_mem"), 1)
            g.memset(zero, 0.0).then_inc(sem("pool_mem"), 1)
            for i in range(HROT):
                f = float(np.float32(500000.0 ** (-2.0 * i / ROT)))
                g.memset(freq[:, i:i + 1], f).then_inc(sem("pool_mem"), 1)
            g.memset(eps2, GD * EPS).then_inc(sem("pool_mem2"), 1)
            for i in range(16):
                g.memset(invc[:, i:i + 1], 1.0 / (i + 1)).then_inc(sem("pool_mem2"), 1)
            pool.wait_ge(sem("pool_mem"), 1)
            g.affine_select(out=ident, in_=ident, compare_op=ALU.not_equal, fill=1.0, base=0,
                            pattern=[[-1, P]], channel_multiplier=1).then_inc(sem("ident_ready"), 1)
            g.memset(ones, 1.0).then_inc(sem("ident_ready"), 1)

            def split(m, n, cols):
                r = m % 4
                pool.wait_ge(raw_in[n % 4], 16 * (n // 4 + 1))
                if m >= 4:
                    pool.wait_ge(sem(used[m - 4][0]), used[m - 4][1])
                g.tensor_copy(w_hi[:, r, 0:cols], raw[:, n % 4, 0:cols]).then_inc(sem("w_hi_done"), 1)
                pool.wait_ge(sem("w_hi_done"), m + 1)
                g.tensor_tensor(w_lo[:, r, 0:cols], raw[:, n % 4, 0:cols],
                                w_hi[:, r, 0:cols].bitcast(F32), ALU.subtract).then_inc(sem("split_done"), 1)

            m = 0
            for n, (kind, _, (n1, n2)) in enumerate(slots):
                if kind != "w":
                    continue
                if m == 20:
                    pool.wait_ge(sem("pr_turned"), 20)
                    g.memset(idx0, 0.0).then_inc(sem("idx_zero"), 1)
                    pool.wait_ge(sem("idx_zero"), 1)
                    g.affine_select(out=idx0[:, S - P:S], in_=idx0[:, S - P:S], compare_op=ALU.is_ge,
                                    fill=MASKED, base=0, pattern=[[-1, P]],
                                    channel_multiplier=1).then_inc(sem("idx_ready"), 1)
                    for u in range(2 * NCC):
                        for i in range(CONV_K):
                            k = u * CONV_K + i
                            tap = CONV_K - 1 - i
                            if k >= 8:
                                pool.wait_ge(sem("tap_used"), k - 7)
                            g.tensor_scalar(diag[:, k % 8, :], ident, cw[:, tap * NCC + u // 2:tap * NCC + u // 2 + 1],
                                            None, ALU.mult).then_inc(sem("diag_ready"), 1)
                    pool.wait_ge(sem("attn_lo"), NT)
                split(m, n, n1 * n2)
                m += 1

            def mlp(k, n0, m0):
                with pool.Fori(0, GROUPS) as g:
                    for s in range(8):
                        r = s % 4
                        pool.wait_ge(raw_in[r], g * 32 + (16 * (n0 // 4) + 16 * (s // 4 + 1)))
                        if s < 4 and s % 2 == 0:
                            pool.wait_ge(sem(f"down_part{k}"), g * 2 + (s // 2 - 2 + 3))
                        if s < 4 and s % 2 == 1:
                            pool.wait_ge(sem(f"down_full{k}"), g * 16 + (8 * (s // 2) - 16 + 8 + 16))
                        if s >= 4:
                            pool.wait_ge(sem(f"up_full{k}"), g * 8 + (2 * (s - 4) + 2))
                        g_.tensor_tensor(w_hi[:, r, :], raw[:, r, :], zero.to_broadcast([P, 1024]),
                                         ALU.add).then_inc(sem("w_hi_done"), 1)
                        pool.wait_ge(sem("w_hi_done"), g * 8 + (m0 + s + 1))
                        g_.tensor_tensor(w_lo[:, r, :], raw[:, r, :], w_hi[:, r, :].bitcast(F32),
                                         ALU.subtract).then_inc(sem("split_done"), 1)

            g_ = nc.gpsimd
            pool.wait_ge(sem("wo_full"), 2 * NT)
            mlp(0, N_MLP0, M_MLP0)
            pool.wait_ge(sem("ab_in"), 16)
            g.tensor_copy(ab_hi, abraw).then_inc(sem("ab_hi"), 1)
            pool.wait_ge(sem("ab_hi"), 1)
            g.tensor_tensor(ab_lo, abraw, ab_hi.bitcast(F32), ALU.subtract).then_inc(sem("ab_split"), 1)

            def split2(i):
                r = i % 4
                pool.wait_ge(raw_in[r], 16 * ((N_2 + i) // 4 + 1))
                if i >= 4:
                    pool.wait_ge(sem(used2[i - 4][0]), used2[i - 4][1])
                else:
                    pool.wait_ge(sem("down_full0"), 16 + 16 * GROUPS)
                g.tensor_copy(w_hi[:, r, :], raw[:, r, :]).then_inc(sem("w_hi_done"), 1)
                pool.wait_ge(sem("w_hi_done"), M_2 + i + 1)
                g.tensor_tensor(w_lo[:, r, :], raw[:, r, :], w_hi[:, r, :].bitcast(F32),
                                ALU.subtract).then_inc(sem("split_done"), 1)

            for i in range(len(CH2) + 4):
                split2(i)
            pool.wait_ge(sem("conv_silu"), 3 * GH)
            nm = [0]

            def step(ins):
                nm[0] += 1
                ins.then_inc(sem("mask_step"), 1)
                pool.wait_ge(sem("mask_step"), nm[0])

            def within(dst, b):
                d3 = dst.rearrange("p (n m) -> p n m", m=b)
                step(g.affine_select(out=d3, in_=d3, compare_op=ALU.is_ge, fill=0.0, base=0,
                                     pattern=[[-b, P // b], [0, b]], channel_multiplier=1))
                step(g.affine_select(out=d3, in_=d3, compare_op=ALU.is_ge, fill=0.0, base=b - 1,
                                     pattern=[[b, P // b], [0, b]], channel_multiplier=-1))

            step(g.memset(blk, 1.0))
            within(blk, CHUNK)
            step(g.affine_select(out=tri, in_=blk, compare_op=ALU.is_ge, fill=0.0, base=0,
                                 pattern=[[1, P]], channel_multiplier=-1))
            step(g.memset(strict, 1.0))
            step(g.affine_select(out=strict, in_=strict, compare_op=ALU.is_gt, fill=0.0, base=0,
                                 pattern=[[-1, P]], channel_multiplier=1))
            for i in range(6):
                step(g.tensor_copy(level[i], strict))
                within(level[i], 2 << i)
            step(g.tensor_copy(strict, level[5]))
            for i in range(5, 0, -1):
                step(g.tensor_tensor(level[i], level[i], level[i - 1], ALU.subtract))
            g.memset(state, 0.0).then_inc(sem("masks_ready"), 1)

            for kind, t, l in GSTEPS:
                b = prep[t % 2]
                if kind == "head":
                    pool.wait_ge(prep_sem("act", t), prep_count("act", t, "e1"))
                    g.tensor_tensor(b["e1"], b["e1"], hb(strict), ALU.mult).then_inc(prep_sem("pool", t), 1)
                    pool.wait_ge(prep_sem("act", t), prep_count("act", t, "e2"))
                    g.tensor_tensor(b["e2"], b["e2"], hb(tri), ALU.mult).then_inc(prep_sem("pool", t), 1)
                    if t >= 2:
                        pool.wait_ge(sem("scan_mm"), scan_count("mm", t - 2, "kq1"))
                    g.tensor_tensor(b["qdec"], qc[:, :, t * P:(t + 1) * P], b["egb"],
                                    ALU.mult).then_inc(prep_sem("pool", t), 1)
                    pool.wait_ge(prep_sem("dve", t), prep_count("dve", t, "m"))
                    g.tensor_tensor(b["b0"], b["m"], hb(level[0]), ALU.mult).then_inc(prep_sem("pool", t), 1)
                    pool.wait_ge(prep_sem("pool", t), prep_count("pool", t, "b0"))
                    g.tensor_tensor(b["t"], hb(ident), b["b0"], ALU.subtract).then_inc(prep_sem("pool", t), 1)
                    g.tensor_tensor(b["b1"], b["m"], hb(level[1]), ALU.mult).then_inc(prep_sem("pool", t), 1)
                if kind == "level" and l < 5:
                    if l == 1:
                        pool.wait_ge(prep_sem("mm", t), prep_count("mm", t, "turn"))
                        pool.wait_ge(prep_sem("pool", t), prep_count("pool", t, "t0"))
                    else:
                        pool.wait_ge(prep_sem("mm", t), prep_count("mm", t, f"z{l - 1}"))
                    g.tensor_tensor(b[f"b{(l + 1) % 2}"], b["m"], hb(level[l + 1]), ALU.mult).then_inc(prep_sem("pool", t), 1)

            for i in range(len(CH2) + 4, len(slots2)):
                split2(i)
            pool.wait_ge(sem("wo2_full"), 2 * NT)
            mlp(1, N_MLP1, M_MLP1)

        @block.scalar
        def _(act):
            s = nc.scalar
            vrow = 0
            for name, (r0, r1) in VEC.items():
                src = a[name]
                src = src.rearrange("l (k p) -> (l k) p", p=P)
                act.dma_start(rowsv[r0:r1, 0, :], src).then_inc(sem("rows_in"), 16)
            act.dma_start(rowsv[0:CONV_K * NCC, 1, :],
                          a["conv_w"].rearrange("l k (c p) -> (l k c) p", p=P)).then_inc(sem("rows_in"), 16)
            act.dma_start(rowsv[0:TAPS * 12, 2, :],
                          a["conv_w_2"].rearrange("l k (c p) -> (l k c) p", p=P)).then_inc(sem("rows_in"), 16)
            act.dma_start(rowsi, a["positions"].rearrange("b (t p) -> (b t) p", p=P)).then_inc(sem("rows_in"), 16)
            for t in range(NT):
                act.dma_start(x[:, t, :], a["x"][0, t * P:(t + 1) * P, :]).then_inc(sem(f"x_in{t}"), 16)
            act.wait_ge(sem("vec_ready"), 1)
            s.activation(csil, vcols("c"), ACT.Sigmoid).then_inc(sem("c_sig"), 1)
            act.wait_ge(sem("angle_ready"), 1)
            s.activation(sinv, angt[:, 0], ACT.Sin).then_inc(sem("sines"), 1)
            s.activation(angt[:, 1], angt[:, 0], ACT.Sin, scale=0.5).then_inc(sem("sines"), 1)

            def stats(q, src_wait):
                for t in range(NT):
                    src_wait(act, t)
                    if NT * q + t >= 2:
                        act.wait_ge(sem("norm_ss"), NT * q + t - 1)
                    s.activation(junk[:, t % 2, :], x[:, t, :], ACT.Square,
                                 accum_out=ss[:, t:t + 1]).then_inc(sem("norm_ss"), 1)
                    if t % 4 == 3:
                        act.wait_ge(sem("norm_ss"), NT * q + t + 1)
                        s.activation(sd[:, t - 3:t + 1], ss[:, t - 3:t + 1], ACT.Sqrt, scale=1.0 / D,
                                     bias=eps).then_inc(sem("norm_sd"), 1)

            def norm(q, k, src_wait, scale, bias):
                stats(q, src_wait)
                for u in range(2 * NK):
                    c = u % NK
                    act.wait_ge(sem("norm_turned"), 2 * NK * k + u + 1)
                    if u >= 2:
                        act.wait_ge(sem("norm_lo"), 2 * NK * k + u - 1)
                    s.activation(tmp2[:, u % 2, :], ps[:, u % 8, :], ACT.Identity, scale=scale(c),
                                 bias=bias(c)).then_inc(sem("norm_f"), 1)

            act.wait_ge(sem("scale_ready"), 1)
            norm(0, 0, lambda e, t: e.wait_ge(sem(f"x_in{t}"), 16),
                 lambda c: scl[:, 0, c:c + 1], lambda c: mod[:, c:c + 1])

            for t in range(NT):
                act.wait_ge(sem("tm_full"), t + 1)
                s.activation(pr0[:, t, :].rearrange("p (j h d) -> p h j d", h=2, d=HD),
                             ps[:, t, :].rearrange("p (h j d) -> p h j d", h=2, d=HD),
                             ACT.Copy).then_inc(sem("tm_out0"), 1)
            for t in range(NT):
                act.wait_ge(sem("tm_full"), 2 * NT + t + 1)
                for r in range(2):
                    s.activation(pr2[:, t, 256 + r * HD:256 + (r + 1) * HD],
                                 ps[:, t, 256:256 + HD], ACT.Copy).then_inc(sem("tm_out2a"), 1)
                s.activation(pr2[:, t, 0:256], ps[:, t, 0:256], ACT.Copy).then_inc(sem("tm_out2a"), 1)

            def turned(n):
                dst = [qT[:, j, :] for j in range(4)] + [kT] + [qiT[:, j, :] for j in range(4)] + [kiT]
                return dst[n // 2][:, (n % 2) * HALF:(n % 2 + 1) * HALF]

            for n in range(0, 20):
                act.wait_ge(sem("pr_tp"), n + 1)
                s.activation(turned(n), ps[:, 4 + n % 4, :], ACT.Copy).then_inc(sem("pr_turned"), 1)

            for c in range(NCC):
                b = (4 * c) % 8
                for half in range(2):
                    act.wait_ge(sem("cm_full"), 4 * c + 2 + half + 1)
                    if c >= 1:
                        act.wait_ge(sem("glu_ready"), 2 * c - 1 + half)
                    s.activation(tmp2[:, half, :], ps[:, b + 2 + half, :], ACT.Sigmoid).then_inc(sem("glu_sig"), 1)

            for kind, t, i in MICRO:
                w = (t + 1) * P
                cols = slice(t * HALF, (t + 1) * HALF)
                if kind == "index":
                    n = NH * (t - IDX_TILES[0]) + i
                    u = unit_of[kind, t, i]
                    act.wait_ge(sem("score_full"), u + 1)
                    if n >= 2:
                        act.wait_ge(sem("acc_done"), n - 1)
                    s.activation(relu[:, n % 2, 0:w], ps[:, 2 * (u % 2):2 * (u % 2) + 2, :]
                                 .rearrange("p a b -> p (a b)")[:, 0:w], ACT.Relu,
                                 scale=HD ** -0.5).then_inc(sem("relu_done"), 1)
                if kind == "turn":
                    n = NH * t + i
                    for g in range(t // 4 + 1):
                        u = tp_of[t, i, g]
                        nb = min(4, t + 1 - 4 * g)
                        act.wait_ge(sem("tp_full"), tp_count[u])
                        if n >= 2:
                            act.wait_ge(sem("pv_done"), n - 1)
                        s.activation(probT[:, n % 2, 4 * g:4 * g + nb, :], ps[:, 4 + u % 2, 0:nb * P]
                                     .rearrange("p (b q) -> p b q", q=P), ACT.Copy).then_inc(sem("tp_out"), 1)
                if kind == "exp":
                    h = HEADS[i]
                    n = NH * t + i
                    act.wait_ge(sem("smax_ready"), n + 1)
                    if i == 0 and t >= 2:
                        act.wait_ge(sem("o_ready"), t - 1)
                    s.activation(prob[:, n % 2, 0:w], prob[:, n % 2, 0:w], ACT.Exp, scale=HD ** -0.5,
                                 bias=snm[:, h:h + 1], accum_out=ssum[:, t % 2, h:h + 1]).then_inc(sem("exp_done"), 1)
                if kind == "out":
                    u = tp_of[t, "o"]
                    act.wait_ge(sem("tp_full"), tp_count[u])
                    s.activation(h_hi[:, 0:4, t * P:(t + 1) * P], ps[:, 4 + u % 2, :].rearrange("p (c q) -> p c q", q=P),
                                 ACT.Copy).then_inc(sem("attn_hi"), 1)
                if kind == "conv":
                    for unit in range(2 * NCC):
                        if t < CONV_K * (unit + 1) <= i:
                            act.wait_ge(sem("tap_used"), CONV_K * (unit + 1))
                            c, half = unit // 2, unit % 2
                            s.activation(conv[:, c, half * HALF:(half + 1) * HALF], ps[:, 7, :], ACT.Identity,
                                         bias=vcol("conv_b", c)).then_inc(sem("conv_out"), 1)
                if kind == "ln_square":
                    for c in range(NCC):
                        n = NCC * t + c
                        act.wait_ge(sem("ln_cent"), n + 1)
                        if n:
                            act.wait_ge(sem("ln_summed"), n)
                        if t and c == 0:
                            act.wait_ge(sem("ln_silu"), NCC * t)
                        s.activation(tmp2[:, 0, :], conv[:, c, cols], ACT.Square).then_inc(sem("ln_sq"), 1)
                if kind == "ln_scale":
                    act.wait_ge(sem("ln_summed"), NCC * (t + 1))
                    if t:
                        act.wait_ge(sem("ln_scaled"), NCC * t)
                    s.activation(tmp2[:, 1, :], ps[:, 7, :], ACT.Sqrt, scale=1.0 / CONV_CH,
                                 bias=eps).then_inc(sem("ln_sd"), 1)
                if kind == "ln_silu":
                    for c in range(NCC):
                        n = NCC * t + c
                        act.wait_ge(sem("ln_aff"), n + 1)
                        if c:
                            act.wait_ge(sem("ln_silu"), n)
                        s.activation(tmp2[:, 0, :], conv[:, c, cols], ACT.Sigmoid).then_inc(sem("ln_sig"), 1)
                        act.wait_ge(sem("ln_silu"), n + 1)
                        s.activation(h_hi[:, 4 + c, cols], conv[:, c, cols], ACT.Copy).then_inc(sem("conv_hi"), 1)
            act.wait_ge(sem("attn_lo"), NT)
            for t in range(NT):
                act.dma_start(x[:, t, :], a["x"][0, t * P:(t + 1) * P, :]).then_inc(sem(f"x_in{t}"), 16)

            for g in range(4):
                act.wait_ge(sem("gate_mm"), g + 1)
                dst = (gate1, gate2)[g // 2][:, (g % 2) * HALF:(g % 2 + 1) * HALF]
                s.activation(dst, ps[:, g, :], ACT.Copy).then_inc(sem("gate_out"), 1)
            norm(1, 1, lambda e, t: e.wait_ge(sem("x_mixed"), NT + t + 1),
                 lambda c: scl[:, 1, c:c + 1], lambda c: mod[:, 3 * NK + c:3 * NK + c + 1])

            def mlp(k):
                with act.Fori(0, GROUPS) as g:
                    for b in range(9):
                        if b < 8:
                            act.wait_ge(sem(f"up_full{k}"), g * 8 + (b + 1))
                            act.wait_ge(sem(f"u_lo{k}"), g * 8 + (b + 1))
                            s.activation(act_r[:, b % 4, :], ps[:, b, :], ACT.Relu).then_inc(sem(f"up_relu{k}"), 1)
                        if b:
                            c = b - 1
                            act.wait_ge(sem(f"u_sq{k}"), g * 8 + (c + 1))
                            s.activation(u_hi[:, c // 2, (c % 2) * HALF:(c % 2 + 1) * HALF], act_r[:, c % 4, :],
                                         ACT.Copy).then_inc(sem(f"u_hi{k}"), 1)

            mlp(0)
            act.dma_start(frow, a["g_final"].rearrange("(o d) -> o d", o=1).to_broadcast([P, D])).then_inc(sem("frow_in"), 16)
            act.dma_start(abraw, w_in_2[:, :, ABC:ABC + 2 * GH]).then_inc(sem("ab_in"), 16)
            act.dma_start(dtb, a["dt_bias_2"].to_broadcast([P, GH])).then_inc(sem("gs_in"), 16)
            act.dma_start(alog, a["a_log_2"].to_broadcast([P, GH])).then_inc(sem("gs_in"), 16)
            act.dma_start(wpool, a["w_pool_2"].rearrange("l g c d -> (l c) g d")).then_inc(sem("wpool_in"), 16)
            stats(2, lambda e, t: e.wait_ge(sem("x_sum0"), 2 + 16 * (GROUPS - 1) + NT + t + 1))
            norm(3, 2, lambda e, t: e.wait_ge(sem("x_final"), t + 1), lambda c: vcol("norm_mix_2", c), lambda c: zero)

            def chunk_of(c):
                return (qc, kc, vc)[c // GH][:, c % GH, :]

            def pair(i):
                return ps[:, 2 * (i % 3):2 * (i % 3) + 2, :].rearrange("p a b -> p (a b)")

            def aux_out(i):
                kind, c = CH2[i]
                y = yt[:, i % 2, :]
                both = ps[:, 6:8, :].rearrange("p a b -> p (a b)")
                if kind == "pool":
                    act.wait_ge(sem("pool_mm"), c + 1)
                    s.activation(pm[:, c, :], both, ACT.Copy, scale=vcol("pool_scale_2", c)).then_inc(sem("pm_out"), 1)
                if kind == "qkv" and c < 2 * GH:
                    act.wait_ge(sem("l2_mm"), c + 1)
                    s.activation(y, both, ACT.Sqrt, scale=float(GD) if c < GH else 1.0,
                                 bias=eps2 if c < GH else eps).then_inc(sem("l2_sd"), 1)

            act.wait_ge(sem("x_out"), 16 * NT)
            for i in range(len(CH2) + 1):
                if i < len(CH2):
                    kind, c = CH2[i]
                    y = yt[:, i % 2, :]
                    act.wait_ge(sem("cm2_full"), 2 * i + 2)
                    if i >= 2 and ch_free[i - 2]:
                        act.wait_ge(sem(ch_free[i - 2][0]), ch_free[i - 2][1])
                    if kind == "pool":
                        s.activation(y, pair(i), ACT.Copy).then_inc(sem("pool_u"), 1)
                    if kind == "qkv":
                        s.activation(y, pair(i), ACT.Copy,
                                     scale=cw2[:, 3 * 12 + c:3 * 12 + c + 1]).then_inc(sem("tap0"), 1)
                    if kind == "z":
                        s.activation(zc[:, c, :], pair(i), ACT.Sigmoid).then_inc(sem("z_sig"), 1)
                if i:
                    aux_out(i - 1)
                if i < len(CH2) and kind == "qkv":
                    act.wait_ge(sem("taps"), 3 * (c + 1))
                    s.activation(chunk_of(c), y, ACT.Sigmoid).then_inc(sem("conv_sig"), 1)
                    if c < 2 * GH:
                        act.wait_ge(sem("conv_silu"), c + 1)
                        s.activation(y, chunk_of(c), ACT.Square).then_inc(sem("l2_sq"), 1)

            act.wait_ge(sem("gs_dve"), 1)
            s.activation(gs["t2"], gs["t1"], ACT.Abs).then_inc(sem("gs_act"), 1)
            act.wait_ge(sem("gs_act"), 1)
            s.activation(gs["t2"], gs["t2"], ACT.Exp, scale=-1.0).then_inc(sem("gs_act"), 1)
            act.wait_ge(sem("gs_act"), 2)
            s.activation(gs["t2"], gs["t2"], ACT.Ln, bias=1.0).then_inc(sem("gs_act"), 1)
            act.wait_ge(sem("gs_in"), 32)
            s.activation(alog, alog, ACT.Exp).then_inc(sem("gs_act"), 1)
            s.activation(gs["beta"], ab[:, :, GH:], ACT.Sigmoid).then_inc(sem("gs_act"), 1)
            act.wait_ge(sem("gs_dve"), 3)
            s.activation(gs["egc"], gs["gcum"], ACT.Exp).then_inc(sem("gs_act"), 1)
            act.wait_ge(sem("gs_dve"), 4)
            s.activation(gs["edec"], gs["edec"], ACT.Exp).then_inc(sem("gs_act"), 1)

            for kind, t, l in GSTEPS:
                b = prep[t % 2]
                x0, x1, x2 = (bank(3 * (t % 2) + i) for i in range(3))
                if kind == "head":
                    act.wait_ge(prep_sem("dve", t), prep_count("dve", t, "df"))
                    if t >= 2:
                        act.wait_ge(sem("scan_dve"), scan_count("dve", t - 2, "sdec1"))
                    s.activation(b["egb"], x0, ACT.Exp).then_inc(prep_sem("act", t), 1)
                    act.wait_ge(prep_sem("dve", t), prep_count("dve", t, "e12"))
                    s.activation(b["e1"], b["e1"], ACT.Exp, scale=-1.0).then_inc(prep_sem("act", t), 1)
                    s.activation(b["e2"], b["e2"], ACT.Exp).then_inc(prep_sem("act", t), 1)
                if kind == "level":
                    act.wait_ge(prep_sem("mm", t), prep_count("mm", t, f"z{l}"))
                    s.activation(b["z"], x0, ACT.Copy).then_inc(prep_sem("act", t), 1)
                if kind == "tail":
                    if t >= 2:
                        act.wait_ge(sem("scan_mm"), scan_count("mm", t - 2, "ai"))
                    act.wait_ge(prep_sem("mm", t), prep_count("mm", t, "val"))
                    s.activation(b["val"], x1, ACT.Copy).then_inc(prep_sem("act", t), 1)
                    act.wait_ge(prep_sem("mm", t), prep_count("mm", t, "kct"))
                    s.activation(b["kct"], x2, ACT.Copy).then_inc(prep_sem("act", t), 1)
                if kind == "finish":
                    act.wait_ge(sem("scan_mm"), scan_count("mm", t, "ai"))
                    s.activation(ot, bank(7), ACT.Copy).then_inc(sem("scan_act"), 1)
                    act.wait_ge(sem("scan_dve"), scan_count("dve", t, "sum"))
                    s.activation(osum, osum, ACT.Sqrt, scale=1.0 / GD, bias=eps).then_inc(sem("scan_act"), 1)

            act.wait_ge(sem("scan_dve"), scan_count("dve", NT - 1, "gated"))
            for t in range(NT):
                act.dma_start(x[:, t, :], x_mid[t]).then_inc(sem(f"x_in{t}"), 16)
            for u in range(2 * NK):
                c, cols = u // 2, slice((u % 2) * HALF, (u % 2 + 1) * HALF)
                src = pm[:, c, cols] if c < GH else zc[:, c - GH, cols]
                s.activation(h_hi[:, c, cols], src, ACT.Copy).then_inc(sem("mix2_hi"), 1)
            act.dma_start(frow, a["norm_final_2"].rearrange("(o d) -> o d", o=1).to_broadcast([P, D])).then_inc(sem("frow_in"), 16)
            norm(4, 3, lambda e, t: e.wait_ge(sem("x_mixed2"), NT + t + 1), lambda c: vcol("norm_mlp_2", c), lambda c: zero)
            mlp(1)
            stats(5, lambda e, t: e.wait_ge(sem("down_out1"), 16 + 16 * (GROUPS - 1) + NT + t + 1))

        @block.vector
        def _(dve):
            v = nc.vector
            chain = [0]

            def link(ins):
                chain[0] += 1
                ins.then_inc(sem("dve_step"), 1)
                dve.wait_ge(sem("dve_step"), chain[0])

            dve.wait_ge(sem("rows_tp"), 1)
            v.tensor_copy(vec[:, 0:NVEC], ps[:, 0, 0:NVEC]).then_inc(sem("vec_ready"), 1)
            link(v.tensor_copy(cw[:, 0:CONV_K * NCC], ps[:, 1, 0:CONV_K * NCC]))
            link(v.tensor_copy(cw2, ps[:, 2, 0:TAPS * 12]))
            dve.wait_ge(sem("c_sig"), 1)
            dve.wait_ge(sem("vec_ready"), 1)
            v.tensor_tensor(csil, csil, vcols("c"), ALU.mult).then_inc(sem("csil_ready"), 1)
            dve.wait_ge(sem("rows_in"), 16 * (len(VEC) + 3))
            v.tensor_copy(rowsp, rowsi).then_inc(sem("rowsp_ready"), 1)
            dve.wait_ge(sem("pos_tp"), 1)
            link(v.tensor_copy(pos, ps[:, 3, 0:NT]))
            dve.wait_ge(sem("pool_mem"), 3 + HROT)
            bc = [P, NT, HROT]
            link(v.tensor_tensor(angt[:, 0], pos.unsqueeze(2).to_broadcast(bc),
                                 freq.unsqueeze(1).to_broadcast(bc), ALU.mult))
            MAGIC = 1.5 * 2.0 ** 23
            link(v.tensor_scalar(angt[:, 1], angt[:, 0], 1.0 / (2 * np.pi), MAGIC, ALU.mult, ALU.add))
            link(v.tensor_scalar(angt[:, 1], angt[:, 1], -MAGIC, None, ALU.add))
            c1 = 6.28125
            c2 = float(np.float32(round((2 * np.pi - c1) * 2 ** 20) / 2 ** 20))
            c3 = 2 * np.pi - c1 - c2
            for cc in (c1, c2, c3):
                link(v.scalar_tensor_tensor(angt[:, 0], angt[:, 1], -cc, angt[:, 0], ALU.mult, ALU.add))
            v.tensor_scalar(angt[:, 0], angt[:, 0], 3.1415925, -3.1415925, ALU.min,
                            ALU.max).then_inc(sem("angle_ready"), 1)
            dve.wait_ge(sem("sines"), 2)
            link(v.tensor_tensor(cosv, angt[:, 1], angt[:, 1], ALU.mult))
            link(v.tensor_scalar(cosv, cosv, -2.0, 1.0, ALU.mult, ALU.add))

            dve.wait_ge(sem("ada_done"), 2 * NK)
            link(v.tensor_tensor(mod[:, 0:2 * NK], ps[:, 4, 0:2 * NK], vec[:, VEC["b_ada"][0]:VEC["b_ada"][0] + 2 * NK], ALU.add))
            v.scalar_tensor_tensor(scl[:, 0, :], mod[:, NK:2 * NK], 1.0, vcols("g_mix"), ALU.add,
                                   ALU.mult).then_inc(sem("scale_ready"), 1)

            def norm(q, k):
                for half in range(2):
                    dve.wait_ge(sem("norm_sd"), 2 * q + half + 1)
                    link(v.reciprocal(rs[:, 4 * half:4 * half + 4], sd[:, 4 * half:4 * half + 4]))
                    for t in range(4 * half, 4 * half + 4):
                        v.tensor_scalar(xn[:, t, :], x[:, t, :], rs[:, t:t + 1], None,
                                        ALU.mult).then_inc(sem("norm_xn"), 1)
                for u in range(2 * NK):
                    c, half = u % NK, u // NK
                    cols = slice(half * HALF, (half + 1) * HALF)
                    n = 2 * NK * k + u + 1
                    dve.wait_ge(sem("norm_f"), n)
                    v.tensor_copy(h_hi[:, c, cols], tmp2[:, u % 2, :]).then_inc(sem("norm_hi"), 1)
                    dve.wait_ge(sem("norm_hi"), n)
                    v.tensor_tensor(h_lo[:, c, cols], tmp2[:, u % 2, :], h_hi[:, c, cols].bitcast(F32),
                                    ALU.subtract).then_inc(sem("norm_lo"), 1)

            norm(0, 0)

            for t in range(NT):
                dve.wait_ge(sem("tm_full"), NT + t + 1)
                v.tensor_copy(pr1[:, t, 0:P], ps[:, t, 0:P]).then_inc(sem("tm_out1"), 1)
                v.tensor_copy(vtok[:, t, :], ps[:, t, P:2 * P]).then_inc(sem("tm_out1"), 1)
                v.tensor_copy(pr1[:, t, P:384], ps[:, t, 256:512]).then_inc(sem("tm_out1"), 1)

            def rope(ap, heads, name):
                sh = [P, NT, heads, HROT]
                x1, x2 = ap[:, :, :, 0:HROT], ap[:, :, :, HROT:ROT]
                co = cosv.unsqueeze(2).to_broadcast(sh)
                si = sinv.unsqueeze(2).to_broadcast(sh)
                t1, t2, t3, t4 = (ropet[:, i, 0:NT * heads * HROT].rearrange("p (t h r) -> p t h r", t=NT, r=HROT)
                                  for i in range(4))
                v.tensor_tensor(t1, x1, co, ALU.mult).then_inc(sem("rope_t"), 1)
                v.tensor_tensor(t2, x2, si, ALU.mult).then_inc(sem("rope_t"), 1)
                v.tensor_tensor(t3, x2, co, ALU.mult).then_inc(sem("rope_t"), 1)
                v.tensor_tensor(t4, x1, si, ALU.mult).then_inc(sem("rope_t"), 1)
                rope.n += 4
                dve.wait_ge(sem("rope_t"), rope.n)
                v.tensor_tensor(x1, t1, t2, ALU.subtract).then_inc(sem("roped"), 1)
                v.tensor_tensor(x2, t3, t4, ALU.add).then_inc(sem("roped"), 1)
                rope.m += 2
                dve.wait_ge(sem("roped"), rope.m)

            rope.n = rope.m = 0
            dve.wait_ge(sem("tm_out0"), NT)
            rope(pr0.rearrange("p t (h d) -> p t h d", d=HD), 8, "q")
            dve.wait_ge(sem("tm_out1"), 3 * NT)
            rope(pr1[:, :, 0:P].rearrange("p t (h d) -> p t h d", d=HD), 2, "k")
            rope(pr1[:, :, P:384].rearrange("p t (h d) -> p t h d", d=HD), 4, "qia")
            for t in range(NT):
                dve.wait_ge(sem("tm_full"), 2 * NT + t + 1)
                dve.wait_ge(sem("tm_out2a"), 3 * (t + 1))
                v.tensor_scalar(wi[:, t, :], ps[:, t, COL_WI - 1024:COL_WI - 1024 + NH], NH ** -0.5, None,
                                ALU.mult).then_inc(sem("tm_out2b"), 1)
            rope(pr2[:, :, 0:256].rearrange("p t (h d) -> p t h d", d=HD), 4, "qib")
            rope(pr2[:, :, 256:384].rearrange("p t (h d) -> p t h d", d=HD), 2, "ki")

            for c in range(NCC):
                b = (4 * c) % 8
                for half in range(2):
                    dve.wait_ge(sem("pr_turned"), 20)
                    dve.wait_ge(sem("cm_full"), 4 * c + half + 1)
                    dve.wait_ge(sem("glu_sig"), 2 * c + half + 1)
                    v.tensor_tensor(glu[:, c, half * HALF:(half + 1) * HALF], ps[:, b + half, :],
                                    tmp2[:, half, :], ALU.mult).then_inc(sem("glu_ready"), 1)
            dve.wait_ge(sem("cm_full"), 4 * NCC)

            def topk(t, r0, r1):
                sc = score[t % 3][:, 0:(t + 1) * P]
                dve.wait_ge(sem("acc_done"), NH * (t - IDX_TILES[0] + 1))
                for r in range(r0, r1):
                    n = 2 * (ROUNDS * (t - IDX_TILES[0]) + r)
                    v.max(best, sc).then_inc(sem("topk_step"), 1)
                    dve.wait_ge(sem("topk_step"), n + 1)
                    v.match_replace(sc, best, sc, TAKEN).then_inc(sem("topk_step"), 1)
                    dve.wait_ge(sem("topk_step"), n + 2)
                if r1 == ROUNDS:
                    link(v.tensor_scalar(sc, sc, TAKEN, MASKED, ALU.not_equal, ALU.mult))

            dve.wait_ge(sem("idx_ready"), 1)
            dve.wait_ge(sem("tm_out2b"), NT)
            nmod = 0
            for kind, t, i in MICRO:
                w = (t + 1) * P
                cols = slice(t * HALF, (t + 1) * HALF)
                if kind == "index":
                    sc = score[t % 3][:, 0:w]
                    n = NH * (t - IDX_TILES[0]) + i
                    dve.wait_ge(sem("relu_done"), n + 1)
                    if i:
                        dve.wait_ge(sem("acc_done"), n)
                    v.scalar_tensor_tensor(sc, relu[:, n % 2, 0:w], wi[:, t, i:i + 1],
                                           sc if i else idx0[:, S - w:S], ALU.mult,
                                           ALU.add).then_inc(sem("acc_done"), 1)
                if kind == "scores":
                    bias = idx0[:, S - w:S] if t < IDX_TILES[0] else score[t % 3][:, 0:w]
                    h = HEADS[i]
                    n = NH * t + i
                    u = unit_of[kind, t, i]
                    dve.wait_ge(sem("score_full"), u + 1)
                    if n >= 2:
                        dve.wait_ge(sem("tp_full"), tp_last[n - 2])
                    v.tensor_tensor_reduce(prob[:, n % 2, 0:w],
                                           ps[:, 2 * (u % 2):2 * (u % 2) + 2, :]
                                           .rearrange("p a b -> p (a b)")[:, 0:w], bias, 1.0, -3.4e38,
                                           ALU.add, ALU.max, smax[:, h:h + 1]).then_inc(sem("masked"), 1)
                    dve.wait_ge(sem("masked"), n + 1)
                    if n >= NH:
                        dve.wait_ge(sem("exp_done"), n - NH + 1)
                    v.tensor_scalar(snm[:, h:h + 1], smax[:, h:h + 1], -HD ** -0.5, None,
                                    ALU.mult).then_inc(sem("smax_ready"), 1)
                if kind == "topk":
                    topk(t, ROUNDS * i // TOPK_PARTS[t], ROUNDS * (i + 1) // TOPK_PARTS[t])
                if kind == "divide":
                    dve.wait_ge(sem("exp_done"), NH * (t + 1))
                    link(v.reciprocal(srec, ssum[:, t % 2, :]))
                    dve.wait_ge(sem("pv_done"), NH * (t + 1))
                    if t:
                        dve.wait_ge(sem("attn_lo"), t)
                    v.tensor_tensor(v3(otok, NH), v3(ps[:, 6, :], NH), srec.unsqueeze(2).to_broadcast([P, NH, HD]),
                                    ALU.mult).then_inc(sem("o_ready"), 1)
                if kind == "out":
                    u = tp_of[t, "o"]
                    dve.wait_ge(sem("attn_hi"), t + 1)
                    v.tensor_tensor(h_lo[:, 0:4, t * P:(t + 1) * P], v3(ps[:, 4 + u % 2, :], 4),
                                    h_hi[:, 0:4, t * P:(t + 1) * P].bitcast(F32),
                                    ALU.subtract).then_inc(sem("attn_lo"), 1)
                if kind == "ada":
                    u = tp_of["ada", t]
                    m0 = 2 * NK + t
                    dve.wait_ge(sem("ada_done"), 2 * NK + i)
                    v.tensor_tensor(mod[:, m0:2 * NK + i], ps[:, 4 + u % 2, 0:i - t],
                                    vec[:, VEC["b_ada"][0] + m0:VEC["b_ada"][0] + 2 * NK + i],
                                    ALU.add).then_inc(sem("mod_out"), 1)
                    nmod += 1
                    if i == 4 * NK:
                        dve.wait_ge(sem("mod_out"), nmod)
                        v.scalar_tensor_tensor(scl[:, 1, :], mod[:, 4 * NK:5 * NK], 1.0, vcols("g_mlp"), ALU.add,
                                               ALU.mult).then_inc(sem("scale_ready"), 1)
                if kind == "ln_mean":
                    dve.wait_ge(sem("ln_mean"), t + 1)
                    for c in range(NCC):
                        v.scalar_tensor_tensor(conv[:, c, cols], ps[:, 7, :], -1.0 / CONV_CH, conv[:, c, cols],
                                               ALU.mult, ALU.add).then_inc(sem("ln_cent"), 1)
                if kind == "ln_scale":
                    dve.wait_ge(sem("ln_sd"), t + 1)
                    link(v.reciprocal(tmp2[:, 1, :], tmp2[:, 1, :]))
                    for c in range(NCC):
                        v.tensor_tensor(conv[:, c, cols], conv[:, c, cols], tmp2[:, 1, :],
                                        ALU.mult).then_inc(sem("ln_scaled"), 1)
                    for c in range(NCC):
                        dve.wait_ge(sem("ln_scaled"), NCC * t + c + 1)
                        v.tensor_scalar(conv[:, c, cols], conv[:, c, cols], vcol("conv_norm_g", c),
                                        vcol("conv_norm_b", c), ALU.mult, ALU.add).then_inc(sem("ln_aff"), 1)
                if kind == "ln_silu":
                    for c in range(NCC):
                        n = NCC * t + c + 1
                        dve.wait_ge(sem("ln_sig"), n)
                        v.tensor_tensor(conv[:, c, cols], conv[:, c, cols], tmp2[:, 0, :],
                                        ALU.mult).then_inc(sem("ln_silu"), 1)
                        dve.wait_ge(sem("conv_hi"), n)
                        v.tensor_tensor(h_lo[:, 4 + c, cols], conv[:, c, cols], h_hi[:, 4 + c, cols].bitcast(F32),
                                        ALU.subtract).then_inc(sem("conv_lo"), 1)
            for gi, base in enumerate((2 * NK, 5 * NK)):
                for c in range(NK):
                    if gi:
                        dve.wait_ge(sem("gate_mm"), 1 + c // 4)
                    v.tensor_scalar(gdiag[:, c, :], ident, mod[:, base + c:base + c + 1], None,
                                    ALU.mult).then_inc(sem("gdiag_ready"), 1)
            for j in range(2):
                for t in range(NT):
                    n = NT * j + t
                    dve.wait_ge(sem("wo_full"), n + 1)
                    if j == 0:
                        dve.wait_ge(sem(f"x_in{t}"), 32)
                    if j == 0 and t == 0:
                        dve.wait_ge(sem("gate_out"), 4)
                    if n >= 2:
                        dve.wait_ge(sem("x_mixed"), n - 1)
                    cols = slice(j * HALF, (j + 1) * HALF)
                    v.tensor_tensor(tmp2[:, n % 2, :], ps[:, t, :], gate1[:, cols], ALU.mult).then_inc(sem("gated"), 1)
                    dve.wait_ge(sem("gated"), n + 1)
                    v.tensor_tensor(x[:, t, cols], x[:, t, cols], tmp2[:, n % 2, :], ALU.add).then_inc(sem("x_mixed"), 1)
            norm(1, 1)

            def mlp(k, gate):
                with dve.Fori(0, GROUPS) as g:
                    for b in range(9):
                        if b < 8:
                            dve.wait_ge(sem(f"up_relu{k}"), g * 8 + (b + 1))
                            v.tensor_tensor(act_r[:, b % 4, :], act_r[:, b % 4, :], act_r[:, b % 4, :],
                                            ALU.mult).then_inc(sem(f"u_sq{k}"), 1)
                        if b:
                            c = b - 1
                            cols = slice((c % 2) * HALF, (c % 2 + 1) * HALF)
                            dve.wait_ge(sem(f"u_hi{k}"), g * 8 + (c + 1))
                            v.tensor_tensor(u_lo[:, c // 2, cols], act_r[:, c % 4, :],
                                            u_hi[:, c // 2, cols].bitcast(F32), ALU.subtract).then_inc(sem(f"u_lo{k}"), 1)
                    for n in range(2 * NT):
                        j, t = n // NT, n % NT
                        cols = slice(j * HALF, (j + 1) * HALF)
                        dve.wait_ge(sem(f"down_full{k}"), g * 16 + (n + 1 + 16))
                        if gate is None:
                            v.tensor_tensor(x[:, t, cols], x[:, t, cols], ps[:, t, :],
                                            ALU.add).then_inc(sem(f"down_out{k}"), 1)
                        else:
                            dve.wait_ge(sem(f"x_sum{k}"), g * 16 + (n + 1))
                            v.tensor_tensor(tmp2[:, n % 2, :], ps[:, t, :], gate[:, cols],
                                            ALU.mult).then_inc(sem(f"down_out{k}"), 1)
                            dve.wait_ge(sem(f"down_out{k}"), g * 16 + (n + 1 + 16))
                            v.tensor_tensor(x[:, t, cols], x[:, t, cols], tmp2[:, n % 2, :],
                                            ALU.add).then_inc(sem(f"x_sum{k}"), 1)

            def mlp_start(k):
                dve.sem_inc(sem(f"down_out{k}"), 16)
                dve.sem_inc(sem(f"u_lo{k}"), 4)
                dve.sem_inc(sem(f"x_sum{k}"), 2)

            def final(q, done):
                for half in range(2):
                    dve.wait_ge(sem("norm_sd"), 2 * q + half + 1)
                    link(v.reciprocal(rs[:, 4 * half:4 * half + 4], sd[:, 4 * half:4 * half + 4]))
                    for t in range(4 * half, 4 * half + 4):
                        v.scalar_tensor_tensor(x[:, t, :], x[:, t, :], rs[:, t:t + 1], frow, ALU.mult,
                                               ALU.mult).then_inc(sem(done), 1)

            mlp_start(0)
            mlp(0, gate2)
            dve.wait_ge(sem("frow_in"), 16)
            final(2, "x_final")
            norm(3, 2)

            def chunk_of(c):
                return (qc, kc, vc)[c // GH][:, c % GH, :]

            def pair(i):
                return ps[:, 2 * (i % 3):2 * (i % 3) + 2, :].rearrange("p a b -> p (a b)")

            ntap = [0]
            for i in range(len(CH2) + 1):
                if i < len(CH2):
                    kind, c = CH2[i]
                    y = yt[:, i % 2, :]
                    if i == 0:
                        dve.wait_ge(sem("ab_full"), 1)
                        v.tensor_copy(ab, ps[:, 6, 0:NT * 2 * GH].rearrange("p (t n) -> p t n", t=NT)).then_inc(sem("ab_out"), 1)
                    if kind == "pool":
                        dve.wait_ge(sem("pool_u"), c + 1)
                        w, src = WINDOWS[c], y
                        k, d = 0, 1
                        while d < w:
                            dst = (zc, pm)[k % 2][:, c, :]
                            v.tensor_copy(dst[:, 0:d], src[:, 0:d])
                            link(v.tensor_tensor(dst[:, d:], src[:, d:], src[:, 0:S - d], ALU.add))
                            src, k, d = dst, k + 1, 2 * d
                        e = w - 1
                        link(v.tensor_tensor(src[:, 0:e], src[:, 0:e], invc[:, 0:e], ALU.mult))
                        v.tensor_tensor(y[:, 0:e], src[:, 0:e], y[:, 0:e], ALU.subtract).then_inc(sem("pooled"), 1)
                        v.scalar_tensor_tensor(y[:, e:], src[:, e:], 1.0 / w, y[:, e:], ALU.mult,
                                               ALU.subtract).then_inc(sem("pooled"), 1)
                    if kind == "qkv":
                        dve.wait_ge(sem("tap0"), c + 1)
                        for sft in range(1, TAPS):
                            if ntap[0] % 3:
                                dve.wait_ge(sem("taps"), ntap[0])
                            col = (TAPS - 1 - sft) * 12 + c
                            v.scalar_tensor_tensor(y[:, sft:], pair(i)[:, 0:S - sft], cw2[:, col:col + 1], y[:, sft:],
                                                   ALU.mult, ALU.add).then_inc(sem("taps"), 1)
                            ntap[0] += 1
                    if kind == "z":
                        dve.wait_ge(sem("z_sig"), c + 1)
                        v.tensor_tensor(zc[:, c, :], pair(i), zc[:, c, :], ALU.mult).then_inc(sem("z_silu"), 1)
                if i:
                    kind1, c1 = CH2[i - 1]
                    if kind1 == "qkv" and c1 < 2 * GH:
                        y1 = yt[:, (i - 1) % 2, :]
                        dve.wait_ge(sem("l2_sd"), c1 + 1)
                        link(v.reciprocal(y1, y1))
                        v.tensor_tensor(chunk_of(c1), chunk_of(c1), y1, ALU.mult).then_inc(sem("l2_done"), 1)
                if i < len(CH2) and kind == "qkv":
                    dve.wait_ge(sem("conv_sig"), c + 1)
                    v.tensor_tensor(chunk_of(c), chunk_of(c), y, ALU.mult).then_inc(sem("conv_silu"), 1)

            tn = [P, NT, GH]
            dve.wait_ge(sem("gs_in"), 32)
            dve.wait_ge(sem("ab_out"), 1)
            v.tensor_tensor(gs["t1"], ab[:, :, 0:GH], dtb.unsqueeze(1).to_broadcast(tn), ALU.add).then_inc(sem("gs_dve"), 1)
            dve.wait_ge(sem("gs_act"), 4)
            link(v.tensor_scalar(gs["t1"], gs["t1"], 0.0, None, ALU.max))
            link(v.tensor_tensor(gs["t1"], gs["t1"], gs["t2"], ALU.add))
            v.scalar_tensor_tensor(gs["g"], gs["t1"], -1.0, alog.unsqueeze(1).to_broadcast(tn), ALU.mult,
                                   ALU.mult).then_inc(sem("gs_dve"), 1)
            dve.wait_ge(sem("gs_mm"), 2)
            v.tensor_copy(gs["gcum"], ps[:, 6, 0:32].rearrange("p (t h) -> p t h", h=GH)).then_inc(sem("gs_dve"), 1)
            dve.wait_ge(sem("gs_dve"), 3)
            v.tensor_tensor(gs["edec"], ps[:, 6, 32:64].rearrange("p (t h) -> p t h", h=GH), gs["gcum"],
                            ALU.subtract).then_inc(sem("gs_dve"), 1)
            dve.wait_ge(sem("gs_act"), 7)
            link(v.tensor_tensor(gs["bege"], gs["beta"], gs["egc"], ALU.mult))
            dve.wait_ge(sem("masks_ready"), 1)

            for kind, t, l in GSTEPS:
                b = prep[t % 2]
                x0, x1, x2 = (bank(3 * (t % 2) + i) for i in range(3))
                if kind == "head":
                    if t >= 2:
                        dve.wait_ge(prep_sem("mm", t - 2), prep_count("mm", t - 2, "kct"))
                    v.tensor_tensor(b["z"], hb(tri), tb(gs["g"][:, t, :]), ALU.mult).then_inc(prep_sem("dve", t), 1)
                    dve.wait_ge(prep_sem("mm", t), prep_count("mm", t, "gb"))
                    v.tensor_tensor(b["e1"], x0, tb(gs["gcum"][:, t, :]), ALU.subtract).then_inc(prep_sem("dve", t), 1)
                    dve.wait_ge(prep_sem("dve", t), prep_count("dve", t, "df"))
                    link(v.tensor_scalar(b["e2"], b["e1"], 0.0, None, ALU.min))
                    v.tensor_scalar(b["e1"], b["e1"], 0.0, None, ALU.max).then_inc(prep_sem("dve", t), 1)
                    dve.wait_ge(prep_sem("mm", t), prep_count("mm", t, "gram"))
                    dve.wait_ge(prep_sem("pool", t), prep_count("pool", t, "e1m"))
                    for h in range(GH):
                        last = v.scalar_tensor_tensor(b["m"][:, h, :], x1[:, h, :], gs["beta"][:, t, h:h + 1],
                                                      b["e1"][:, h, :], ALU.mult, ALU.mult)
                    last.then_inc(prep_sem("dve", t), 1)
                    dve.wait_ge(prep_sem("mm", t), prep_count("mm", t, "kq"))
                    dve.wait_ge(prep_sem("pool", t), prep_count("pool", t, "e2m"))
                    if t >= 2:
                        dve.wait_ge(sem("scan_mm"), scan_count("mm", t - 2, "ai"))
                    v.tensor_tensor(b["ait"], x2, b["e2"], ALU.mult).then_inc(prep_sem("dve", t), 1)
                    dve.wait_ge(prep_sem("mm", t), prep_count("mm", t, "turn"))
                    v.tensor_tensor(b["u"], hb(ident), x0, ALU.subtract).then_inc(prep_sem("dve", t), 1)
                if kind == "level":
                    dve.wait_ge(prep_sem("mm", t), prep_count("mm", t, f"u{l}"))
                    if l < 5:
                        if l == 1:
                            dve.wait_ge(prep_sem("pool", t), prep_count("pool", t, "t0"))
                        v.tensor_tensor(b["t"], b["t"], x1, ALU.subtract).then_inc(prep_sem("dve", t), 1)
                    v.tensor_tensor(b["u"], b["u"], x2, ALU.subtract).then_inc(prep_sem("dve", t), 1)
                if kind == "tail":
                    dve.wait_ge(prep_sem("mm", t), prep_count("mm", t, "ktp"))
                    v.tensor_tensor(b["kbe"], x0, tb(gs["bege"][:, t, :]), ALU.mult).then_inc(prep_sem("dve", t), 1)
                    if t >= 2:
                        dve.wait_ge(sem("scan_mm"), scan_count("mm", t - 2, "kdv1"))
                    v.tensor_tensor(b["kd"], x0, tb(gs["edec"][:, t, :]), ALU.mult).then_inc(prep_sem("dve", t), 1)
                    dve.wait_ge(prep_sem("mm", t), prep_count("mm", t, "vtp"))
                    v.tensor_tensor(b["vb"], x1, tb(gs["beta"][:, t, :]), ALU.mult).then_inc(prep_sem("dve", t), 1)
                if kind == "chunk":
                    r = slice(CHUNK * l, CHUNK * (l + 1))
                    e = CHUNK * (l + 1) - 1
                    dve.wait_ge(sem("scan_mm"), scan_count("mm", t, f"kq{l}"))
                    if l == 0 and t:
                        dve.wait_ge(sem("scan_mm"), scan_count("mm", t - 1, "ai"))
                        dve.wait_ge(sem("scan_dve"), scan_count("dve", t - 1, "sum"))
                    v.tensor_tensor(vnew[r], b["val"][r], bank(6)[r], ALU.subtract).then_inc(sem("scan_dve"), 1)
                    v.tensor_tensor(state, state, b["egb"][:, :, e:e + 1].to_broadcast([P, GH, P]),
                                    ALU.mult).then_inc(sem("scan_dve"), 1)
                    dve.wait_ge(sem("scan_mm"), scan_count("mm", t, f"kdv{l}"))
                    dve.wait_ge(sem("scan_dve"), scan_count("dve", t, f"sdec{l}"))
                    v.tensor_tensor(state, state, bank(6), ALU.add).then_inc(sem("scan_dve"), 1)
                if kind == "finish":
                    dve.wait_ge(sem("scan_act"), scan_count("act", t, "ot"))
                    v.tensor_tensor(vnew, ot, ot, ALU.mult).then_inc(sem("scan_dve"), 1)
                    dve.wait_ge(sem("scan_dve"), scan_count("dve", t, "sq"))
                    v.tensor_reduce(osum, vnew, AX.X, ALU.add).then_inc(sem("scan_dve"), 1)
                    dve.wait_ge(sem("scan_act"), scan_count("act", t, "sd"))
                    v.reciprocal(orec, osum).then_inc(sem("scan_dve"), 1)
                    dve.wait_ge(sem("scan_dve"), scan_count("dve", t, "rec"))
                    v.tensor_tensor(ot, ot, tb(orec), ALU.mult).then_inc(sem("scan_dve"), 1)
                    dve.wait_ge(sem("scan_mm"), scan_count("mm", t, "otp"))
                    zt = zc[:, :, t * P:(t + 1) * P]
                    v.scalar_tensor_tensor(zt, bank(7), vcol("gdn_norm_2"), zt, ALU.mult,
                                           ALU.mult).then_inc(sem("scan_dve"), 1)

            for u in range(2 * NK):
                c, cols = u // 2, slice((u % 2) * HALF, (u % 2 + 1) * HALF)
                src = pm[:, c, cols] if c < GH else zc[:, c - GH, cols]
                dve.wait_ge(sem("mix2_hi"), u + 1)
                v.tensor_tensor(h_lo[:, c, cols], src, h_hi[:, c, cols].bitcast(F32),
                                ALU.subtract).then_inc(sem("mix2_lo"), 1)
            for j in range(2):
                for t in range(NT):
                    cols = slice(j * HALF, (j + 1) * HALF)
                    dve.wait_ge(sem("wo2_full"), NT * j + t + 1)
                    if j == 0:
                        dve.wait_ge(sem(f"x_in{t}"), 48)
                    v.tensor_tensor(x[:, t, cols], x[:, t, cols], ps[:, t, :], ALU.add).then_inc(sem("x_mixed2"), 1)
            norm(4, 3)
            dve.sem_inc(sem("down_out1"), 16)
            dve.sem_inc(sem("u_lo1"), 4)
            mlp(1, None)
            dve.wait_ge(sem("frow_in"), 32)
            final(5, "y_final")

        @block.tensor
        def _(pe):
            mm = nc.tensor.matmul
            pe.wait_ge(sem("ident_ready"), 2)
            pe.wait_ge(sem("rows_in"), 16 * (len(VEC) + 3))
            nc.tensor.transpose(ps[:, 0, 0:NVEC], rowsv[0:NVEC, 0, :], ident[0:NVEC, 0:NVEC])
            n = CONV_K * NCC
            nc.tensor.transpose(ps[:, 1, 0:n], rowsv[0:n, 1, :], ident[0:n, 0:n])
            n = TAPS * 12
            nc.tensor.transpose(ps[:, 2, 0:n], rowsv[0:n, 2, :], ident[0:n, 0:n]).then_inc(sem("rows_tp"), 1)
            pe.wait_ge(sem("rowsp_ready"), 1)
            nc.tensor.transpose(ps[:, 3, 0:NT], rowsp, ident[0:NT, 0:NT]).then_inc(sem("pos_tp"), 1)

            def ada(n, j, out_col):
                pe.wait_ge(raw_in[n % 4], 16 * (n // 4 + 1))
                wt = v3(raw[:, n % 4, :], NK)
                for k in range(NK):
                    last = mm(out_col, wt[:, k, :], csil[:, k:k + 1], start=(k == 0), stop=(k == NK - 1))
                last.then_inc(sem("ada_done"), 1)

            pe.wait_ge(sem("csil_ready"), 1)
            for j in range(2 * NK):
                ada(j, j, ps[:, 4, j:j + 1])

            def norm(k):
                for u in range(2 * NK):
                    c, half = u % NK, u // NK
                    if c == 0:
                        pe.wait_ge(sem("norm_xn"), NT * k + 4 * half + 4)
                    if u >= 8:
                        pe.wait_ge(sem("norm_f"), 2 * NK * k + u - 7)
                    for i in range(4):
                        last = nc.tensor.transpose(ps[:, u % 8, i * P:(i + 1) * P],
                                                   xn[:, 4 * half + i, c * P:(c + 1) * P], ident)
                    last.then_inc(sem("norm_turned"), 1)

            def cm(m, half, bank, ready, full):
                r = m % 4
                cols = slice(half * HALF, (half + 1) * HALF)
                for k in range(NK):
                    if ready:
                        ready(k)
                    wh, wl = (v3(w[:, r, :], NK)[:, k, :] for w in (w_hi, w_lo))
                    mm(ps[:, bank, :], wh, h_hi[:, k, cols], start=(k == 0), stop=False)
                    mm(ps[:, bank, :], wh, h_lo[:, k, cols], start=False, stop=False)
                    last = mm(ps[:, bank, :], wl, h_hi[:, k, cols], start=False, stop=(k == NK - 1))
                last.then_inc(sem(full), 1)

            def tm(m, t, k0, width, hi, lo, start, stop):
                r = m % 4
                tok = slice(t * P, (t + 1) * P)
                for k in range(2):
                    wh, wl = (w[:, r, 0:2 * width].rearrange("p (k n) -> p k n", k=2)[:, k, :] for w in (w_hi, w_lo))
                    mm(ps[:, t, 0:width], hi[:, k0 + k, tok], wh, start=(start and k == 0), stop=False)
                    mm(ps[:, t, 0:width], hi[:, k0 + k, tok], wl, start=False, stop=False)
                    last = mm(ps[:, t, 0:width], lo[:, k0 + k, tok], wh, start=False, stop=(stop and k == 1))
                return last

            norm(0)
            for j, (c0, width) in enumerate(TM_COLS):
                for kk in range(4):
                    m = 4 * j + kk
                    pe.wait_ge(sem("split_done"), m + 1)
                    for t in range(NT):
                        if j == 0 and t % 4 == 0:
                            pe.wait_ge(sem("norm_lo"), NK * (t // 4) + 2 * kk + 2)
                            if kk == 0:
                                pe.wait_ge(sem("norm_f"), 2 * NK)
                        if kk == 0 and j == 1:
                            pe.wait_ge(sem("tm_out0"), t + 1)
                        if kk == 0 and j == 2:
                            pe.wait_ge(sem("tm_out1"), 3 * (t + 1))
                        last = tm(m, t, 2 * kk, width, h_hi, h_lo, kk == 0, kk == 3)
                        if kk == 3:
                            last.then_inc(sem("tm_full"), 1)
                        elif t == NT - 1:
                            last.then_inc(sem("tm_part"), 1)

            def cu(i):
                c, part = i // 2, i % 2
                pe.wait_ge(sem("split_done"), 12 + i + 1)
                for half in range(2):
                    b = (4 * c) % 8 + 2 * part + half
                    if c == 0:
                        pe.wait_ge(sem("tm_out2a"), 3 * (b + 1))
                        pe.wait_ge(sem("tm_out2b"), b + 1)
                    if c == 1:
                        pe.wait_ge(sem("pr_turned"), 20)
                    if c >= 2:
                        pe.wait_ge(sem("glu_ready"), 2 * (c - 1))
                    cm(12 + i, half, b, None, "cm_full")

            cu(0)
            cu(1)
            pe.wait_ge(sem("roped"), 10)
            pe.wait_ge(sem("tm_out2a"), 3 * NT)
            pe.wait_ge(sem("tm_out2b"), NT)
            srcs = [pr0[:, :, j * P:(j + 1) * P] for j in range(4)] + [pr1[:, :, j * P:(j + 1) * P] for j in range(3)] \
                + [pr2[:, :, j * P:(j + 1) * P] for j in range(3)]
            for n in range(20):
                if n >= 4:
                    pe.wait_ge(sem("pr_turned"), n - 3)
                for i in range(4):
                    last = nc.tensor.transpose(ps[:, 4 + n % 4, i * P:(i + 1) * P],
                                               srcs[n // 2][:, 4 * (n % 2) + i, :], ident)
                last.then_inc(sem("pr_tp"), 1)
            for i in range(2, 2 * NCC):
                cu(i)

            def score_mm(kind, t, i, qt, kt, row, j):
                u = unit_of[kind, t, i]
                if u >= 2:
                    pe.wait_ge(sem(units[u - 2][0]), units[u - 2][1])
                w = (t + 1) * P
                b = 2 * (u % 2)
                for c0 in range(0, w, HALF):
                    cn = min(HALF, w - c0)
                    last = mm(ps[:, b + c0 // HALF, 0:cn], qt[row:row + HD, j, t * P:(t + 1) * P],
                              kt[row:row + HD, c0:c0 + cn], start=True, stop=True)
                last.then_inc(sem("score_full"), 1)

            pe.wait_ge(sem("glu_ready"), 2 * NCC)
            for kind, t, i in MICRO:
                if kind == "index":
                    score_mm(kind, t, i, qiT, kiT, HD * (i % 2), i // 2)
                if kind == "scores":
                    score_mm(kind, t, i, qT, kT, HD * (HEADS[i] // 4), HEADS[i] % 4)
                if kind == "turn":
                    n = NH * t + i
                    pe.wait_ge(sem("exp_done"), n + 1)
                    for g in range(t // 4 + 1):
                        u = tp_of[t, i, g]
                        if u >= 2:
                            pe.wait_ge(sem(tp_free[u - 2][0]), tp_free[u - 2][1])
                        for bb in range(4 * g, min(4 * g + 4, t + 1)):
                            last = nc.tensor.transpose(ps[:, 4 + u % 2, (bb % 4) * P:(bb % 4 + 1) * P],
                                                       prob[:, n % 2, bb * P:(bb + 1) * P], ident)
                        last.then_inc(sem("tp_full"), 1)
                if kind == "values":
                    n = NH * t + i
                    pe.wait_ge(sem("tp_out"), tp_outs[n])
                    if i == 0 and t:
                        pe.wait_ge(sem("o_ready"), t)
                    h, kv = HEADS[i], HEADS[i] // 4
                    for bb in range(t + 1):
                        last = mm(ps[:, 6, h * HD:(h + 1) * HD], probT[:, n % 2, bb, :],
                                  vtok[:, bb, kv * HD:(kv + 1) * HD], start=(bb == 0), stop=(bb == t))
                    last.then_inc(sem("pv_done"), 1)
                if kind == "out":
                    u = tp_of[t, "o"]
                    pe.wait_ge(sem("o_ready"), t + 1)
                    pe.wait_ge(sem(tp_free[u - 2][0]), tp_free[u - 2][1])
                    for c in range(4):
                        last = nc.tensor.transpose(ps[:, 4 + u % 2, c * P:(c + 1) * P],
                                                   otok[:, c * P:(c + 1) * P], ident)
                    last.then_inc(sem("tp_full"), 1)
                if kind == "conv":
                    for k in range(t, i):
                        unit, tap = k // CONV_K, k % CONV_K
                        c, half = unit // 2, unit % 2
                        if tap == 0 and unit:
                            pe.wait_ge(sem("conv_out"), unit)
                        pe.wait_ge(sem("diag_ready"), k + 1)
                        lo = tap if half == 0 else 0
                        mm(ps[:, 7, lo:HALF], diag[:, k % 8, :],
                           glu[:, c, half * HALF + lo - tap:(half + 1) * HALF - tap], start=(tap == 0),
                           stop=(tap == CONV_K - 1)).then_inc(sem("tap_used"), 1)
                if kind == "ada":
                    u = tp_of["ada", t]
                    if u >= 2:
                        pe.wait_ge(sem(tp_free[u - 2][0]), tp_free[u - 2][1])
                    for j in range(t, i):
                        ada(2 * NK + 20 + j, j, ps[:, 4 + u % 2, j - t:j - t + 1])
                if kind == "ln_mean":
                    if t == 0:
                        pe.wait_ge(sem("conv_out"), 2 * NCC)
                    else:
                        pe.wait_ge(sem("ln_sd"), t)
                    for c in range(NCC):
                        last = mm(ps[:, 7, :], ones, conv[:, c, t * HALF:(t + 1) * HALF], start=(c == 0),
                                  stop=(c == NCC - 1))
                    last.then_inc(sem("ln_mean"), 1)
                if kind == "ln_square":
                    pe.wait_ge(sem("ln_cent"), NCC * (t + 1))
                    for c in range(NCC):
                        pe.wait_ge(sem("ln_sq"), NCC * t + c + 1)
                        mm(ps[:, 7, :], ones, tmp2[:, 0, :], start=(c == 0),
                           stop=(c == NCC - 1)).then_inc(sem("ln_summed"), 1)
            pe.wait_ge(sem("gdiag_ready"), NK)
            for g in range(2):
                if g:
                    pe.wait_ge(sem("gdiag_ready"), 2 * NK)
                for j in range(2):
                    mm(ps[:, 2 * g + j, :], ones, gdiag[:, 4 * j:4 * j + 4, :].rearrange("p a b -> p (a b)"),
                       start=True, stop=True).then_inc(sem("gate_mm"), 1)
            pe.wait_ge(sem("gate_out"), 4)
            pe.wait_ge(sem("conv_lo"), 2 * NCC)
            for j in range(2):
                for kk in range(4):
                    m = 20 + 4 * j + kk
                    pe.wait_ge(sem("split_done"), m + 1)
                    for t in range(NT):
                        if kk == 0 and j:
                            pe.wait_ge(sem("gated"), t + 1)
                        last = tm(m, t, 2 * kk, HALF, h_hi, h_lo, kk == 0, kk == 3)
                        if kk == 3:
                            last.then_inc(sem("wo_full"), 1)
                        elif t == NT - 1:
                            last.then_inc(sem("wo_part"), 1)
            norm(1)

            def mlp(k, m0):
                pe.sem_inc(sem(f"down_full{k}"), 16)
                pe.sem_inc(sem(f"down_part{k}"), 2)
                with pe.Fori(0, GROUPS) as g:
                    for s in range(4):
                        pe.wait_ge(sem("split_done"), g * 8 + (m0 + s + 1))
                        for half in range(2):
                            b = 2 * s + half
                            pe.wait_ge(sem(f"down_out{k}"), g * 16 + (b + 9))
                            cm(s, half, b, None, f"up_full{k}")
                    for j in range(2):
                        for kk in range(2):
                            s = 4 + 2 * j + kk
                            pe.wait_ge(sem("split_done"), g * 8 + (m0 + s + 1))
                            if j == 0:
                                pe.wait_ge(sem(f"u_lo{k}"), g * 8 + (4 * kk + 4 + 4))
                            for t in range(NT):
                                if kk == 0 and j == 0:
                                    pe.wait_ge(sem(f"up_relu{k}"), g * 8 + (t + 1))
                                if kk == 0 and j == 1:
                                    pe.wait_ge(sem(f"down_out{k}"), g * 16 + (t + 1 + 16))
                                last = tm(s, t, 2 * kk, HALF, u_hi, u_lo, kk == 0, kk == 1)
                                if kk == 1:
                                    last.then_inc(sem(f"down_full{k}"), 1)
                                elif t == NT - 1:
                                    last.then_inc(sem(f"down_part{k}"), 1)

            pe.wait_ge(sem("norm_lo"), 4 * NK)
            mlp(0, W_FIRST)
            norm(2)
            pe.wait_ge(sem("norm_lo"), 6 * NK)
            for i in range(len(CH2) + 1):
                if i < len(CH2):
                    pe.wait_ge(sem("split_done"), M_2 + i + 1)
                    if i >= 3:
                        pe.wait_ge(sem(ch_read[i - 3][0]), ch_read[i - 3][1])
                    for half in range(2):
                        cm(i, half, 2 * (i % 3) + half, None, "cm2_full")
                if i == 0:
                    pe.wait_ge(sem("ab_split"), 1)
                    for t in range(NT):
                        tok, o = slice(t * P, (t + 1) * P), ps[:, 6, t * 2 * GH:(t + 1) * 2 * GH]
                        for k in range(NK):
                            mm(o, h_hi[:, k, tok], ab_hi[:, k, :], start=(k == 0), stop=False)
                            mm(o, h_hi[:, k, tok], ab_lo[:, k, :], start=False, stop=False)
                            last = mm(o, h_lo[:, k, tok], ab_hi[:, k, :], start=False, stop=(k == NK - 1))
                    last.then_inc(sem("ab_full"), 1)
                if i and (i - 1) in aux_read:
                    kind, c = CH2[i - 1]
                    if i == 1:
                        pe.wait_ge(sem("ab_out"), 1)
                    elif (i - 2) in aux_read:
                        pe.wait_ge(sem(aux_read[i - 2][0]), aux_read[i - 2][1])
                    y = yt[:, (i - 1) % 2, :]
                    if kind == "pool":
                        pe.wait_ge(sem("wpool_in"), 16)
                        pe.wait_ge(sem("pooled"), 2 * (c + 1))
                    else:
                        pe.wait_ge(sem("l2_sq"), c + 1)
                    for half in range(2):
                        last = mm(ps[:, 6 + half, :], wpool[:, c, :] if kind == "pool" else ones,
                                  y[:, half * HALF:(half + 1) * HALF], start=True, stop=True)
                    last.then_inc(sem("pool_mm" if kind == "pool" else "l2_mm"), 1)

            pe.wait_ge(sem("masks_ready"), 1)
            pe.wait_ge(sem("gs_dve"), 2)
            pe.wait_ge(sem("z_silu"), GH)
            g32 = gs["g"].rearrange("p t h -> p (t h)")
            mm(ps[:, 6, 0:32], tri, g32, start=True, stop=True).then_inc(sem("gs_mm"), 1)
            mm(ps[:, 6, 32:64], blk, g32, start=True, stop=True).then_inc(sem("gs_mm"), 1)

            for kind, t, l in GSTEPS:
                b = prep[t % 2]
                n0 = 3 * (t % 2)
                x0, x1, x2 = (bank(n0 + i) for i in range(3))
                tok = slice(t * P, (t + 1) * P)

                def heads(out, lhs, rhs, what):
                    for h in range(GH):
                        last = mm(out[:, h, :], lhs[:, h, :], rhs[:, h, :], start=True, stop=True)
                    last.then_inc(prep_sem("mm", t), 1)

                def turns(out, src):
                    for h in range(GH):
                        last = nc.tensor.transpose(out[:, h, :], src[:, h, :], ident)
                    return last

                if kind == "head":
                    if t >= 2:
                        pe.wait_ge(prep_sem("act", t - 2), prep_count("act", t - 2, "kct"))
                    pe.wait_ge(prep_sem("dve", t), prep_count("dve", t, "tg"))
                    mm(ps[:, n0, :], ones, b["z"].rearrange("p h m -> p (h m)"), start=True,
                       stop=True).then_inc(prep_sem("mm", t), 1)
                    heads(x1, kc[:, :, tok], kc[:, :, tok], "gram")
                    heads(x2, kc[:, :, tok], qc[:, :, tok], "kq")
                    pe.wait_ge(prep_sem("pool", t), prep_count("pool", t, "b0"))
                    pe.wait_ge(prep_sem("act", t), prep_count("act", t, "egb"))
                    turns(x0, b["b0"]).then_inc(prep_sem("mm", t), 1)
                if kind == "level":
                    pe.wait_ge(prep_sem("pool", t), prep_count("pool", t, f"b{l}"))
                    pe.wait_ge(prep_sem("dve", t), prep_count("dve", t, f"u{l - 1}"))
                    heads(x0, b[f"b{l % 2}"], b["u"], f"z{l}")
                    pe.wait_ge(prep_sem("act", t), prep_count("act", t, f"z{l}"))
                    if l < 5:
                        pe.wait_ge(prep_sem("pool", t), prep_count("pool", t, "t0"))
                        heads(x1, b["z"], b["t"], f"t{l}")
                    heads(x2, b["t"], b["z"], f"u{l}")
                if kind == "tail":
                    turns(x0, kc[:, :, tok]).then_inc(prep_sem("mm", t), 1)
                    turns(x1, vc[:, :, tok]).then_inc(prep_sem("mm", t), 1)
                    pe.wait_ge(prep_sem("dve", t), prep_count("dve", t, "vb"))
                    heads(x1, b["u"], b["vb"], "val")
                    heads(x2, b["kbe"], b["u"], "kct")
                if kind == "chunk":
                    r = slice(CHUNK * l, CHUNK * (l + 1))
                    if l == 0:
                        pe.wait_ge(prep_sem("act", t), prep_count("act", t, "kct"))
                        pe.wait_ge(prep_sem("pool", t), prep_count("pool", t, "qdec"))
                        if t:
                            pe.wait_ge(sem("scan_dve"), scan_count("dve", t - 1, "gated"))
                            pe.wait_ge(sem("scan_dve"), scan_count("dve", t - 1, "snew1"))
                    else:
                        pe.wait_ge(sem("scan_dve"), scan_count("dve", t, "snew0"))
                    for h in range(GH):
                        mm(bank(6)[r, h, :], b["kct"][:, h, r], state[:, h, :], start=True, stop=True)
                    for h in range(GH):
                        last = mm(bank(7)[r, h, :], b["qdec"][:, h, r], state[:, h, :], start=(h == 0), stop=False,
                                  skip_group_check=True)
                    last.then_inc(sem("scan_mm"), 1)
                    pe.wait_ge(sem("scan_dve"), scan_count("dve", t, f"vnew{l}"))
                    for h in range(GH):
                        last = mm(bank(6)[:, h, :], b["kd"][r, h, :], vnew[r, h, :], start=True, stop=True)
                    last.then_inc(sem("scan_mm"), 1)
                    if l:
                        for h in range(GH):
                            last = mm(bank(7)[:, h, :], b["ait"][:, h, :], vnew[:, h, :], start=False, stop=(h == GH - 1),
                                      skip_group_check=True)
                        last.then_inc(sem("scan_mm"), 1)
                if kind == "finish":
                    pe.wait_ge(sem("scan_dve"), scan_count("dve", t, "on"))
                    turns(bank(7), ot).then_inc(sem("scan_mm"), 1)

            for j in range(2):
                for kk in range(4):
                    pe.wait_ge(sem("split_done"), M_2 + len(CH2) + 4 * j + kk + 1)
                    if j == 0:
                        pe.wait_ge(sem("mix2_lo"), 4 * (kk + 1))
                    for t in range(NT):
                        if kk == 0 and j == 0 and t >= 6:
                            pe.wait_ge(sem("scan_dve"), scan_count("dve", NT - 1, "gated"))
                        if kk == 0 and j:
                            pe.wait_ge(sem("x_mixed2"), t + 1)
                        last = tm(kk, t, 2 * kk, HALF, h_hi, h_lo, kk == 0, kk == 3)
                        if kk == 3:
                            last.then_inc(sem("wo2_full"), 1)
                        elif t == NT - 1:
                            last.then_inc(sem("wo2_part"), 1)
            norm(3)
            pe.wait_ge(sem("norm_lo"), 8 * NK)
            mlp(1, M_MLP1)


_INS = ["x", "c", "positions", "w_ada", "b_ada", "g_mix", "w_in", "conv_w", "conv_b", "conv_norm_g",
        "conv_norm_b", "w_out", "g_mlp", "w_up", "w_down", "g_final", "norm_mix_2", "w_in_2", "conv_w_2",
        "w_pool_2", "pool_scale_2", "a_log_2", "dt_bias_2", "gdn_norm_2", "w_out_2", "norm_mlp_2", "w_up_2",
        "w_down_2", "norm_final_2"]


def kernel(**inputs):
    import concourse.bacc as bacc
    from concourse.bass_utils import run_bass_kernel_spmd

    nc = bacc.Bacc("TRN2", target_bir_lowering=False, num_devices=1)
    arrays, aps = {}, {}
    for name in _INS:
        v = np.ascontiguousarray(inputs[name])
        arrays[f"in_{name}_dram"] = v
        aps[name] = nc.dram_tensor(f"in_{name}_dram", v.shape, mybir.dt.from_np(v.dtype), kind="ExternalInput").ap()
    out = nc.dram_tensor("out_0_dram", (1, S, D), F32, kind="ExternalOutput").ap()
    build(nc, aps, out)
    r = run_bass_kernel_spmd(nc, [arrays], core_ids=[0])
    return r.results[0]["out_0_dram"]
```

```python
from contextlib import ExitStack

import numpy as np
import concourse.bass as bass
from concourse import mybir

ALU = mybir.AluOpType
ACT = mybir.ActivationFunctionType
AX = mybir.AxisListType
F32 = mybir.dt.float32
F32R = mybir.dt.float32r
I32 = mybir.dt.int32

P = 128
S = 1024
D = 1024
NT = S // P
NK = D // P
HALF = 512
DFF = 4 * D
EPS = 1e-6

NH, NKV, HD = 8, 2, 64
TOPK = 256
CONV_CH, CONV_K = 512, 31
NCC = CONV_CH // P
ROT = HD // 4
HROT = ROT // 2
COL_Q, COL_K, COL_V = 0, NH * HD, NH * HD + NKV * HD
COL_QI = COL_V + NKV * HD
COL_KI = COL_QI + NH * HD
COL_WI = COL_KI + HD
COL_CU = COL_WI + NH
TM_COLS = [(0, HALF), (HALF, HALF), (2 * HALF, COL_CU - 2 * HALF)]
MASKED = -3.0e38
TAKEN = -3.4e38
ROUNDS = TOPK // 8
PAD = 2
DT = 3
IDX_TILES = [t for t in range(NT) if (t + 1) * P > TOPK]

PW, GW = D // 2, D // 2
GH, GD, CHUNK = 4, 128, 64
WINDOWS = (2, 4, 8, 16)
TAPS = 4
ABC = PW + 4 * GW

VEC = {}
_n = 0
for _name, _rows in (("c", NK), ("b_ada", 6 * NK), ("g_mix", NK), ("g_mlp", NK), ("conv_b", NCC),
                     ("conv_norm_g", NCC), ("conv_norm_b", NCC), ("norm_mix_2", NK),
                     ("norm_mlp_2", NK), ("pool_scale_2", GH), ("gdn_norm_2", 1)):
    VEC[_name] = (_n, _n + _rows)
    _n += _rows
NVEC = _n

def build(nc, a, out):
    with ExitStack() as ctx:
        sems = {}

        def sem(name):
            if name not in sems:
                sems[name] = ctx.enter_context(nc.semaphore(name))
            return sems[name]

        BASE = 16512
        AX_, ARAW, AWHI, AWLO, AH, AU, AC = (BASE + 1024 * n for n in (0, 32, 48, 64, 80, 144, 176))

        def at(name, shape, dt, offset):
            return nc.alloc_sbuf_tensor_at(name, shape, dt, offset=offset).ap()

        K1 = 1024
        x = at("x", [P, NT, D], F32, AX_)
        raw = at("raw", [P, 4, 1024], F32, ARAW)
        w_hi = at("w_hi", [P, 4, 1024], F32R, AWHI)
        w_lo = at("w_lo", [P, 4, 1024], F32R, AWLO)
        h_hi = at("h_hi", [P, NK, S], F32R, AH)
        h_lo = at("h_lo", [P, NK, S], F32R, AH + 32 * K1)
        xn = at("xn", [P, NT, D], F32, AU)
        u_hi = at("u_hi", [P, 4, S], F32R, AU)
        u_lo = at("u_lo", [P, 4, S], F32R, AU + 16 * K1)
        qT = at("qT", [P, 4, S], F32, AX_)
        qiT = at("qiT", [P, 4, S], F32, AX_ + 16 * K1)
        ropet = at("ropet", [P, 4, HALF], F32, AX_ + 16 * K1)
        pr0 = at("pr0", [P, NT, 512], F32, AU)
        pr1 = at("pr1", [P, NT, 384], F32, AU + 16 * K1)
        vtok = at("vtok", [P, NT, P], F32, AU + 28 * K1)
        glu = at("glu", [P, NCC, PAD + S], F32, AU - 32)
        squares = at("squares", [P, NCC, HALF], F32, AWHI)
        gates = at("gates", [P, NCC, HALF], F32, AU)
        glu_hi = at("glu_hi", [P, NCC, PAD + S], F32R, AH + 16 * K1 - 32)
        glu_lo = at("glu_lo", [P, NCC, PAD + S], F32R, AU - 32)
        idx0 = at("idx0", [P, S], F32, AU + 16 * K1)
        q_hi = at("q_hi", [P, 4, S], F32R, AX_ + 16 * K1)
        q_lo = at("q_lo", [P, 4, S], F32R, AX_)
        qi_lo = at("qi_lo", [P, 4, S], F32R, AX_ + 16 * K1)
        otok = at("otok", [P, 512], F32, AU + 20 * K1)
        diag_hi = at("diag_hi", [P, 2, DT, P], F32R, AU + 22 * K1)
        diag_lo = at("diag_lo", [P, 2, DT, P], F32R, AU + 25 * K1)
        relu_all = at("relu", [P, 2, S], F32, AWHI)
        relu_early = at("relu_early", [P, 2, 3 * P], F32, AU + 22 * K1)
        prob = at("prob", [P, 2, S], F32, AWHI + 8 * K1)
        probT = at("probT", [P, 2, NT, P], F32, AWLO)
        qi_hi_all = at("qi_hi", [P, 2, NT, P], F32R, AWLO)[:, :, 6:8, :]
        qi_hi_early = at("qi_hi_early", [P, 2, 2, P], F32R, AU + 20 * K1)
        score01 = at("score01", [P, 2, S], F32, AWLO + 8 * K1)
        conv = at("conv", [P, NCC, S], F32, AH + 48 * K1)
        off = [AC]

        def small(name, shape, dt=F32):
            n = int(np.prod(shape[1:])) * 4
            t = at(name, shape, dt, off[0])
            off[0] += (n + 31) // 32 * 32
            return t

        ident = small("ident", [P, P])
        ones = small("ones", [P, P])
        vec = small("vec", [P, P])
        cw = small("cw", [P, P])
        cw2 = small("cw2", [P, TAPS * 12])
        mod = small("mod", [P, 6 * NK])
        csil = small("csil", [P, NK])
        eps = small("eps", [P, 1])
        zero = small("zero", [P, 1])
        scl = small("scl", [P, 2, NK])
        pos = small("pos", [P, NT])
        freq = small("freq", [P, HROT])
        cosv = small("cosv", [P, NT, HROT])
        sinv = small("sinv", [P, NT, HROT])
        ss = small("ss", [P, NT])
        sd = small("sd", [P, NT])
        rs = small("rs", [P, NT])
        wi = small("wi", [P, NT, NH])
        best = small("best", [P, 8])
        smax = small("smax", [P, NH])
        snm = small("snm", [P, NH])
        ssum = small("ssum", [P, 2, NH])
        srec = small("srec", [P, NH])
        invc = small("invc", [P, 16])
        dtb = small("dtb", [P, GH])
        alog = small("alog", [P, GH])
        abraw = small("abraw", [P, NK, 2 * GH])
        ab_hi = small("ab_hi", [P, NK, 2 * GH], F32R)
        ab_lo = small("ab_lo", [P, NK, 2 * GH], F32R)
        ab = small("ab", [P, NT, 2 * GH])
        cw_hi = at("cw_hi", [P, CONV_K * NCC], F32R, off[0])
        cw_lo = at("cw_lo", [P, CONV_K * NCC], F32R, off[0] + 512)
        gs = {nm: small(f"g_{nm}", [P, NT, GH]) for nm in ("t1", "t2", "g", "beta", "gcum", "egc", "edec", "bege")}
        osum = small("osum", [P, GH])
        orec = small("orec", [P, GH])
        eps2 = small("eps2", [P, 1])
        AD = off[0]
        pr2 = at("pr2", [P, NT, 392], F32, AD)
        tmp2 = at("tmp2", [P, 2, HALF], F32, AD)
        act_r = at("act_r", [P, 4, HALF], F32, AD + 4 * K1)
        score = [score01[:, 0, :], score01[:, 1, :], at("score2", [P, S], F32, AD + 4 * K1)]
        junk = at("junk", [P, 2, D], F32, AD + 4 * K1)
        rowsv = at("rowsv", [P, 3, P], F32, AD)
        rowsi = at("rowsi", [NT, P], I32, AD + 2 * K1)
        rowsp = at("rowsp", [NT, P], F32, AD + 3 * K1)
        angt = at("angt", [P, 4, NT, HROT], F32, AD + 4 * K1)
        AE = AD + 12 * K1 + 256
        kT = at("kT", [P, S], F32, AE)
        kiT = at("kiT", [P, S], F32, AE + 4 * K1)
        k_lo = at("k_lo", [P, S], F32R, AE)
        ki_lo = at("ki_lo", [P, S], F32R, AE + 4 * K1)
        k_hi = at("k_hi", [P, S], F32R, AE + 8 * K1)
        ki_hi = at("ki_hi", [P, S], F32R, AD + 8 * K1)
        gate1 = at("gate1", [P, D], F32, AE + 8 * K1)
        gate2 = at("gate2", [P, D], F32, AE)
        frow = at("frow", [P, D], F32, AE + 4 * K1)
        gdiag = at("gdiag", [P, NK, P], F32, AU)

        qc = at("qc", [P, GH, S], F32, AX_)
        kc = at("kc", [P, GH, S], F32, AX_ + 16 * K1)
        vc = at("vc", [P, GH, S], F32, AU)
        zc = at("zc", [P, GH, S], F32, AU + 16 * K1)
        abT = zc[0:2 * GH, GH - 1, :]
        pm = at("pm", [P, GH, S], F32, AD)
        yt = at("yt", [P, 2, S], F32, AD + 16 * K1)
        wpool = at("wpool", [P, GH, P], F32, AD + 24 * K1)
        masks = at("masks", [P, 8, P], F32, AD + 16 * K1)
        tri, strict, blk = masks[:, 0, :], masks[:, 1, :], cw
        level = [masks[:, 2 + i, :] for i in range(6)]
        state = at("state", [P, GH, P], F32, AD + 16 * K1 + 4096)
        vnew = at("vnew", [P, GH, P], F32, AD + 16 * K1 + 6144)
        ot = at("ot", [P, GH, P], F32, AD + 16 * K1 + 8192)
        prep = []
        for i in range(2):
            names = ["e1", "e2", "egb", "m", "b0", "b1", "z", "t", "u", "kbe", "vb", "ait", "kd", "val", "kct", "qdec"]
            prep.append({nm: at(f"{nm}_{i}", [P, GH, P], F32, AH + i * 32 * K1 + j * 2 * K1)
                         for j, nm in enumerate(names)})

        ps = nc.alloc_psum_tensor("ps", [P, 8, HALF], F32).ap()

        def v3(ap, n):
            return ap.rearrange("p (n m) -> p n m", n=n)

        def vcol(name, i=0):
            return vec[:, VEC[name][0] + i:VEC[name][0] + i + 1]

        def vcols(name):
            return vec[:, VEC[name][0]:VEC[name][1]]

        def kp(name):
            return a[name].rearrange("l (k p) n -> (l p) k n", p=P) if len(a[name].shape) == 3 else a[name]

        w_ada, w_in, w_out = kp("w_ada"), kp("w_in"), kp("w_out")
        slots = []
        for j in range(2 * NK):
            slots.append(("ada", w_ada[:, :, j * P:(j + 1) * P], (NK, P)))
        for c0, cn in TM_COLS:
            for kk in range(4):
                slots.append(("w", w_in[:, 2 * kk:2 * kk + 2, c0:c0 + cn], (2, cn)))
        for c in range(NCC):
            for part in range(2):
                c0 = COL_CU + part * CONV_CH + c * P
                slots.append(("w", w_in[:, :, c0:c0 + P], (NK, P)))
        for j in range(2 * NK, 6 * NK):
            slots.append(("ada", w_ada[:, :, j * P:(j + 1) * P], (NK, P)))
        for j in range(2):
            for kk in range(4):
                slots.append(("w", w_out[:, 2 * kk:2 * kk + 2, j * HALF:(j + 1) * HALF], (2, HALF)))
        N_FIRST = len(slots)
        assert N_FIRST % 4 == 0
        nw = nada = 0
        freed = []
        for kind, _, _ in slots:
            if kind == "w":
                nw += 1
                freed.append(("split_done", nw))
            else:
                nada += 1
                freed.append(("ada_done", nada))
        W_FIRST = nw
        used = []
        for j in range(len(TM_COLS)):
            used += [("tm_part", 3 * j + kk + 1) for kk in range(3)] + [("tm_full", NT * (j + 1))]
        used += [("cm_full", 2 * i + 2) for i in range(2 * NCC)]
        for j in range(2):
            used += [("wo_part", 3 * j + kk + 1) for kk in range(3)] + [("wo_full", NT * (j + 1))]
        assert len(used) == W_FIRST
        raw_in = [sem(f"raw_in{r}") for r in range(4)]
        w_in_2, w_out_2 = kp("w_in_2"), kp("w_out_2")
        CH2 = [("pool", i) for i in range(GH)] + [("qkv", i) for i in range(3 * GH)] + [("z", i) for i in range(GH)]
        slots2 = [("w", w_in_2[:, :, i * P:(i + 1) * P], (NK, P)) for i in range(len(CH2))]
        for j in range(2):
            for kk in range(4):
                slots2.append(("w", w_out_2[:, 2 * kk:2 * kk + 2, j * HALF:(j + 1) * HALF], (2, HALF)))
        GROUPS = DFF // 512
        N_MLP0, M_MLP0 = N_FIRST, W_FIRST
        N_2, M_2 = N_MLP0 + 8 * GROUPS, M_MLP0 + 8 * GROUPS
        N_MLP1, M_MLP1 = N_2 + len(slots2), M_2 + len(slots2)
        assert len(slots2) % 4 == 0 and M_2 % 4 == 0
        used2 = [("cm2_full", 2 * i + 2) for i in range(len(CH2))]
        for j in range(2):
            used2 += [("wo2_part", 3 * j + kk + 1) for kk in range(3)] + [("wo2_full", NT * (j + 1))]

        ch_read, ch_free = [], []
        for kind, c in CH2:
            ch_read.append({"pool": ("pool_u", c + 1), "qkv": ("taps", 3 * (c + 1)), "z": ("z_silu", c + 1)}[kind])
            ch_free.append({"pool": ("pm_out", c + 1), "qkv": ("l2_done", c + 1) if c < 2 * GH else ("conv_silu", c + 1),
                            "z": None}[kind])
        aux_read = {i: (("pm_out", c + 1) if kind == "pool" else ("l2_sd", c + 1))
                    for i, (kind, c) in enumerate(CH2) if kind == "pool" or (kind == "qkv" and c < 2 * GH)}

        G_ORDER = [("finish_a", 8, 0), ("chunk_a", 7, 0), ("head_a", 0, 0)]
        G_ORDER += [("level_z", l, l) for l in range(1, 6)] + [("tail_a", 6, 0)]
        G_ORDER += [("chunk_b", 7, 0), ("finish_b", 8, 0)]
        G_ORDER += [("level_tu", l, l) for l in range(1, 6)]
        G_ORDER += [("chunk_a", 7, 1), ("finish_c", 8, 0), ("tail_b", 6, 0), ("head_b", 0, 0), ("chunk_b", 7, 1)]
        GSTEPS = []
        for slot in range(4 * NT + 10):
            for kind, j, l in G_ORDER:
                for t in range(NT):
                    if slot - 4 * t == j:
                        GSTEPS.append((kind, t, l))
        PREP = {
            "mm": ["gb", "gram", "kq", "turn"] + [x for l in range(1, 6) for x in ((f"z{l}", f"t{l}", f"u{l}") if l < 5 else ("z5", "u5"))]
                  + ["ktp", "vtp", "val", "kct"],
            "dve": ["tg", "df", "e12", "m", "ait", "u0"] + [x for l in range(1, 6) for x in ((f"t{l}", f"u{l}") if l < 5 else ("u5",))]
                   + ["kbe", "kd", "vb"],
            "act": ["egb", "e1", "e2"] + [f"z{l}" for l in range(1, 6)] + ["val", "kct"],
            "pool": ["e1m", "e2m", "qdec", "b0", "t0", "b1", "b2", "b3", "b4", "b5"],
        }
        SCAN = {
            "mm": ["kq0", "kdv0", "kq1", "kdv1", "ai", "otp"],
            "dve": ["vnew0", "sdec0", "snew0", "vnew1", "sdec1", "snew1", "sq", "sum", "rec", "on", "gated"],
            "act": ["ot", "sd"],
        }

        def prep_sem(kind, t):
            return sem(f"prep_{kind}{t % 2}")

        def prep_count(kind, t, what):
            return (t // 2) * len(PREP[kind]) + PREP[kind].index(what) + 1

        def scan_count(kind, t, what):
            return t * len(SCAN[kind]) + SCAN[kind].index(what) + 1

        def hb(mask):
            return mask.unsqueeze(1).to_broadcast([P, GH, P])

        def tb(col):
            return col.unsqueeze(2).to_broadcast([P, GH, P])

        def bank(b):
            return v3(ps[:, b, :], GH)


        def relu_of(t):
            return relu_early if t == IDX_TILES[0] else relu_all

        def qi_hi_of(t):
            return qi_hi_early if t == IDX_TILES[0] else qi_hi_all

        IDX0 = IDX_TILES[0]
        EARLY = [("index", IDX0, h) for h in range(NH)]
        EARLY_PARTS = [[], [], range(0, 4), range(4, 8)]
        INDEX_SLOTS = {3: range(0, 8), 4: range(8, 16), 5: range(24, 32), 6: range(32, 40), 7: range(40, 48)}
        TOPK_SLOTS = {2: range(0, 8), 3: range(8, 19), 4: range(19, 32), 5: range(32, 40), 6: range(40, 48),
                      7: range(48, 56)}
        TOPK_PARTS = {t: len(r) + (8 if t == IDX0 else 0) for t, r in TOPK_SLOTS.items()}
        TAPS_PER_SLOT = [5, 4, 5, 5, 6, 6, 0, 0]
        assert NH * sum(TAPS_PER_SLOT) == 2 * NCC * CONV_K
        LN_STEPS = ("ln_mean", "ln_square", "ln_sum", "ln_scale", "ln_gate", "ln_silu", "ln_hi", "ln_lo")
        LN_SLOTS = {half: {48 + 4 * half + k: kind for k, kind in enumerate(LN_STEPS)} for half in range(2)}
        MICRO = [("split_q", 0, 0), ("split_q", 1, 0), ("split_qi", IDX0 + 1, 0)]
        tap = 0
        for t in range(NT):
            for i in range(NH):
                n = NH * t + i
                MICRO.append(("scores", t, i))
                for ti, at_slots in INDEX_SLOTS.items():
                    if n in at_slots:
                        per = NH // len(at_slots)
                        h0 = per * (n - at_slots[0])
                        MICRO += [("index", ti, h) for h in range(h0, h0 + per)]
                        if n == at_slots[-1] and ti < NT - 1:
                            MICRO.append(("split_qi", ti + 1, 0))
                if 1 <= t < NT - 1 and i == 4:
                    MICRO.append(("split_q", t + 1, 0))
                last = (t, i - 1) if i else (t - 1, NH - 1)
                if n:
                    MICRO.append(("turn",) + last)
                if n < 4 * NK:
                    MICRO.append(("ada", n, n + 1))
                if TAPS_PER_SLOT[t]:
                    MICRO.append(("conv", tap, tap + TAPS_PER_SLOT[t]))
                    tap += TAPS_PER_SLOT[t]
                MICRO.append(("exp", t, i))
                for half in range(2):
                    if n in LN_SLOTS[half]:
                        MICRO.append((LN_SLOTS[half][n], half, 0))
                if n:
                    MICRO.append(("values",) + last)
                for ti, at_slots in TOPK_SLOTS.items():
                    if n in at_slots:
                        MICRO.append(("topk", ti, n - at_slots[0] + (8 if ti == IDX0 else 0)))
                if n < 4 * NK:
                    MICRO.append(("ada_out", n, n + 1))
                if n and i == 0:
                    MICRO.append(("divide", t - 1, 0))
                if t and i == 1:
                    MICRO.append(("out", t - 1, 0))
        MICRO += [("turn", NT - 1, NH - 1), ("values", NT - 1, NH - 1), ("divide", NT - 1, 0), ("out", NT - 1, 0)]
        DIAGS = [(u, tap, min(DT, CONV_K - tap)) for u in range(2 * NCC) for tap in range(0, CONV_K, DT)]
        diag_end = [CONV_K * u + tap + n for u, tap, n in DIAGS]
        unit_of, units = {}, []
        for kind, t, i in EARLY + MICRO:
            if kind == "index":
                unit_of[kind, t, i] = len(units)
                units.append(("relu_done", NH * (t - IDX_TILES[0]) + i + 1))
            if kind == "scores":
                unit_of[kind, t, i] = len(units)
                units.append(("masked", NH * t + i + 1))
        tp_of, tp_free = {}, []
        tp_count = []
        tp_last, tp_outs = [], []
        n_full = n_out = n_ada = 0
        for kind, t, i in MICRO:
            if kind == "turn":
                for g in range(t // 4 + 1):
                    tp_of[t, i, g] = len(tp_free)
                    n_out += 1
                    n_full += 1
                    tp_free.append(("tp_out", n_out))
                    tp_count.append(n_full)
                tp_last.append(n_full)
                tp_outs.append(n_out)
            if kind == "out":
                tp_of[t, "o"] = len(tp_free)
                n_full += 1
                tp_free.append(("attn_lo", t + 1))
                tp_count.append(n_full)
            if kind == "ada":
                tp_of["ada", t] = len(tp_free)
                n_ada += 1
                tp_free.append(("mod_out", n_ada))
                tp_count.append(n_full)
        HEADS = [j + 4 * half for j in range(4) for half in range(2)]

        x_mid = nc.dram_tensor("x_mid", [NT, P, D], F32, kind="Internal").ap()

        block = ctx.enter_context(nc.Block())

        @block.sync
        def _(sp):
            n = 0
            for kind, src, (n1, n2) in slots:
                if n >= 4:
                    sp.wait_ge(sem(freed[n - 4][0]), freed[n - 4][1])
                dst = raw[:, n % 4, 0:n1 * n2].rearrange("p (k n) -> p k n", k=n1)
                sp.dma_start(dst, src).then_inc(raw_in[n % 4], 16)
                n += 1

            def mlp(k, n0, freed0, up, down):
                with sp.Fori(0, GROUPS) as g:
                    for s in range(8):
                        sp.wait_ge(sem("split_done"), g * 8 + (freed0 + s - 3))
                        if s < 4:
                            dst = v3(raw[:, s, :], NK)
                            src = up[:, :, bass.ds(g * 512 + s * P, P)]
                        else:
                            j, kk = (s - 4) // 2, s % 2
                            dst = v3(raw[:, s - 4, :], 2)
                            src = down[:, :, bass.ds(g * 4 + 2 * kk, 2), j * HALF:(j + 1) * HALF].rearrange("l p k n -> (l p) k n")
                        sp.dma_start(dst, src).then_inc(raw_in[s % 4], 16)

            w_down = a["w_down"].rearrange("l (k p) n -> l p k n", p=P)
            mlp(0, N_FIRST, W_FIRST, kp("w_up"), w_down)
            for i, (_, src, (n1, n2)) in enumerate(slots2):
                sp.wait_ge(sem("split_done"), M_2 + i - 3)
                sp.dma_start(raw[:, i % 4, :].rearrange("p (k n) -> p k n", k=n1), src).then_inc(raw_in[i % 4], 16)
                if i == 3:
                    for t in range(NT):
                        sp.wait_ge(sem("x_final"), t + 1)
                        sp.dma_start(x_mid[t], x[:, t, :]).then_inc(sem("x_out"), 16)
            mlp(1, N_MLP1, M_MLP1, kp("w_up_2"), a["w_down_2"].rearrange("l (k p) n -> l p k n", p=P))
            for t in range(NT):
                sp.wait_ge(sem("y_final"), t + 1)
                sp.dma_start(out[0, t * P:(t + 1) * P, :], x[:, t, :]).then_inc(sem("out_done"), 16)
            sp.wait_ge(sem("out_done"), 16 * NT)

        @block.gpsimd
        def _(pool):
            g = nc.gpsimd
            g.memset(ident, 0.0).then_inc(sem("pool_mem"), 1)
            g.memset(eps, EPS).then_inc(sem("pool_mem"), 1)
            g.memset(zero, 0.0).then_inc(sem("pool_mem"), 1)
            for i in range(HROT):
                f = float(np.float32(500000.0 ** (-2.0 * i / ROT)))
                g.memset(freq[:, i:i + 1], f).then_inc(sem("pool_mem"), 1)
            g.memset(eps2, GD * EPS).then_inc(sem("pool_mem2"), 1)
            for i in range(16):
                g.memset(invc[:, i:i + 1], 1.0 / (i + 1)).then_inc(sem("pool_mem2"), 1)
            pool.wait_ge(sem("pool_mem"), 1)
            g.affine_select(out=ident, in_=ident, compare_op=ALU.not_equal, fill=1.0, base=0,
                            pattern=[[-1, P]], channel_multiplier=1).then_inc(sem("ident_ready"), 1)
            g.memset(ones, 1.0).then_inc(sem("ident_ready"), 1)

            def split(m, n, cols):
                r = m % 4
                pool.wait_ge(raw_in[n % 4], 16 * (n // 4 + 1))
                if m >= 4:
                    pool.wait_ge(sem(used[m - 4][0]), used[m - 4][1])
                g.tensor_copy(w_hi[:, r, 0:cols], raw[:, n % 4, 0:cols]).then_inc(sem("w_hi_done"), 1)
                pool.wait_ge(sem("w_hi_done"), m + 1)
                g.tensor_tensor(w_lo[:, r, 0:cols], raw[:, n % 4, 0:cols],
                                w_hi[:, r, 0:cols].bitcast(F32), ALU.subtract).then_inc(sem("split_done"), 1)

            def split_qi(t):
                done = t - IDX0
                if done:
                    pool.wait_ge(sem("score_full"), unit_of["index", t - 1, NH - 1] + 1)
                tok = slice(t * P, (t + 1) * P)
                x4, lo4 = (x[:, :, tok].rearrange("p (a b) q -> p a b q", a=2) for x in (qiT, qi_lo))
                g.tensor_tensor(qi_hi_of(t), x4, zero.unsqueeze(2).unsqueeze(3).to_broadcast([P, 2, 2, P]),
                                ALU.add).then_inc(sem("qi_hi"), 1)
                pool.wait_ge(sem("qi_hi"), done + 1)
                g.tensor_tensor(lo4, x4, qi_hi_of(t).bitcast(F32), ALU.subtract).then_inc(sem("qi_split"), 1)

            m = 0
            for n, (kind, _, (n1, n2)) in enumerate(slots):
                if kind != "w":
                    continue
                if m == 12 + NCC:
                    pool.wait_ge(sem("pr_turned"), 20)
                    g.memset(idx0, 0.0).then_inc(sem("cw_step"), 1)
                    pool.wait_ge(sem("cw_step"), 1)
                    g.affine_select(out=idx0[:, S - P:S], in_=idx0[:, S - P:S], compare_op=ALU.is_ge,
                                    fill=MASKED, base=0, pattern=[[-1, P]],
                                    channel_multiplier=1).then_inc(sem("idx_ready"), 1)
                    split_qi(IDX0)
                if m == 20:
                    pool.wait_ge(sem("cw_ready"), CONV_K)
                    g.tensor_copy(cw_hi, cw[:, 0:CONV_K * NCC]).then_inc(sem("cw_step"), 1)
                    pool.wait_ge(sem("cw_step"), 2)
                    g.tensor_tensor(cw_lo, cw[:, 0:CONV_K * NCC], cw_hi.bitcast(F32),
                                    ALU.subtract).then_inc(sem("cw_step"), 1)
                    pool.wait_ge(sem("cw_step"), 3)
                    pool.wait_ge(sem("cm_full"), 4 * NCC)
                    pool.wait_ge(sem("acc_done"), NH)
                    for kind, t, i in MICRO:
                        tok = slice(t * P, (t + 1) * P)
                        if kind == "split_q":
                            if t >= IDX_TILES[0]:
                                pool.wait_ge(sem("score_full"), unit_of["index", t, NH - 1] + 1)
                            g.tensor_tensor(q_hi[:, :, tok], qT[:, :, tok], zero.unsqueeze(2).to_broadcast([P, 4, P]),
                                            ALU.add).then_inc(sem("q_hi"), 1)
                            pool.wait_ge(sem("q_hi"), t + 1)
                            g.tensor_tensor(q_lo[:, :, tok], qT[:, :, tok], q_hi[:, :, tok].bitcast(F32),
                                            ALU.subtract).then_inc(sem("q_split"), 1)
                        if kind == "split_qi":
                            split_qi(t)
                        if kind == "conv":
                            for d, (unit, tap, taps) in enumerate(DIAGS):
                                if t <= CONV_K * unit + tap < i:
                                    if d >= 2:
                                        pool.wait_ge(sem("tap_used"), diag_end[d - 2])
                                    cols = [(w.rearrange("p (i c) -> p c i", c=NCC)[:, unit // 2, tap:tap + taps]
                                             .unsqueeze(2).to_broadcast([P, taps, P])) for w in
                                            (cw_hi.bitcast(F32), cw_lo.bitcast(F32))]
                                    for dst, col in zip((diag_hi, diag_lo), cols):
                                        g.tensor_tensor(dst[:, d % 2, 0:taps, :],
                                                        ident.unsqueeze(1).to_broadcast([P, taps, P]), col,
                                                        ALU.mult).then_inc(sem("diag_ready"), 1)
                    pool.wait_ge(sem("attn_lo"), NT)
                split(m, n, n1 * n2)
                m += 1

            def mlp(k, n0, m0):
                with pool.Fori(0, GROUPS) as g:
                    for s in range(8):
                        r = s % 4
                        pool.wait_ge(raw_in[r], g * 32 + (16 * (n0 // 4) + 16 * (s // 4 + 1)))
                        if s < 4 and s % 2 == 0:
                            pool.wait_ge(sem(f"down_part{k}"), g * 2 + (s // 2 - 2 + 3))
                        if s < 4 and s % 2 == 1:
                            pool.wait_ge(sem(f"down_full{k}"), g * 16 + (8 * (s // 2) - 16 + 8 + 16))
                        if s >= 4:
                            pool.wait_ge(sem(f"up_full{k}"), g * 8 + (2 * (s - 4) + 2))
                        g_.tensor_tensor(w_hi[:, r, :], raw[:, r, :], zero.to_broadcast([P, 1024]),
                                         ALU.add).then_inc(sem("w_hi_done"), 1)
                        pool.wait_ge(sem("w_hi_done"), g * 8 + (m0 + s + 1))
                        g_.tensor_tensor(w_lo[:, r, :], raw[:, r, :], w_hi[:, r, :].bitcast(F32),
                                         ALU.subtract).then_inc(sem("split_done"), 1)

            g_ = nc.gpsimd
            pool.wait_ge(sem("wo_full"), 2 * NT)
            mlp(0, N_MLP0, M_MLP0)
            pool.wait_ge(sem("ab_in"), 16)
            g.tensor_copy(ab_hi, abraw).then_inc(sem("ab_parts"), 1)
            pool.wait_ge(sem("ab_parts"), 1)
            g.tensor_tensor(ab_lo, abraw, ab_hi.bitcast(F32), ALU.subtract).then_inc(sem("ab_parts"), 1)

            def split2(i):
                r = i % 4
                pool.wait_ge(raw_in[r], 16 * ((N_2 + i) // 4 + 1))
                if i >= 4:
                    pool.wait_ge(sem(used2[i - 4][0]), used2[i - 4][1])
                else:
                    pool.wait_ge(sem("down_full0"), 16 + 16 * GROUPS)
                g.tensor_copy(w_hi[:, r, :], raw[:, r, :]).then_inc(sem("w_hi_done"), 1)
                pool.wait_ge(sem("w_hi_done"), M_2 + i + 1)
                g.tensor_tensor(w_lo[:, r, :], raw[:, r, :], w_hi[:, r, :].bitcast(F32),
                                ALU.subtract).then_inc(sem("split_done"), 1)

            for i in range(len(CH2)):
                split2(i)
            pool.wait_ge(sem("conv_silu"), 3 * GH)
            nm = [0]

            def step(ins):
                nm[0] += 1
                ins.then_inc(sem("mask_step"), 1)
                pool.wait_ge(sem("mask_step"), nm[0])

            def within(dst, b):
                d3 = dst.rearrange("p (n m) -> p n m", m=b)
                step(g.affine_select(out=d3, in_=d3, compare_op=ALU.is_ge, fill=0.0, base=0,
                                     pattern=[[-b, P // b], [0, b]], channel_multiplier=1))
                step(g.affine_select(out=d3, in_=d3, compare_op=ALU.is_ge, fill=0.0, base=b - 1,
                                     pattern=[[b, P // b], [0, b]], channel_multiplier=-1))

            step(g.memset(blk, 1.0))
            within(blk, CHUNK)
            step(g.affine_select(out=tri, in_=blk, compare_op=ALU.is_ge, fill=0.0, base=0,
                                 pattern=[[1, P]], channel_multiplier=-1))
            step(g.memset(strict, 1.0))
            step(g.affine_select(out=strict, in_=strict, compare_op=ALU.is_gt, fill=0.0, base=0,
                                 pattern=[[-1, P]], channel_multiplier=1))
            for i in range(6):
                step(g.tensor_copy(level[i], strict))
                within(level[i], 2 << i)
            step(g.tensor_copy(strict, level[5]))
            for i in range(5, 0, -1):
                step(g.tensor_tensor(level[i], level[i], level[i - 1], ALU.subtract))
            g.memset(state, 0.0).then_inc(sem("masks_ready"), 1)
            for i in range(len(CH2), len(CH2) + 4):
                split2(i)

            for kind, t, l in GSTEPS:
                b = prep[t % 2]
                if kind == "head_a":
                    pool.wait_ge(prep_sem("act", t), prep_count("act", t, "e1"))
                    g.tensor_tensor(b["e1"], b["e1"], hb(strict), ALU.mult).then_inc(prep_sem("pool", t), 1)
                    pool.wait_ge(prep_sem("act", t), prep_count("act", t, "e2"))
                    g.tensor_tensor(b["e2"], b["e2"], hb(tri), ALU.mult).then_inc(prep_sem("pool", t), 1)
                    if t >= 2:
                        pool.wait_ge(sem("scan_mm"), scan_count("mm", t - 2, "kq1"))
                    g.tensor_tensor(b["qdec"], qc[:, :, t * P:(t + 1) * P], b["egb"],
                                    ALU.mult).then_inc(prep_sem("pool", t), 1)
                if kind == "head_b":
                    pool.wait_ge(prep_sem("dve", t), prep_count("dve", t, "m"))
                    g.tensor_tensor(b["b0"], b["m"], hb(level[0]), ALU.mult).then_inc(prep_sem("pool", t), 1)
                    pool.wait_ge(prep_sem("pool", t), prep_count("pool", t, "b0"))
                    g.tensor_tensor(b["t"], hb(ident), b["b0"], ALU.subtract).then_inc(prep_sem("pool", t), 1)
                    g.tensor_tensor(b["b1"], b["m"], hb(level[1]), ALU.mult).then_inc(prep_sem("pool", t), 1)
                if kind == "level_z" and l < 5:
                    if l == 1:
                        pool.wait_ge(prep_sem("mm", t), prep_count("mm", t, "turn"))
                        pool.wait_ge(prep_sem("pool", t), prep_count("pool", t, "t0"))
                    else:
                        pool.wait_ge(prep_sem("mm", t), prep_count("mm", t, f"z{l - 1}"))
                    g.tensor_tensor(b[f"b{(l + 1) % 2}"], b["m"], hb(level[l + 1]), ALU.mult).then_inc(prep_sem("pool", t), 1)

            for i in range(len(CH2) + 4, len(slots2)):
                split2(i)
            pool.wait_ge(sem("wo2_full"), 2 * NT)
            mlp(1, N_MLP1, M_MLP1)

        @block.scalar
        def _(act):
            s = nc.scalar
            vrow = 0
            for name, (r0, r1) in VEC.items():
                src = a[name]
                src = src.rearrange("l (k p) -> (l k) p", p=P)
                act.dma_start(rowsv[r0:r1, 0, :], src).then_inc(sem("rows_in"), 16)
            act.dma_start(rowsv[0:CONV_K * NCC, 1, :],
                          a["conv_w"].rearrange("l k (c p) -> (l k c) p", p=P)).then_inc(sem("rows_in"), 16)
            act.dma_start(rowsv[0:TAPS * 12, 2, :],
                          a["conv_w_2"].rearrange("l k (c p) -> (l k c) p", p=P)).then_inc(sem("rows_in"), 16)
            act.dma_start(rowsi, a["positions"].rearrange("b (t p) -> (b t) p", p=P)).then_inc(sem("rows_in"), 16)
            for t in range(NT):
                act.dma_start(x[:, t, :], a["x"][0, t * P:(t + 1) * P, :]).then_inc(sem(f"x_in{t // 2}"), 16)
            act.wait_ge(sem("vec_ready"), 1)
            s.activation(csil, vcols("c"), ACT.Sigmoid).then_inc(sem("c_sig"), 1)
            act.wait_ge(sem("angle_ready"), 1)
            s.activation(sinv, angt[:, 0], ACT.Sin).then_inc(sem("sines"), 1)
            s.activation(angt[:, 1], angt[:, 0], ACT.Sin, scale=0.5).then_inc(sem("sines"), 1)

            def stats(q, src_wait):
                for t in range(NT):
                    src_wait(act, t)
                    if NT * q + t >= 2:
                        act.wait_ge(sem("norm_ss"), NT * q + t - 1)
                    s.activation(junk[:, t % 2, :], x[:, t, :], ACT.Square,
                                 accum_out=ss[:, t:t + 1]).then_inc(sem("norm_ss"), 1)
                    if t % 4 == 3:
                        act.wait_ge(sem("norm_ss"), NT * q + t + 1)
                        s.activation(sd[:, t - 3:t + 1], ss[:, t - 3:t + 1], ACT.Sqrt, scale=1.0 / D,
                                     bias=eps).then_inc(sem("norm_sd"), 1)

            def norm(q, k, src_wait, scale, bias):
                stats(q, src_wait)
                for u in range(2 * NK):
                    c = u % NK
                    act.wait_ge(sem("norm_turned"), 2 * NK * k + u + 1)
                    if u >= 2:
                        act.wait_ge(sem("norm_lo"), 2 * NK * k + u - 1)
                    s.activation(tmp2[:, u % 2, :], ps[:, u % 8, :], ACT.Identity, scale=scale(c),
                                 bias=bias(c)).then_inc(sem("norm_f"), 1)

            act.wait_ge(sem("scale_ready"), 1)
            norm(0, 0, lambda e, t: e.wait_ge(sem(f"x_in{t // 2}"), 32),
                 lambda c: scl[:, 0, c:c + 1], lambda c: mod[:, c:c + 1])

            for t in range(NT):
                act.wait_ge(sem("tm_full"), t + 1)
                s.activation(pr0[:, t, :].rearrange("p (j h d) -> p h j d", h=2, d=HD),
                             ps[:, t, :].rearrange("p (h j d) -> p h j d", h=2, d=HD),
                             ACT.Copy).then_inc(sem("tm_out0"), 1)
            for t in range(NT):
                act.wait_ge(sem("tm_full"), 2 * NT + t + 1)
                for r in range(2):
                    s.activation(pr2[:, t, 256 + r * HD:256 + (r + 1) * HD],
                                 ps[:, t, 256:256 + HD], ACT.Copy).then_inc(sem("tm_out2a"), 1)
                s.activation(pr2[:, t, 0:256], ps[:, t, 0:256], ACT.Copy).then_inc(sem("tm_out2a"), 1)

            def turned(n):
                dst = [qT[:, j, :] for j in range(4)] + [kT] + [qiT[:, j, :] for j in range(4)] + [kiT]
                return dst[n // 2][:, (n % 2) * HALF:(n % 2 + 1) * HALF]

            for n in range(0, 20):
                act.wait_ge(sem("pr_tp"), n + 1)
                s.activation(turned(n), ps[:, 4 + n % 4, :], ACT.Copy).then_inc(sem("pr_turned"), 1)

            act.wait_ge(sem("pr_turned"), 20)
            s.activation(ki_hi, kiT, ACT.Copy).then_inc(sem("rounded"), 1)
            s.activation(k_hi, kT, ACT.Copy).then_inc(sem("rounded"), 1)

            def relu_step(t, i):
                n = NH * (t - IDX0) + i
                w = (t + 1) * P
                u = unit_of["index", t, i]
                act.wait_ge(sem("score_full"), u + 1)
                if n >= 2:
                    act.wait_ge(sem("acc_done"), n - 1)
                s.activation(relu_of(t)[:, n % 2, 0:w], ps[:, 2 * (u % 2):2 * (u % 2) + 2, :]
                             .rearrange("p a b -> p (a b)")[:, 0:w], ACT.Relu,
                             scale=HD ** -0.5).then_inc(sem("relu_done"), 1)

            for c in range(NCC):
                if c == 2:
                    for _, t, i in EARLY:
                        relu_step(t, i)
                b = (4 * c) % 8
                for half in range(2):
                    act.wait_ge(sem("cm_full"), 4 * c + 2 + half + 1)
                    if c >= 1:
                        act.wait_ge(sem("glu_ready"), 2 * c - 1 + half)
                    s.activation(tmp2[:, half, :], ps[:, b + 2 + half, :], ACT.Sigmoid).then_inc(sem("glu_sig"), 1)

            act.wait_ge(sem("cm_full"), 4 * NCC)
            for c in range(NCC):
                act.wait_ge(sem("glu_ready"), 2 * NCC + 1)
                s.activation(glu_hi[:, NCC - 1 - c, :], glu[:, NCC - 1 - c, :], ACT.Copy).then_inc(sem("rounded"), 1)

            for kind, t, i in MICRO:
                w = (t + 1) * P
                cols = slice(t * HALF, (t + 1) * HALF)
                if kind == "index":
                    relu_step(t, i)
                if kind == "turn":
                    n = NH * t + i
                    for g in range(t // 4 + 1):
                        u = tp_of[t, i, g]
                        nb = min(4, t + 1 - 4 * g)
                        act.wait_ge(sem("tp_full"), tp_count[u])
                        if n >= 2:
                            act.wait_ge(sem("pv_done"), n - 1)
                        s.activation(probT[:, n % 2, 4 * g:4 * g + nb, :], ps[:, 4 + u % 2, 0:nb * P]
                                     .rearrange("p (b q) -> p b q", q=P), ACT.Copy).then_inc(sem("tp_out"), 1)
                if kind == "exp":
                    h = HEADS[i]
                    n = NH * t + i
                    act.wait_ge(sem("smax_ready"), n + 1)
                    if i == 0 and t >= 2:
                        act.wait_ge(sem("o_ready"), t - 1)
                    s.activation(prob[:, n % 2, 0:w], prob[:, n % 2, 0:w], ACT.Exp, scale=HD ** -0.5,
                                 bias=snm[:, h:h + 1], accum_out=ssum[:, t % 2, h:h + 1]).then_inc(sem("exp_done"), 1)
                if kind == "out":
                    u = tp_of[t, "o"]
                    act.wait_ge(sem("tp_full"), tp_count[u])
                    s.activation(h_hi[:, 0:4, t * P:(t + 1) * P], ps[:, 4 + u % 2, :].rearrange("p (c q) -> p c q", q=P),
                                 ACT.Copy).then_inc(sem("attn_hi"), 1)
                if kind == "conv":
                    for unit in range(2 * NCC):
                        if t < CONV_K * (unit + 1) <= i:
                            act.wait_ge(sem("tap_used"), CONV_K * (unit + 1))
                            c, half = unit // 2, unit % 2
                            s.activation(conv[:, c, half * HALF:(half + 1) * HALF], ps[:, 7, :], ACT.Identity,
                                         bias=vcol("conv_b", c)).then_inc(sem("conv_out"), 1)
                if kind == "ln_square":
                    if t:
                        act.wait_ge(sem("ln_summed"), NCC * t)
                    for c in range(NCC):
                        act.wait_ge(sem("ln_cent"), NCC * t + c + 1)
                        s.activation(squares[:, c, :], conv[:, c, cols], ACT.Square).then_inc(sem("ln_sq"), 1)
                if kind == "ln_scale":
                    act.wait_ge(sem("ln_summed"), NCC * (t + 1))
                    if t:
                        act.wait_ge(sem("ln_scaled"), NCC * t)
                    s.activation(tmp2[:, 1, :], ps[:, 7, :], ACT.Sqrt, scale=1.0 / CONV_CH,
                                 bias=eps).then_inc(sem("ln_sd"), 1)
                if kind == "ln_gate":
                    if t:
                        act.wait_ge(sem("ln_silu"), NCC * t)
                    for c in range(NCC):
                        act.wait_ge(sem("ln_aff"), NCC * t + c + 1)
                        s.activation(gates[:, c, :], conv[:, c, cols], ACT.Sigmoid).then_inc(sem("ln_sig"), 1)
                if kind == "ln_hi":
                    for c in range(NCC):
                        act.wait_ge(sem("ln_silu"), NCC * t + c + 1)
                        s.activation(h_hi[:, 4 + c, cols], conv[:, c, cols], ACT.Copy).then_inc(sem("conv_hi"), 1)
            act.wait_ge(sem("attn_lo"), NT)
            for t in range(NT):
                act.dma_start(x[:, t, :], a["x"][0, t * P:(t + 1) * P, :]).then_inc(sem(f"x_in{t // 2}"), 16)

            for g in range(4):
                act.wait_ge(sem("gate_mm"), g + 1)
                dst = (gate1, gate2)[g // 2][:, (g % 2) * HALF:(g % 2 + 1) * HALF]
                s.activation(dst, ps[:, g, :], ACT.Copy).then_inc(sem("gate_out"), 1)
            norm(1, 1, lambda e, t: e.wait_ge(sem("x_mixed"), NT + t + 1),
                 lambda c: scl[:, 1, c:c + 1], lambda c: mod[:, 3 * NK + c:3 * NK + c + 1])

            def mlp(k):
                with act.Fori(0, GROUPS) as g:
                    for b in range(9):
                        if b < 8:
                            act.wait_ge(sem(f"up_full{k}"), g * 8 + (b + 1))
                            act.wait_ge(sem(f"u_lo{k}"), g * 8 + (b + 1))
                            s.activation(act_r[:, b % 4, :], ps[:, b, :], ACT.Relu).then_inc(sem(f"up_relu{k}"), 1)
                        if b:
                            c = b - 1
                            act.wait_ge(sem(f"u_sq{k}"), g * 8 + (c + 1))
                            s.activation(u_hi[:, c // 2, (c % 2) * HALF:(c % 2 + 1) * HALF], act_r[:, c % 4, :],
                                         ACT.Copy).then_inc(sem(f"u_hi{k}"), 1)

            mlp(0)
            act.dma_start(frow, a["g_final"].rearrange("(o d) -> o d", o=1).to_broadcast([P, D])).then_inc(sem("frow_in"), 16)
            act.dma_start(abraw, w_in_2[:, :, ABC:ABC + 2 * GH]).then_inc(sem("ab_in"), 16)
            act.dma_start(dtb, a["dt_bias_2"].to_broadcast([P, GH])).then_inc(sem("gs_in"), 16)
            act.dma_start(alog, a["a_log_2"].to_broadcast([P, GH])).then_inc(sem("gs_in"), 16)
            act.dma_start(wpool, a["w_pool_2"].rearrange("l g c d -> (l c) g d")).then_inc(sem("wpool_in"), 16)
            stats(2, lambda e, t: e.wait_ge(sem("x_sum0"), 2 + 16 * (GROUPS - 1) + NT + t + 1))
            norm(3, 2, lambda e, t: e.wait_ge(sem("x_final"), t + 1), lambda c: vcol("norm_mix_2", c), lambda c: zero)

            def chunk_of(c):
                return (qc, kc, vc)[c // GH][:, c % GH, :]

            def pair(i):
                return ps[:, 2 * (i % 3):2 * (i % 3) + 2, :].rearrange("p a b -> p (a b)")

            def aux_out(i):
                kind, c = CH2[i]
                y = yt[:, i % 2, :]
                both = ps[:, 6:8, :].rearrange("p a b -> p (a b)")
                if kind == "pool":
                    act.wait_ge(sem("pool_mm"), c + 1)
                    s.activation(pm[:, c, :], both, ACT.Copy, scale=vcol("pool_scale_2", c)).then_inc(sem("pm_out"), 1)
                if kind == "qkv" and c < 2 * GH:
                    act.wait_ge(sem("l2_mm"), c + 1)
                    s.activation(y, both, ACT.Sqrt, scale=float(GD) if c < GH else 1.0,
                                 bias=eps2 if c < GH else eps).then_inc(sem("l2_sd"), 1)

            act.wait_ge(sem("x_out"), 16 * NT)
            for i in range(len(CH2) + 1):
                if i < len(CH2):
                    kind, c = CH2[i]
                    y = yt[:, i % 2, :]
                    act.wait_ge(sem("cm2_full"), 2 * i + 2)
                    if i >= 2 and ch_free[i - 2]:
                        act.wait_ge(sem(ch_free[i - 2][0]), ch_free[i - 2][1])
                    if kind == "pool":
                        s.activation(y, pair(i), ACT.Copy).then_inc(sem("pool_u"), 1)
                    if kind == "qkv":
                        s.activation(y, pair(i), ACT.Copy,
                                     scale=cw2[:, 3 * 12 + c:3 * 12 + c + 1]).then_inc(sem("tap0"), 1)
                    if kind == "z":
                        s.activation(zc[:, c, :], pair(i), ACT.Sigmoid).then_inc(sem("z_sig"), 1)
                if i:
                    aux_out(i - 1)
                if i < len(CH2) and kind == "qkv":
                    act.wait_ge(sem("taps"), 3 * (c + 1))
                    s.activation(chunk_of(c), y, ACT.Sigmoid).then_inc(sem("conv_sig"), 1)
                    if c < 2 * GH:
                        act.wait_ge(sem("conv_silu"), c + 1)
                        s.activation(y, chunk_of(c), ACT.Square).then_inc(sem("l2_sq"), 1)

            act.wait_ge(sem("gs_dve"), 1)
            s.activation(gs["t2"], gs["t1"], ACT.Abs).then_inc(sem("gs_act"), 1)
            act.wait_ge(sem("gs_act"), 1)
            s.activation(gs["t2"], gs["t2"], ACT.Exp, scale=-1.0).then_inc(sem("gs_act"), 1)
            act.wait_ge(sem("gs_act"), 2)
            s.activation(gs["t2"], gs["t2"], ACT.Ln, bias=1.0).then_inc(sem("gs_act"), 1)
            act.wait_ge(sem("gs_in"), 32)
            s.activation(alog, alog, ACT.Exp).then_inc(sem("gs_act"), 1)
            s.activation(gs["beta"], ab[:, :, GH:], ACT.Sigmoid).then_inc(sem("gs_act"), 1)
            act.wait_ge(sem("gs_dve"), 3)
            s.activation(gs["egc"], gs["gcum"], ACT.Exp).then_inc(sem("gs_act"), 1)
            act.wait_ge(sem("gs_dve"), 4)
            s.activation(gs["edec"], gs["edec"], ACT.Exp).then_inc(sem("gs_act"), 1)

            for kind, t, l in GSTEPS:
                b = prep[t % 2]
                x0, x1, x2 = (bank(3 * (t % 2) + i) for i in range(3))
                if kind == "head_a":
                    act.wait_ge(prep_sem("dve", t), prep_count("dve", t, "df"))
                    if t >= 2:
                        act.wait_ge(sem("scan_dve"), scan_count("dve", t - 2, "sdec1"))
                    s.activation(b["egb"], x0, ACT.Exp).then_inc(prep_sem("act", t), 1)
                    act.wait_ge(prep_sem("dve", t), prep_count("dve", t, "e12"))
                    s.activation(b["e1"], b["e1"], ACT.Exp, scale=-1.0).then_inc(prep_sem("act", t), 1)
                    s.activation(b["e2"], b["e2"], ACT.Exp).then_inc(prep_sem("act", t), 1)
                if kind == "level_z":
                    act.wait_ge(prep_sem("mm", t), prep_count("mm", t, f"z{l}"))
                    s.activation(b["z"], x0, ACT.Copy).then_inc(prep_sem("act", t), 1)
                if kind == "tail_b":
                    if t >= 2:
                        act.wait_ge(sem("scan_mm"), scan_count("mm", t - 2, "ai"))
                    act.wait_ge(prep_sem("mm", t), prep_count("mm", t, "val"))
                    s.activation(b["val"], x1, ACT.Copy).then_inc(prep_sem("act", t), 1)
                    act.wait_ge(prep_sem("mm", t), prep_count("mm", t, "kct"))
                    s.activation(b["kct"], x2, ACT.Copy).then_inc(prep_sem("act", t), 1)
                if kind == "finish_a":
                    act.wait_ge(sem("scan_mm"), scan_count("mm", t, "ai"))
                    s.activation(ot, bank(7), ACT.Copy).then_inc(sem("scan_act"), 1)
                if kind == "finish_b":
                    act.wait_ge(sem("scan_dve"), scan_count("dve", t, "sum"))
                    s.activation(osum, osum, ACT.Sqrt, scale=1.0 / GD, bias=eps).then_inc(sem("scan_act"), 1)

            act.wait_ge(sem("scan_dve"), scan_count("dve", NT - 1, "gated"))
            for t in range(NT):
                act.dma_start(x[:, t, :], x_mid[t]).then_inc(sem(f"x_in{t // 2}"), 16)
            for u in range(2 * NK):
                c, cols = u // 2, slice((u % 2) * HALF, (u % 2 + 1) * HALF)
                src = pm[:, c, cols] if c < GH else zc[:, c - GH, cols]
                s.activation(h_hi[:, c, cols], src, ACT.Copy).then_inc(sem("mix2_hi"), 1)
            act.dma_start(frow, a["norm_final_2"].rearrange("(o d) -> o d", o=1).to_broadcast([P, D])).then_inc(sem("frow_in"), 16)
            norm(4, 3, lambda e, t: e.wait_ge(sem("x_mixed2"), NT + t + 1), lambda c: vcol("norm_mlp_2", c), lambda c: zero)
            mlp(1)
            stats(5, lambda e, t: e.wait_ge(sem("down_out1"), 16 + 16 * (GROUPS - 1) + NT + t + 1))

        @block.vector
        def _(dve):
            v = nc.vector
            chain = [0]

            def link(ins):
                chain[0] += 1
                ins.then_inc(sem("dve_step"), 1)
                dve.wait_ge(sem("dve_step"), chain[0])

            dve.wait_ge(sem("rows_tp"), 1)
            v.tensor_copy(vec[:, 0:NVEC], ps[:, 0, 0:NVEC]).then_inc(sem("vec_ready"), 1)
            for i in range(CONV_K):
                o = CONV_K - 1 - i
                v.tensor_copy(cw[:, i * NCC:(i + 1) * NCC],
                              ps[:, 1, o * NCC:(o + 1) * NCC]).then_inc(sem("cw_ready"), 1)
            link(v.tensor_copy(cw2, ps[:, 2, 0:TAPS * 12]))
            dve.wait_ge(sem("c_sig"), 1)
            dve.wait_ge(sem("vec_ready"), 1)
            v.tensor_tensor(csil, csil, vcols("c"), ALU.mult).then_inc(sem("csil_ready"), 1)
            dve.wait_ge(sem("rows_in"), 16 * (len(VEC) + 3))
            v.tensor_copy(rowsp, rowsi).then_inc(sem("rowsp_ready"), 1)
            dve.wait_ge(sem("rows_tp"), 2)
            link(v.tensor_copy(pos, ps[:, 3, 0:NT]))
            dve.wait_ge(sem("pool_mem"), 3 + HROT)
            bc = [P, NT, HROT]
            link(v.tensor_tensor(angt[:, 0], pos.unsqueeze(2).to_broadcast(bc),
                                 freq.unsqueeze(1).to_broadcast(bc), ALU.mult))
            MAGIC = 1.5 * 2.0 ** 23
            link(v.tensor_scalar(angt[:, 1], angt[:, 0], 1.0 / (2 * np.pi), MAGIC, ALU.mult, ALU.add))
            link(v.tensor_scalar(angt[:, 1], angt[:, 1], -MAGIC, None, ALU.add))
            c1 = 6.28125
            c2 = float(np.float32(round((2 * np.pi - c1) * 2 ** 20) / 2 ** 20))
            c3 = 2 * np.pi - c1 - c2
            for cc in (c1, c2, c3):
                link(v.scalar_tensor_tensor(angt[:, 0], angt[:, 1], -cc, angt[:, 0], ALU.mult, ALU.add))
            v.tensor_scalar(angt[:, 0], angt[:, 0], 3.1415925, -3.1415925, ALU.min,
                            ALU.max).then_inc(sem("angle_ready"), 1)
            dve.wait_ge(sem("sines"), 2)
            link(v.tensor_tensor(cosv, angt[:, 1], angt[:, 1], ALU.mult))
            link(v.tensor_scalar(cosv, cosv, -2.0, 1.0, ALU.mult, ALU.add))

            dve.wait_ge(sem("ada_done"), 2 * NK)
            link(v.tensor_tensor(mod[:, 0:2 * NK], ps[:, 4, 0:2 * NK], vec[:, VEC["b_ada"][0]:VEC["b_ada"][0] + 2 * NK], ALU.add))
            v.scalar_tensor_tensor(scl[:, 0, :], mod[:, NK:2 * NK], 1.0, vcols("g_mix"), ALU.add,
                                   ALU.mult).then_inc(sem("scale_ready"), 1)

            def norm(q, k):
                for half in range(2):
                    dve.wait_ge(sem("norm_sd"), 2 * q + half + 1)
                    link(v.reciprocal(rs[:, 4 * half:4 * half + 4], sd[:, 4 * half:4 * half + 4]))
                    for t in range(4 * half, 4 * half + 4):
                        v.tensor_scalar(xn[:, t, :], x[:, t, :], rs[:, t:t + 1], None,
                                        ALU.mult).then_inc(sem("norm_xn"), 1)
                for u in range(2 * NK):
                    c, half = u % NK, u // NK
                    cols = slice(half * HALF, (half + 1) * HALF)
                    n = 2 * NK * k + u + 1
                    dve.wait_ge(sem("norm_f"), n)
                    v.tensor_copy(h_hi[:, c, cols], tmp2[:, u % 2, :]).then_inc(sem("norm_hi"), 1)
                    dve.wait_ge(sem("norm_hi"), n)
                    v.tensor_tensor(h_lo[:, c, cols], tmp2[:, u % 2, :], h_hi[:, c, cols].bitcast(F32),
                                    ALU.subtract).then_inc(sem("norm_lo"), 1)

            norm(0, 0)

            for t in range(NT):
                dve.wait_ge(sem("tm_full"), NT + t + 1)
                v.tensor_copy(pr1[:, t, 0:P], ps[:, t, 0:P]).then_inc(sem("tm_out1"), 1)
                v.tensor_copy(vtok[:, t, :], ps[:, t, P:2 * P]).then_inc(sem("tm_out1"), 1)
                v.tensor_copy(pr1[:, t, P:384], ps[:, t, 256:512]).then_inc(sem("tm_out1"), 1)

            def rope(ap, heads, name):
                sh = [P, NT, heads, HROT]
                x1, x2 = ap[:, :, :, 0:HROT], ap[:, :, :, HROT:ROT]
                co = cosv.unsqueeze(2).to_broadcast(sh)
                si = sinv.unsqueeze(2).to_broadcast(sh)
                t1, t2, t3, t4 = (ropet[:, i, 0:NT * heads * HROT].rearrange("p (t h r) -> p t h r", t=NT, r=HROT)
                                  for i in range(4))
                v.tensor_tensor(t1, x1, co, ALU.mult).then_inc(sem("rope_t"), 1)
                v.tensor_tensor(t2, x2, si, ALU.mult).then_inc(sem("rope_t"), 1)
                v.tensor_tensor(t3, x2, co, ALU.mult).then_inc(sem("rope_t"), 1)
                v.tensor_tensor(t4, x1, si, ALU.mult).then_inc(sem("rope_t"), 1)
                rope.n += 4
                dve.wait_ge(sem("rope_t"), rope.n)
                v.tensor_tensor(x1, t1, t2, ALU.subtract).then_inc(sem("roped"), 1)
                v.tensor_tensor(x2, t3, t4, ALU.add).then_inc(sem("roped"), 1)
                rope.m += 2
                dve.wait_ge(sem("roped"), rope.m)

            rope.n = rope.m = 0
            dve.wait_ge(sem("tm_out0"), NT)
            rope(pr0.rearrange("p t (h d) -> p t h d", d=HD), 8, "q")
            dve.wait_ge(sem("tm_out1"), 3 * NT)
            rope(pr1[:, :, 0:P].rearrange("p t (h d) -> p t h d", d=HD), 2, "k")
            rope(pr1[:, :, P:384].rearrange("p t (h d) -> p t h d", d=HD), 4, "qia")
            for t in range(NT):
                dve.wait_ge(sem("tm_full"), 2 * NT + t + 1)
                dve.wait_ge(sem("tm_out2a"), 3 * (t + 1))
                v.tensor_scalar(wi[:, t, :], ps[:, t, COL_WI - 1024:COL_WI - 1024 + NH], NH ** -0.5, None,
                                ALU.mult).then_inc(sem("tm_out2b"), 1)
            rope(pr2[:, :, 0:256].rearrange("p t (h d) -> p t h d", d=HD), 4, "qib")
            rope(pr2[:, :, 256:384].rearrange("p t (h d) -> p t h d", d=HD), 2, "ki")

            dve.wait_ge(sem("pr_turned"), 20)
            for n, (lo, whole, hi) in enumerate(((ki_lo, kiT, ki_hi), (k_lo, kT, k_hi))):
                dve.wait_ge(sem("rounded"), n + 1)
                v.tensor_tensor(lo, whole, hi.bitcast(F32), ALU.subtract).then_inc(sem("rests"), 1)

            topk_n = [0]

            def topk(t, part):
                sc = score[t % 3][:, 0:(t + 1) * P]
                r0, r1 = ROUNDS * part // TOPK_PARTS[t], ROUNDS * (part + 1) // TOPK_PARTS[t]
                dve.wait_ge(sem("acc_done"), NH * (t - IDX0 + 1))
                for r in range(r0, r1):
                    v.max(best, sc).then_inc(sem("topk_step"), 1)
                    dve.wait_ge(sem("topk_step"), topk_n[0] + 1)
                    v.match_replace(sc, best, sc, TAKEN).then_inc(sem("topk_step"), 1)
                    dve.wait_ge(sem("topk_step"), topk_n[0] + 2)
                    topk_n[0] += 2
                if r1 == ROUNDS:
                    link(v.tensor_scalar(sc, sc, TAKEN, MASKED, ALU.not_equal, ALU.mult))

            def acc_step(t, i):
                w = (t + 1) * P
                sc = score[t % 3][:, 0:w]
                n = NH * (t - IDX0) + i
                dve.wait_ge(sem("relu_done"), n + 1)
                if i:
                    dve.wait_ge(sem("acc_done"), n)
                v.scalar_tensor_tensor(sc, relu_of(t)[:, n % 2, 0:w], wi[:, t, i:i + 1],
                                       sc if i else idx0[:, S - w:S], ALU.mult, ALU.add).then_inc(sem("acc_done"), 1)

            for c in range(NCC):
                if c == 2:
                    dve.wait_ge(sem("idx_ready"), 1)
                    dve.wait_ge(sem("tm_out2b"), NT)
                    for _, t, i in EARLY:
                        acc_step(t, i)
                b = (4 * c) % 8
                for half in range(2):
                    dve.wait_ge(sem("cm_full"), 4 * c + half + 1)
                    dve.wait_ge(sem("glu_sig"), 2 * c + half + 1)
                    if c == NCC - 1:
                        dve.wait_ge(sem("cm_full"), 4 * NCC)
                    v.tensor_tensor(glu[:, NCC - 1 - c, PAD + half * HALF:PAD + (half + 1) * HALF], ps[:, b + half, :],
                                    tmp2[:, half, :], ALU.mult).then_inc(sem("glu_ready"), 1)
                if c == NCC - 1:
                    dve.wait_ge(sem("cm_full"), 4 * NCC)
                    v.memset(glu[:, :, 0:PAD], 0.0).then_inc(sem("glu_ready"), 1)
                for part in EARLY_PARTS[c]:
                    topk(IDX0, part)
            for c in range(NCC):
                dve.wait_ge(sem("rounded"), 2 + c + 1)
                gc = NCC - 1 - c
                v.tensor_tensor(glu_lo[:, gc, :], glu[:, gc, :], glu_hi[:, gc, :].bitcast(F32),
                                ALU.subtract).then_inc(sem("rests"), 1)

            nmod = 0
            for kind, t, i in MICRO:
                w = (t + 1) * P
                cols = slice(t * HALF, (t + 1) * HALF)
                if kind == "index":
                    acc_step(t, i)
                if kind == "scores":
                    bias = idx0[:, S - w:S] if t < IDX_TILES[0] else score[t % 3][:, 0:w]
                    h = HEADS[i]
                    n = NH * t + i
                    u = unit_of[kind, t, i]
                    dve.wait_ge(sem("score_full"), u + 1)
                    if n >= 2:
                        dve.wait_ge(sem("tp_full"), tp_last[n - 2])
                    v.tensor_tensor_reduce(prob[:, n % 2, 0:w],
                                           ps[:, 2 * (u % 2):2 * (u % 2) + 2, :]
                                           .rearrange("p a b -> p (a b)")[:, 0:w], bias, 1.0, -3.4e38,
                                           ALU.add, ALU.max, smax[:, h:h + 1]).then_inc(sem("masked"), 1)
                    dve.wait_ge(sem("masked"), n + 1)
                    if n >= NH:
                        dve.wait_ge(sem("exp_done"), n - NH + 1)
                    v.tensor_scalar(snm[:, h:h + 1], smax[:, h:h + 1], -HD ** -0.5, None,
                                    ALU.mult).then_inc(sem("smax_ready"), 1)
                if kind == "topk":
                    topk(t, i)
                if kind == "divide":
                    dve.wait_ge(sem("exp_done"), NH * (t + 1))
                    link(v.reciprocal(srec, ssum[:, t % 2, :]))
                    dve.wait_ge(sem("pv_done"), NH * (t + 1))
                    if t:
                        dve.wait_ge(sem("attn_lo"), t)
                    v.tensor_tensor(v3(otok, NH), v3(ps[:, 6, :], NH), srec.unsqueeze(2).to_broadcast([P, NH, HD]),
                                    ALU.mult).then_inc(sem("o_ready"), 1)
                if kind == "out":
                    u = tp_of[t, "o"]
                    dve.wait_ge(sem("attn_hi"), t + 1)
                    v.tensor_tensor(h_lo[:, 0:4, t * P:(t + 1) * P], v3(ps[:, 4 + u % 2, :], 4),
                                    h_hi[:, 0:4, t * P:(t + 1) * P].bitcast(F32),
                                    ALU.subtract).then_inc(sem("attn_lo"), 1)
                if kind == "ada_out":
                    u = tp_of["ada", t]
                    m0 = 2 * NK + t
                    dve.wait_ge(sem("ada_done"), 2 * NK + i)
                    v.tensor_tensor(mod[:, m0:2 * NK + i], ps[:, 4 + u % 2, 0:i - t],
                                    vec[:, VEC["b_ada"][0] + m0:VEC["b_ada"][0] + 2 * NK + i],
                                    ALU.add).then_inc(sem("mod_out"), 1)
                    nmod += 1
                    if i == 4 * NK:
                        dve.wait_ge(sem("mod_out"), nmod)
                        v.scalar_tensor_tensor(scl[:, 1, :], mod[:, 4 * NK:5 * NK], 1.0, vcols("g_mlp"), ALU.add,
                                               ALU.mult).then_inc(sem("scale_ready"), 1)
                if kind == "ln_mean":
                    dve.wait_ge(sem("ln_mean"), t + 1)
                    for c in range(NCC):
                        v.scalar_tensor_tensor(conv[:, c, cols], ps[:, 7, :], -1.0 / CONV_CH, conv[:, c, cols],
                                               ALU.mult, ALU.add).then_inc(sem("ln_cent"), 1)
                if kind == "ln_scale":
                    dve.wait_ge(sem("ln_sd"), t + 1)
                    link(v.reciprocal(tmp2[:, 1, :], tmp2[:, 1, :]))
                    for c in range(NCC):
                        v.tensor_tensor(conv[:, c, cols], conv[:, c, cols], tmp2[:, 1, :],
                                        ALU.mult).then_inc(sem("ln_scaled"), 1)
                    for c in range(NCC):
                        dve.wait_ge(sem("ln_scaled"), NCC * t + c + 1)
                        v.tensor_scalar(conv[:, c, cols], conv[:, c, cols], vcol("conv_norm_g", c),
                                        vcol("conv_norm_b", c), ALU.mult, ALU.add).then_inc(sem("ln_aff"), 1)
                if kind == "ln_silu":
                    for c in range(NCC):
                        dve.wait_ge(sem("ln_sig"), NCC * t + c + 1)
                        v.tensor_tensor(conv[:, c, cols], conv[:, c, cols], gates[:, c, :],
                                        ALU.mult).then_inc(sem("ln_silu"), 1)
                if kind == "ln_lo":
                    for c in range(NCC):
                        dve.wait_ge(sem("conv_hi"), NCC * t + c + 1)
                        v.tensor_tensor(h_lo[:, 4 + c, cols], conv[:, c, cols], h_hi[:, 4 + c, cols].bitcast(F32),
                                        ALU.subtract).then_inc(sem("conv_lo"), 1)

            for gi, base in enumerate((2 * NK, 5 * NK)):
                for c in range(NK):
                    if gi:
                        dve.wait_ge(sem("gate_mm"), 1 + c // 4)
                    v.tensor_scalar(gdiag[:, c, :], ident, mod[:, base + c:base + c + 1], None,
                                    ALU.mult).then_inc(sem("gdiag_ready"), 1)
            for j in range(2):
                for t in range(NT):
                    n = NT * j + t
                    dve.wait_ge(sem("wo_full"), n + 1)
                    if j == 0:
                        dve.wait_ge(sem(f"x_in{t // 2}"), 64)
                    if j == 0 and t == 0:
                        dve.wait_ge(sem("gate_out"), 4)
                    if n >= 2:
                        dve.wait_ge(sem("x_mixed"), n - 1)
                    cols = slice(j * HALF, (j + 1) * HALF)
                    v.tensor_tensor(tmp2[:, n % 2, :], ps[:, t, :], gate1[:, cols], ALU.mult).then_inc(sem("gated"), 1)
                    dve.wait_ge(sem("gated"), n + 1)
                    v.tensor_tensor(x[:, t, cols], x[:, t, cols], tmp2[:, n % 2, :], ALU.add).then_inc(sem("x_mixed"), 1)
            norm(1, 1)

            def mlp(k, gate):
                with dve.Fori(0, GROUPS) as g:
                    for b in range(9):
                        if b < 8:
                            dve.wait_ge(sem(f"up_relu{k}"), g * 8 + (b + 1))
                            v.tensor_tensor(act_r[:, b % 4, :], act_r[:, b % 4, :], act_r[:, b % 4, :],
                                            ALU.mult).then_inc(sem(f"u_sq{k}"), 1)
                        if b:
                            c = b - 1
                            cols = slice((c % 2) * HALF, (c % 2 + 1) * HALF)
                            dve.wait_ge(sem(f"u_hi{k}"), g * 8 + (c + 1))
                            v.tensor_tensor(u_lo[:, c // 2, cols], act_r[:, c % 4, :],
                                            u_hi[:, c // 2, cols].bitcast(F32), ALU.subtract).then_inc(sem(f"u_lo{k}"), 1)
                    for n in range(2 * NT):
                        j, t = n // NT, n % NT
                        cols = slice(j * HALF, (j + 1) * HALF)
                        dve.wait_ge(sem(f"down_full{k}"), g * 16 + (n + 1 + 16))
                        if gate is None:
                            v.tensor_tensor(x[:, t, cols], x[:, t, cols], ps[:, t, :],
                                            ALU.add).then_inc(sem(f"down_out{k}"), 1)
                        else:
                            dve.wait_ge(sem(f"x_sum{k}"), g * 16 + (n + 1))
                            v.tensor_tensor(tmp2[:, n % 2, :], ps[:, t, :], gate[:, cols],
                                            ALU.mult).then_inc(sem(f"down_out{k}"), 1)
                            dve.wait_ge(sem(f"down_out{k}"), g * 16 + (n + 1 + 16))
                            v.tensor_tensor(x[:, t, cols], x[:, t, cols], tmp2[:, n % 2, :],
                                            ALU.add).then_inc(sem(f"x_sum{k}"), 1)

            def mlp_start(k):
                dve.sem_inc(sem(f"down_out{k}"), 16)
                dve.sem_inc(sem(f"u_lo{k}"), 4)
                dve.sem_inc(sem(f"x_sum{k}"), 2)

            def final(q, done):
                for half in range(2):
                    dve.wait_ge(sem("norm_sd"), 2 * q + half + 1)
                    link(v.reciprocal(rs[:, 4 * half:4 * half + 4], sd[:, 4 * half:4 * half + 4]))
                    for t in range(4 * half, 4 * half + 4):
                        v.scalar_tensor_tensor(x[:, t, :], x[:, t, :], rs[:, t:t + 1], frow, ALU.mult,
                                               ALU.mult).then_inc(sem(done), 1)

            mlp_start(0)
            mlp(0, gate2)
            dve.wait_ge(sem("frow_in"), 16)
            final(2, "x_final")
            norm(3, 2)

            def chunk_of(c):
                return (qc, kc, vc)[c // GH][:, c % GH, :]

            def pair(i):
                return ps[:, 2 * (i % 3):2 * (i % 3) + 2, :].rearrange("p a b -> p (a b)")

            ntap = [0]
            for i in range(len(CH2) + 1):
                if i < len(CH2):
                    kind, c = CH2[i]
                    y = yt[:, i % 2, :]
                    if i == 0:
                        dve.wait_ge(sem("ab_full"), 1)
                        v.tensor_copy(abT, ps[0:2 * GH, 6:8, :].rearrange("p a b -> p (a b)")).then_inc(sem("ab_out"), 1)
                    if i == 1:
                        dve.wait_ge(sem("ab_full"), 2)
                        v.tensor_copy(ab, ps[:, 6, 0:NT * 2 * GH].rearrange("p (t n) -> p t n", t=NT)).then_inc(sem("ab_out"), 1)
                    if kind == "pool":
                        dve.wait_ge(sem("pool_u"), c + 1)
                        w, src = WINDOWS[c], y
                        k, d = 0, 1
                        while d < w:
                            dst = (zc, pm)[k % 2][:, c, :]
                            v.tensor_copy(dst[:, 0:d], src[:, 0:d])
                            link(v.tensor_tensor(dst[:, d:], src[:, d:], src[:, 0:S - d], ALU.add))
                            src, k, d = dst, k + 1, 2 * d
                        e = w - 1
                        link(v.tensor_tensor(src[:, 0:e], src[:, 0:e], invc[:, 0:e], ALU.mult))
                        v.tensor_tensor(y[:, 0:e], src[:, 0:e], y[:, 0:e], ALU.subtract).then_inc(sem("pooled"), 1)
                        v.scalar_tensor_tensor(y[:, e:], src[:, e:], 1.0 / w, y[:, e:], ALU.mult,
                                               ALU.subtract).then_inc(sem("pooled"), 1)
                    if kind == "qkv":
                        dve.wait_ge(sem("tap0"), c + 1)
                        for sft in range(1, TAPS):
                            if ntap[0] % 3:
                                dve.wait_ge(sem("taps"), ntap[0])
                            col = (TAPS - 1 - sft) * 12 + c
                            v.scalar_tensor_tensor(y[:, sft:], pair(i)[:, 0:S - sft], cw2[:, col:col + 1], y[:, sft:],
                                                   ALU.mult, ALU.add).then_inc(sem("taps"), 1)
                            ntap[0] += 1
                    if kind == "z":
                        dve.wait_ge(sem("z_sig"), c + 1)
                        v.tensor_tensor(zc[:, c, :], pair(i), zc[:, c, :], ALU.mult).then_inc(sem("z_silu"), 1)
                if i:
                    kind1, c1 = CH2[i - 1]
                    if kind1 == "qkv" and c1 < 2 * GH:
                        y1 = yt[:, (i - 1) % 2, :]
                        dve.wait_ge(sem("l2_sd"), c1 + 1)
                        link(v.reciprocal(y1, y1))
                        v.tensor_tensor(chunk_of(c1), chunk_of(c1), y1, ALU.mult).then_inc(sem("l2_done"), 1)
                if i < len(CH2) and kind == "qkv":
                    dve.wait_ge(sem("conv_sig"), c + 1)
                    v.tensor_tensor(chunk_of(c), chunk_of(c), y, ALU.mult).then_inc(sem("conv_silu"), 1)

            tn = [P, NT, GH]
            dve.wait_ge(sem("gs_in"), 32)
            dve.wait_ge(sem("ab_out"), 2)
            v.tensor_tensor(gs["t1"], ab[:, :, 0:GH], dtb.unsqueeze(1).to_broadcast(tn), ALU.add).then_inc(sem("gs_dve"), 1)
            dve.wait_ge(sem("gs_act"), 4)
            link(v.tensor_scalar(gs["t1"], gs["t1"], 0.0, None, ALU.max))
            link(v.tensor_tensor(gs["t1"], gs["t1"], gs["t2"], ALU.add))
            v.scalar_tensor_tensor(gs["g"], gs["t1"], -1.0, alog.unsqueeze(1).to_broadcast(tn), ALU.mult,
                                   ALU.mult).then_inc(sem("gs_dve"), 1)
            dve.wait_ge(sem("gs_mm"), 2)
            v.tensor_copy(gs["gcum"], ps[:, 6, 0:32].rearrange("p (t h) -> p t h", h=GH)).then_inc(sem("gs_dve"), 1)
            dve.wait_ge(sem("gs_dve"), 3)
            v.tensor_tensor(gs["edec"], ps[:, 6, 32:64].rearrange("p (t h) -> p t h", h=GH), gs["gcum"],
                            ALU.subtract).then_inc(sem("gs_dve"), 1)
            dve.wait_ge(sem("gs_act"), 7)
            link(v.tensor_tensor(gs["bege"], gs["beta"], gs["egc"], ALU.mult))
            dve.wait_ge(sem("masks_ready"), 1)

            for kind, t, l in GSTEPS:
                b = prep[t % 2]
                x0, x1, x2 = (bank(3 * (t % 2) + i) for i in range(3))
                if kind == "head_a":
                    if t >= 2:
                        dve.wait_ge(prep_sem("mm", t - 2), prep_count("mm", t - 2, "kct"))
                    v.tensor_tensor(b["z"], hb(tri), tb(gs["g"][:, t, :]), ALU.mult).then_inc(prep_sem("dve", t), 1)
                    dve.wait_ge(prep_sem("mm", t), prep_count("mm", t, "gb"))
                    v.tensor_tensor(b["e1"], x0, tb(gs["gcum"][:, t, :]), ALU.subtract).then_inc(prep_sem("dve", t), 1)
                    dve.wait_ge(prep_sem("dve", t), prep_count("dve", t, "df"))
                    link(v.tensor_scalar(b["e2"], b["e1"], 0.0, None, ALU.min))
                    v.tensor_scalar(b["e1"], b["e1"], 0.0, None, ALU.max).then_inc(prep_sem("dve", t), 1)
                if kind == "head_b":
                    dve.wait_ge(prep_sem("mm", t), prep_count("mm", t, "gram"))
                    dve.wait_ge(prep_sem("pool", t), prep_count("pool", t, "e1m"))
                    for h in range(GH):
                        last = v.scalar_tensor_tensor(b["m"][:, h, :], x1[:, h, :], gs["beta"][:, t, h:h + 1],
                                                      b["e1"][:, h, :], ALU.mult, ALU.mult)
                    last.then_inc(prep_sem("dve", t), 1)
                    dve.wait_ge(prep_sem("mm", t), prep_count("mm", t, "kq"))
                    dve.wait_ge(prep_sem("pool", t), prep_count("pool", t, "e2m"))
                    if t >= 2:
                        dve.wait_ge(sem("scan_mm"), scan_count("mm", t - 2, "ai"))
                    v.tensor_tensor(b["ait"], x2, b["e2"], ALU.mult).then_inc(prep_sem("dve", t), 1)
                    dve.wait_ge(prep_sem("mm", t), prep_count("mm", t, "turn"))
                    v.tensor_tensor(b["u"], hb(ident), x0, ALU.subtract).then_inc(prep_sem("dve", t), 1)
                if kind == "level_tu":
                    dve.wait_ge(prep_sem("mm", t), prep_count("mm", t, f"u{l}"))
                    if l < 5:
                        if l == 1:
                            dve.wait_ge(prep_sem("pool", t), prep_count("pool", t, "t0"))
                        v.tensor_tensor(b["t"], b["t"], x1, ALU.subtract).then_inc(prep_sem("dve", t), 1)
                    v.tensor_tensor(b["u"], b["u"], x2, ALU.subtract).then_inc(prep_sem("dve", t), 1)
                if kind == "tail_a":
                    dve.wait_ge(prep_sem("mm", t), prep_count("mm", t, "ktp"))
                    v.tensor_tensor(b["kbe"], x0, tb(gs["bege"][:, t, :]), ALU.mult).then_inc(prep_sem("dve", t), 1)
                    if t >= 2:
                        dve.wait_ge(sem("scan_mm"), scan_count("mm", t - 2, "kdv1"))
                    v.tensor_tensor(b["kd"], x0, tb(gs["edec"][:, t, :]), ALU.mult).then_inc(prep_sem("dve", t), 1)
                    dve.wait_ge(prep_sem("mm", t), prep_count("mm", t, "vtp"))
                    v.tensor_tensor(b["vb"], x1, tb(gs["beta"][:, t, :]), ALU.mult).then_inc(prep_sem("dve", t), 1)
                if kind in ("chunk_a", "chunk_b"):
                    r = slice(CHUNK * l, CHUNK * (l + 1))
                    e = CHUNK * (l + 1) - 1
                if kind == "chunk_a":
                    dve.wait_ge(sem("scan_mm"), scan_count("mm", t, f"kq{l}"))
                    if l == 0 and t:
                        dve.wait_ge(sem("scan_mm"), scan_count("mm", t - 1, "ai"))
                        dve.wait_ge(sem("scan_dve"), scan_count("dve", t - 1, "sum"))
                    v.tensor_tensor(vnew[r], b["val"][r], bank(6)[r], ALU.subtract).then_inc(sem("scan_dve"), 1)
                    v.tensor_tensor(state, state, b["egb"][:, :, e:e + 1].to_broadcast([P, GH, P]),
                                    ALU.mult).then_inc(sem("scan_dve"), 1)
                if kind == "chunk_b":
                    dve.wait_ge(sem("scan_mm"), scan_count("mm", t, f"kdv{l}"))
                    dve.wait_ge(sem("scan_dve"), scan_count("dve", t, f"sdec{l}"))
                    v.tensor_tensor(state, state, bank(6), ALU.add).then_inc(sem("scan_dve"), 1)
                if kind == "finish_a":
                    dve.wait_ge(sem("scan_act"), scan_count("act", t, "ot"))
                    v.tensor_tensor(vnew, ot, ot, ALU.mult).then_inc(sem("scan_dve"), 1)
                    dve.wait_ge(sem("scan_dve"), scan_count("dve", t, "sq"))
                    v.tensor_reduce(osum, vnew, AX.X, ALU.add).then_inc(sem("scan_dve"), 1)
                if kind == "finish_b":
                    dve.wait_ge(sem("scan_act"), scan_count("act", t, "sd"))
                    v.reciprocal(orec, osum).then_inc(sem("scan_dve"), 1)
                    dve.wait_ge(sem("scan_dve"), scan_count("dve", t, "rec"))
                    v.tensor_tensor(ot, ot, tb(orec), ALU.mult).then_inc(sem("scan_dve"), 1)
                if kind == "finish_c":
                    dve.wait_ge(sem("scan_mm"), scan_count("mm", t, "otp"))
                    zt = zc[:, :, t * P:(t + 1) * P]
                    v.scalar_tensor_tensor(zt, bank(7), vcol("gdn_norm_2"), zt, ALU.mult,
                                           ALU.mult).then_inc(sem("scan_dve"), 1)

            for u in range(2 * NK):
                c, cols = u // 2, slice((u % 2) * HALF, (u % 2 + 1) * HALF)
                src = pm[:, c, cols] if c < GH else zc[:, c - GH, cols]
                dve.wait_ge(sem("mix2_hi"), u + 1)
                v.tensor_tensor(h_lo[:, c, cols], src, h_hi[:, c, cols].bitcast(F32),
                                ALU.subtract).then_inc(sem("mix2_lo"), 1)
            for j in range(2):
                for t in range(NT):
                    cols = slice(j * HALF, (j + 1) * HALF)
                    dve.wait_ge(sem("wo2_full"), NT * j + t + 1)
                    if j == 0:
                        dve.wait_ge(sem(f"x_in{t // 2}"), 96)
                    v.tensor_tensor(x[:, t, cols], x[:, t, cols], ps[:, t, :], ALU.add).then_inc(sem("x_mixed2"), 1)
            norm(4, 3)
            dve.sem_inc(sem("down_out1"), 16)
            dve.sem_inc(sem("u_lo1"), 4)
            mlp(1, None)
            dve.wait_ge(sem("frow_in"), 32)
            final(5, "y_final")

        @block.tensor
        def _(pe):
            mm = nc.tensor.matmul
            pe.wait_ge(sem("ident_ready"), 2)
            pe.wait_ge(sem("rows_in"), 16 * (len(VEC) + 3))
            nc.tensor.transpose(ps[:, 0, 0:NVEC], rowsv[0:NVEC, 0, :], ident[0:NVEC, 0:NVEC])
            n = CONV_K * NCC
            nc.tensor.transpose(ps[:, 1, 0:n], rowsv[0:n, 1, :], ident[0:n, 0:n])
            n = TAPS * 12
            nc.tensor.transpose(ps[:, 2, 0:n], rowsv[0:n, 2, :], ident[0:n, 0:n]).then_inc(sem("rows_tp"), 1)
            pe.wait_ge(sem("rowsp_ready"), 1)
            nc.tensor.transpose(ps[:, 3, 0:NT], rowsp, ident[0:NT, 0:NT]).then_inc(sem("rows_tp"), 1)

            def ada(n, j, out_col):
                pe.wait_ge(raw_in[n % 4], 16 * (n // 4 + 1))
                wt = v3(raw[:, n % 4, :], NK)
                for k in range(NK):
                    last = mm(out_col, wt[:, k, :], csil[:, k:k + 1], start=(k == 0), stop=(k == NK - 1))
                last.then_inc(sem("ada_done"), 1)

            pe.wait_ge(sem("csil_ready"), 1)
            for j in range(2 * NK):
                ada(j, j, ps[:, 4, j:j + 1])

            def norm(k):
                for u in range(2 * NK):
                    c, half = u % NK, u // NK
                    if c == 0:
                        pe.wait_ge(sem("norm_xn"), NT * k + 4 * half + 4)
                    if u >= 8:
                        pe.wait_ge(sem("norm_f"), 2 * NK * k + u - 7)
                    for i in range(4):
                        last = nc.tensor.transpose(ps[:, u % 8, i * P:(i + 1) * P],
                                                   xn[:, 4 * half + i, c * P:(c + 1) * P], ident)
                    last.then_inc(sem("norm_turned"), 1)

            def cm(m, half, bank, ready, full):
                r = m % 4
                cols = slice(half * HALF, (half + 1) * HALF)
                for k in range(NK):
                    if ready:
                        ready(k)
                    wh, wl = (v3(w[:, r, :], NK)[:, k, :] for w in (w_hi, w_lo))
                    mm(ps[:, bank, :], wh, h_hi[:, k, cols], start=(k == 0), stop=False)
                    mm(ps[:, bank, :], wh, h_lo[:, k, cols], start=False, stop=False)
                    last = mm(ps[:, bank, :], wl, h_hi[:, k, cols], start=False, stop=(k == NK - 1))
                last.then_inc(sem(full), 1)

            def tm(m, t, k0, width, hi, lo, start, stop):
                r = m % 4
                tok = slice(t * P, (t + 1) * P)
                for k in range(2):
                    wh, wl = (w[:, r, 0:2 * width].rearrange("p (k n) -> p k n", k=2)[:, k, :] for w in (w_hi, w_lo))
                    mm(ps[:, t, 0:width], hi[:, k0 + k, tok], wh, start=(start and k == 0), stop=False)
                    mm(ps[:, t, 0:width], hi[:, k0 + k, tok], wl, start=False, stop=False)
                    last = mm(ps[:, t, 0:width], lo[:, k0 + k, tok], wh, start=False, stop=(stop and k == 1))
                return last

            norm(0)
            for j, (c0, width) in enumerate(TM_COLS):
                for kk in range(4):
                    m = 4 * j + kk
                    pe.wait_ge(sem("split_done"), m + 1)
                    for t in range(NT):
                        if j == 0 and t % 4 == 0:
                            pe.wait_ge(sem("norm_lo"), NK * (t // 4) + 2 * kk + 2)
                            if kk == 0:
                                pe.wait_ge(sem("norm_f"), 2 * NK)
                        if kk == 0 and j == 1:
                            pe.wait_ge(sem("tm_out0"), t + 1)
                        if kk == 0 and j == 2:
                            pe.wait_ge(sem("tm_out1"), 3 * (t + 1))
                        last = tm(m, t, 2 * kk, width, h_hi, h_lo, kk == 0, kk == 3)
                        if kk == 3:
                            last.then_inc(sem("tm_full"), 1)
                        elif t == NT - 1:
                            last.then_inc(sem("tm_part"), 1)

            def cu(i):
                c, part = i // 2, i % 2
                pe.wait_ge(sem("split_done"), 12 + i + 1)
                for half in range(2):
                    b = (4 * c) % 8 + 2 * part + half
                    if c == 0:
                        pe.wait_ge(sem("tm_out2a"), 3 * (b + 1))
                        pe.wait_ge(sem("tm_out2b"), b + 1)
                    if c == 1:
                        pe.wait_ge(sem("pr_turned"), 20)
                    if c >= 2:
                        pe.wait_ge(sem("glu_ready"), 2 * (c - 1))
                    cm(12 + i, half, b, None, "cm_full")

            cu(0)
            cu(1)
            pe.wait_ge(sem("roped"), 10)
            pe.wait_ge(sem("tm_out2a"), 3 * NT)
            pe.wait_ge(sem("tm_out2b"), NT)
            srcs = [pr0[:, :, j * P:(j + 1) * P] for j in range(4)] + [pr1[:, :, j * P:(j + 1) * P] for j in range(3)] \
                + [pr2[:, :, j * P:(j + 1) * P] for j in range(3)]
            for n in range(20):
                if n >= 4:
                    pe.wait_ge(sem("pr_turned"), n - 3)
                for i in range(4):
                    last = nc.tensor.transpose(ps[:, 4 + n % 4, i * P:(i + 1) * P],
                                               srcs[n // 2][:, 4 * (n % 2) + i, :], ident)
                last.then_inc(sem("pr_tp"), 1)
            def score_mm(kind, t, i, q, k, row):
                u = unit_of[kind, t, i]
                if u >= 2:
                    pe.wait_ge(sem(units[u - 2][0]), units[u - 2][1])
                w = (t + 1) * P
                b = 2 * (u % 2)
                qh, ql = (x[row:row + HD] for x in q)
                for c0 in range(0, w, HALF):
                    cn = min(HALF, w - c0)
                    o = ps[:, b + c0 // HALF, 0:cn]
                    kh, kl = (x[row:row + HD, c0:c0 + cn] for x in k)
                    mm(o, qh, kh, start=True, stop=False)
                    mm(o, qh, kl, start=False, stop=False)
                    last = mm(o, ql, kh, start=False, stop=True)
                last.then_inc(sem("score_full"), 1)

            def index_mm(t, i):
                pe.wait_ge(sem("qi_split"), t - IDX0 + 1)
                j = i // 2
                score_mm("index", t, i, (qi_hi_of(t)[:, j // 2, j % 2, :], qi_lo[:, j, t * P:(t + 1) * P]), (ki_hi, ki_lo),
                         HD * (i % 2))

            for i in range(2, 2 * NCC):
                if i == 4:
                    pe.wait_ge(sem("glu_ready"), 2)
                    pe.wait_ge(sem("rests"), 2)
                    for _, t, h in EARLY:
                        index_mm(t, h)
                    pe.wait_ge(sem("relu_done"), NH)
                cu(i)

            pe.wait_ge(sem("glu_ready"), 2 * NCC)
            for kind, t, i in MICRO:
                tok = slice(t * P, (t + 1) * P)
                if kind == "index":
                    index_mm(t, i)
                if kind == "scores":
                    pe.wait_ge(sem("q_split"), t + 1)
                    j = HEADS[i] % 4
                    score_mm(kind, t, i, (q_hi[:, j, tok], q_lo[:, j, tok]), (k_hi, k_lo), HD * (HEADS[i] // 4))
                if kind == "turn":
                    n = NH * t + i
                    pe.wait_ge(sem("exp_done"), n + 1)
                    for g in range(t // 4 + 1):
                        u = tp_of[t, i, g]
                        if u >= 2:
                            pe.wait_ge(sem(tp_free[u - 2][0]), tp_free[u - 2][1])
                        for bb in range(4 * g, min(4 * g + 4, t + 1)):
                            last = nc.tensor.transpose(ps[:, 4 + u % 2, (bb % 4) * P:(bb % 4 + 1) * P],
                                                       prob[:, n % 2, bb * P:(bb + 1) * P], ident)
                        last.then_inc(sem("tp_full"), 1)
                if kind == "values":
                    n = NH * t + i
                    pe.wait_ge(sem("tp_out"), tp_outs[n])
                    if i == 0 and t:
                        pe.wait_ge(sem("o_ready"), t)
                    h, kv = HEADS[i], HEADS[i] // 4
                    for bb in range(t + 1):
                        last = mm(ps[:, 6, h * HD:(h + 1) * HD], probT[:, n % 2, bb, :],
                                  vtok[:, bb, kv * HD:(kv + 1) * HD], start=(bb == 0), stop=(bb == t))
                    last.then_inc(sem("pv_done"), 1)
                if kind == "out":
                    u = tp_of[t, "o"]
                    pe.wait_ge(sem("o_ready"), t + 1)
                    pe.wait_ge(sem(tp_free[u - 2][0]), tp_free[u - 2][1])
                    for c in range(4):
                        last = nc.tensor.transpose(ps[:, 4 + u % 2, c * P:(c + 1) * P],
                                                   otok[:, c * P:(c + 1) * P], ident)
                    last.then_inc(sem("tp_full"), 1)
                if kind == "conv":
                    for k in range(t, i):
                        unit, tap = k // CONV_K, k % CONV_K
                        c, half = unit // 2, unit % 2
                        if tap == 0 and unit:
                            pe.wait_ge(sem("conv_out"), unit)
                        if tap == 0:
                            pe.wait_ge(sem("rests"), 2 + c + 1)
                        n = next(m for m, e in enumerate(diag_end) if k < e)
                        pe.wait_ge(sem("diag_ready"), 2 * (n + 1))
                        d = k - diag_end[n] + DIAGS[n][2]
                        lo = tap // 2 * 2 if half == 0 else 0
                        o = ps[:, 7, lo:HALF]
                        gc = NCC - 1 - c
                        src = slice(PAD + half * HALF + lo - tap, PAD + (half + 1) * HALF - tap)
                        mm(o, diag_hi[:, n % 2, d, :], glu_hi[:, gc, src], start=(tap == 0), stop=False)
                        mm(o, diag_hi[:, n % 2, d, :], glu_lo[:, gc, src], start=False, stop=False)
                        mm(o, diag_lo[:, n % 2, d, :], glu_hi[:, gc, src], start=False,
                           stop=(tap == CONV_K - 1)).then_inc(sem("tap_used"), 1)
                if kind == "ada":
                    u = tp_of["ada", t]
                    if u >= 2:
                        pe.wait_ge(sem(tp_free[u - 2][0]), tp_free[u - 2][1])
                    for j in range(t, i):
                        ada(2 * NK + 20 + j, j, ps[:, 4 + u % 2, j - t:j - t + 1])
                if kind == "ln_mean":
                    if t == 0:
                        pe.wait_ge(sem("conv_out"), 2 * NCC)
                    else:
                        pe.wait_ge(sem("ln_sd"), t)
                    for c in range(NCC):
                        last = mm(ps[:, 7, :], ones, conv[:, c, t * HALF:(t + 1) * HALF], start=(c == 0),
                                  stop=(c == NCC - 1))
                    last.then_inc(sem("ln_mean"), 1)
                if kind == "ln_sum":
                    for c in range(NCC):
                        pe.wait_ge(sem("ln_sq"), NCC * t + c + 1)
                        mm(ps[:, 7, :], ones, squares[:, c, :], start=(c == 0),
                           stop=(c == NCC - 1)).then_inc(sem("ln_summed"), 1)

            pe.wait_ge(sem("gdiag_ready"), NK)
            for g in range(2):
                if g:
                    pe.wait_ge(sem("gdiag_ready"), 2 * NK)
                for j in range(2):
                    mm(ps[:, 2 * g + j, :], ones, gdiag[:, 4 * j:4 * j + 4, :].rearrange("p a b -> p (a b)"),
                       start=True, stop=True).then_inc(sem("gate_mm"), 1)
            pe.wait_ge(sem("gate_out"), 4)
            pe.wait_ge(sem("conv_lo"), 2 * NCC)
            for j in range(2):
                for kk in range(4):
                    m = 20 + 4 * j + kk
                    pe.wait_ge(sem("split_done"), m + 1)
                    for t in range(NT):
                        if kk == 0 and j:
                            pe.wait_ge(sem("gated"), t + 1)
                        last = tm(m, t, 2 * kk, HALF, h_hi, h_lo, kk == 0, kk == 3)
                        if kk == 3:
                            last.then_inc(sem("wo_full"), 1)
                        elif t == NT - 1:
                            last.then_inc(sem("wo_part"), 1)
            norm(1)

            def mlp(k, m0):
                pe.sem_inc(sem(f"down_full{k}"), 16)
                pe.sem_inc(sem(f"down_part{k}"), 2)
                with pe.Fori(0, GROUPS) as g:
                    for s in range(4):
                        pe.wait_ge(sem("split_done"), g * 8 + (m0 + s + 1))
                        for half in range(2):
                            b = 2 * s + half
                            pe.wait_ge(sem(f"down_out{k}"), g * 16 + (b + 9))
                            cm(s, half, b, None, f"up_full{k}")
                    for j in range(2):
                        for kk in range(2):
                            s = 4 + 2 * j + kk
                            pe.wait_ge(sem("split_done"), g * 8 + (m0 + s + 1))
                            if j == 0:
                                pe.wait_ge(sem(f"u_lo{k}"), g * 8 + (4 * kk + 4 + 4))
                            for t in range(NT):
                                if kk == 0 and j == 0:
                                    pe.wait_ge(sem(f"up_relu{k}"), g * 8 + (t + 1))
                                if kk == 0 and j == 1:
                                    pe.wait_ge(sem(f"down_out{k}"), g * 16 + (t + 1 + 16))
                                last = tm(s, t, 2 * kk, HALF, u_hi, u_lo, kk == 0, kk == 1)
                                if kk == 1:
                                    last.then_inc(sem(f"down_full{k}"), 1)
                                elif t == NT - 1:
                                    last.then_inc(sem(f"down_part{k}"), 1)

            pe.wait_ge(sem("norm_lo"), 4 * NK)
            mlp(0, W_FIRST)
            norm(2)
            pe.wait_ge(sem("norm_lo"), 6 * NK)
            for i in range(len(CH2) + 1):
                if i < len(CH2):
                    pe.wait_ge(sem("split_done"), M_2 + i + 1)
                    if i >= 3:
                        pe.wait_ge(sem(ch_read[i - 3][0]), ch_read[i - 3][1])
                    for half in range(2):
                        cm(i, half, 2 * (i % 3) + half, None, "cm2_full")
                if i == 0:
                    pe.wait_ge(sem("ab_parts"), 2)
                    for half in range(2):
                        cols, o = slice(half * HALF, (half + 1) * HALF), ps[0:2 * GH, 6 + half, :]
                        for k in range(NK):
                            mm(o, ab_hi[:, k, :], h_hi[:, k, cols], start=(k == 0), stop=False)
                            mm(o, ab_hi[:, k, :], h_lo[:, k, cols], start=False, stop=False)
                            last = mm(o, ab_lo[:, k, :], h_hi[:, k, cols], start=False, stop=(k == NK - 1))
                    last.then_inc(sem("ab_full"), 1)
                if i == 1:
                    pe.wait_ge(sem("ab_out"), 1)
                    for t in range(NT):
                        last = nc.tensor.transpose(ps[:, 6, t * 2 * GH:(t + 1) * 2 * GH], abT[:, t * P:(t + 1) * P],
                                                   ident[0:2 * GH, 0:2 * GH])
                    last.then_inc(sem("ab_full"), 1)
                if i and (i - 1) in aux_read:
                    kind, c = CH2[i - 1]
                    if i == 1:
                        pe.wait_ge(sem("ab_out"), 2)
                    elif (i - 2) in aux_read:
                        pe.wait_ge(sem(aux_read[i - 2][0]), aux_read[i - 2][1])
                    y = yt[:, (i - 1) % 2, :]
                    if kind == "pool":
                        pe.wait_ge(sem("wpool_in"), 16)
                        pe.wait_ge(sem("pooled"), 2 * (c + 1))
                    else:
                        pe.wait_ge(sem("l2_sq"), c + 1)
                    for half in range(2):
                        last = mm(ps[:, 6 + half, :], wpool[:, c, :] if kind == "pool" else ones,
                                  y[:, half * HALF:(half + 1) * HALF], start=True, stop=True)
                    last.then_inc(sem("pool_mm" if kind == "pool" else "l2_mm"), 1)

            pe.wait_ge(sem("masks_ready"), 1)
            pe.wait_ge(sem("gs_dve"), 2)
            pe.wait_ge(sem("z_silu"), GH)
            g32 = gs["g"].rearrange("p t h -> p (t h)")
            mm(ps[:, 6, 0:32], tri, g32, start=True, stop=True).then_inc(sem("gs_mm"), 1)
            mm(ps[:, 6, 32:64], blk, g32, start=True, stop=True).then_inc(sem("gs_mm"), 1)

            for kind, t, l in GSTEPS:
                b = prep[t % 2]
                n0 = 3 * (t % 2)
                x0, x1, x2 = (bank(n0 + i) for i in range(3))
                tok = slice(t * P, (t + 1) * P)

                def heads(out, lhs, rhs, what):
                    for h in range(GH):
                        last = mm(out[:, h, :], lhs[:, h, :], rhs[:, h, :], start=True, stop=True)
                    last.then_inc(prep_sem("mm", t), 1)

                def turns(out, src):
                    for h in range(GH):
                        last = nc.tensor.transpose(out[:, h, :], src[:, h, :], ident)
                    return last

                if kind == "head_a":
                    if t >= 2:
                        pe.wait_ge(prep_sem("act", t - 2), prep_count("act", t - 2, "kct"))
                    pe.wait_ge(prep_sem("dve", t), prep_count("dve", t, "tg"))
                    mm(ps[:, n0, :], ones, b["z"].rearrange("p h m -> p (h m)"), start=True,
                       stop=True).then_inc(prep_sem("mm", t), 1)
                    heads(x1, kc[:, :, tok], kc[:, :, tok], "gram")
                    heads(x2, kc[:, :, tok], qc[:, :, tok], "kq")
                if kind == "head_b":
                    pe.wait_ge(prep_sem("pool", t), prep_count("pool", t, "b0"))
                    pe.wait_ge(prep_sem("act", t), prep_count("act", t, "egb"))
                    turns(x0, b["b0"]).then_inc(prep_sem("mm", t), 1)
                if kind == "level_z":
                    pe.wait_ge(prep_sem("pool", t), prep_count("pool", t, f"b{l}"))
                    pe.wait_ge(prep_sem("dve", t), prep_count("dve", t, f"u{l - 1}"))
                    heads(x0, b[f"b{l % 2}"], b["u"], f"z{l}")
                if kind == "level_tu":
                    pe.wait_ge(prep_sem("act", t), prep_count("act", t, f"z{l}"))
                    if l < 5:
                        pe.wait_ge(prep_sem("pool", t), prep_count("pool", t, "t0"))
                        heads(x1, b["z"], b["t"], f"t{l}")
                    heads(x2, b["t"], b["z"], f"u{l}")
                if kind == "tail_a":
                    turns(x0, kc[:, :, tok]).then_inc(prep_sem("mm", t), 1)
                    turns(x1, vc[:, :, tok]).then_inc(prep_sem("mm", t), 1)
                if kind == "tail_b":
                    pe.wait_ge(prep_sem("dve", t), prep_count("dve", t, "vb"))
                    heads(x1, b["u"], b["vb"], "val")
                    heads(x2, b["kbe"], b["u"], "kct")
                if kind in ("chunk_a", "chunk_b"):
                    r = slice(CHUNK * l, CHUNK * (l + 1))
                if kind == "chunk_a":
                    if l == 0:
                        pe.wait_ge(prep_sem("act", t), prep_count("act", t, "kct"))
                        pe.wait_ge(prep_sem("pool", t), prep_count("pool", t, "qdec"))
                        if t:
                            pe.wait_ge(sem("scan_dve"), scan_count("dve", t - 1, "gated"))
                            pe.wait_ge(sem("scan_dve"), scan_count("dve", t - 1, "snew1"))
                    else:
                        pe.wait_ge(sem("scan_dve"), scan_count("dve", t, "snew0"))
                    for h in range(GH):
                        mm(bank(6)[r, h, :], b["kct"][:, h, r], state[:, h, :], start=True, stop=True)
                    for h in range(GH):
                        last = mm(bank(7)[r, h, :], b["qdec"][:, h, r], state[:, h, :], start=(h == 0), stop=False,
                                  skip_group_check=True)
                    last.then_inc(sem("scan_mm"), 1)
                if kind == "chunk_b":
                    pe.wait_ge(sem("scan_dve"), scan_count("dve", t, f"vnew{l}"))
                    for h in range(GH):
                        last = mm(bank(6)[:, h, :], b["kd"][r, h, :], vnew[r, h, :], start=True, stop=True)
                    last.then_inc(sem("scan_mm"), 1)
                    if l:
                        for h in range(GH):
                            last = mm(bank(7)[:, h, :], b["ait"][:, h, :], vnew[:, h, :], start=False, stop=(h == GH - 1),
                                      skip_group_check=True)
                        last.then_inc(sem("scan_mm"), 1)
                if kind == "finish_c":
                    pe.wait_ge(sem("scan_dve"), scan_count("dve", t, "on"))
                    turns(bank(7), ot).then_inc(sem("scan_mm"), 1)

            for j in range(2):
                for kk in range(4):
                    pe.wait_ge(sem("split_done"), M_2 + len(CH2) + 4 * j + kk + 1)
                    if j == 0:
                        pe.wait_ge(sem("mix2_lo"), 4 * (kk + 1))
                    for t in range(NT):
                        if kk == 0 and j == 0 and t >= 6:
                            pe.wait_ge(sem("scan_dve"), scan_count("dve", NT - 1, "gated"))
                        if kk == 0 and j:
                            pe.wait_ge(sem("x_mixed2"), t + 1)
                        last = tm(kk, t, 2 * kk, HALF, h_hi, h_lo, kk == 0, kk == 3)
                        if kk == 3:
                            last.then_inc(sem("wo2_full"), 1)
                        elif t == NT - 1:
                            last.then_inc(sem("wo2_part"), 1)
            norm(3)
            pe.wait_ge(sem("norm_lo"), 8 * NK)
            mlp(1, M_MLP1)


_INS = ["x", "c", "positions", "w_ada", "b_ada", "g_mix", "w_in", "conv_w", "conv_b", "conv_norm_g",
        "conv_norm_b", "w_out", "g_mlp", "w_up", "w_down", "g_final", "norm_mix_2", "w_in_2", "conv_w_2",
        "w_pool_2", "pool_scale_2", "a_log_2", "dt_bias_2", "gdn_norm_2", "w_out_2", "norm_mlp_2", "w_up_2",
        "w_down_2", "norm_final_2"]


def kernel(**inputs):
    import concourse.bacc as bacc
    from concourse.bass_utils import run_bass_kernel_spmd

    nc = bacc.Bacc("TRN2", target_bir_lowering=False, num_devices=1)
    arrays, aps = {}, {}
    for name in _INS:
        v = np.ascontiguousarray(inputs[name])
        arrays[f"in_{name}_dram"] = v
        aps[name] = nc.dram_tensor(f"in_{name}_dram", v.shape, mybir.dt.from_np(v.dtype), kind="ExternalInput").ap()
    out = nc.dram_tensor("out_0_dram", (1, S, D), F32, kind="ExternalOutput").ap()
    build(nc, aps, out)
    r = run_bass_kernel_spmd(nc, [arrays], core_ids=[0])
    return r.results[0]["out_0_dram"]
```
